# Optimizing a Trainium2 kernel written in Bass

```python
import jax, jax.numpy as jnp
from jax import lax
import numpy as np

D_MODEL = 2048
BATCH = 1
SEQ = 256
DEPTH = 2

N_A_LAYERS = DEPTH // 2
N_B_LAYERS = DEPTH - N_A_LAYERS
EXPAND = 2
D_INNER = EXPAND * D_MODEL

HG_KEY_DIM = 128
HG_HEADS = D_MODEL // HG_KEY_DIM
HG_KEY_TOTAL = HG_HEADS * HG_KEY_DIM
HG_VAL_DIM = D_INNER // HG_HEADS
HG_CHUNK = 64

MLA_HEADS = 32
Q_LORA = 768
KV_LORA = 512
NOPE_DIM = 128
ROPE_DIM = 64
V_DIM = 128
ATTN_BLOCK = 128
ROPE_THETA = 10000.0
EPS = 1e-6

kernel_name = "yoco_hgrn2_mla_hybrid"

def rmsnorm(x, g):
    xf = x.astype(jnp.float32)
    y = xf * lax.rsqrt(jnp.mean(xf * xf, axis=-1, keepdims=True) + EPS)
    return (y * g.astype(jnp.float32)).astype(x.dtype)

def rope_tables(seq):
    pos = jnp.arange(seq, dtype=jnp.float32)
    inv_freq = ROPE_THETA ** (-jnp.arange(0, ROPE_DIM, 2, dtype=jnp.float32) / ROPE_DIM)
    ang = pos[:, None] * inv_freq[None, :]
    return jnp.cos(ang), jnp.sin(ang)

def apply_rope(x, cos, sin):
    xf = x.astype(jnp.float32)
    x1, x2 = jnp.split(xf, 2, axis=-1)
    out = jnp.concatenate([x1 * cos - x2 * sin, x2 * cos + x1 * sin], axis=-1)
    return out.astype(x.dtype)

def hgrn2_mixer(h, w_in, g_norm, w_out, lb):
    B, S, _ = h.shape
    proj = h @ w_in
    q, f, i, g = jnp.split(proj, [HG_KEY_TOTAL, 2 * HG_KEY_TOTAL, 2 * HG_KEY_TOTAL + D_INNER], axis=-1)
    ff = f.astype(jnp.float32)
    lb = lb.astype(jnp.float32)
    log_f = jnp.log(lb + (1.0 - lb) * jax.nn.sigmoid(ff))
    k = (1.0 - lb) * jax.nn.sigmoid(-ff)
    nc = S // HG_CHUNK

    def to_chunks(t, d):
        return t.astype(jnp.float32).reshape(B, nc, HG_CHUNK, HG_HEADS, d).transpose(1, 0, 3, 2, 4)

    qc, kc, gc = to_chunks(q, HG_KEY_DIM), to_chunks(k, HG_KEY_DIM), to_chunks(log_f, HG_KEY_DIM)
    vc = to_chunks(i, HG_VAL_DIM)
    causal = jnp.tril(jnp.ones((HG_CHUNK, HG_CHUNK), dtype=bool))

    def step(state, inp):
        q_, k_, v_, g_ = inp
        b = jnp.cumsum(g_, axis=2)
        o_inter = jnp.einsum('bhck,bhkv->bhcv', q_ * jnp.exp(b), state)
        rel = b[:, :, :, None, :] - b[:, :, None, :, :]
        decay = jnp.exp(jnp.where(causal[None, None, :, :, None], rel, -jnp.inf))
        scores = jnp.einsum('bhtk,bhsk,bhtsk->bhts', q_, k_, decay)
        o_intra = jnp.einsum('bhts,bhsv->bhtv', scores, v_)
        b_last = b[:, :, -1:, :]
        new_state = jnp.exp(b_last[:, :, 0, :])[..., None] * state + \
            jnp.einsum('bhsk,bhsv->bhkv', k_ * jnp.exp(b_last - b), v_)
        return new_state, o_inter + o_intra

    state0 = jnp.zeros((B, HG_HEADS, HG_KEY_DIM, HG_VAL_DIM), jnp.float32)
    _, o = lax.scan(step, state0, (qc, kc, vc, gc))
    o = o.transpose(1, 0, 3, 2, 4).reshape(B, S, HG_HEADS, HG_VAL_DIM).astype(h.dtype)
    o = rmsnorm(o, g_norm).reshape(B, S, D_INNER)
    return (o * jax.nn.silu(g)) @ w_out

def shared_mla_kv(stream, kv_in_norm_g, w_kv_down, kv_norm_g, w_kv_up, cos, sin):
    B, S, _ = stream.shape
    ckv = rmsnorm(stream, kv_in_norm_g) @ w_kv_down
    c, k_rope = jnp.split(ckv, [KV_LORA], axis=-1)
    kv = (rmsnorm(c, kv_norm_g) @ w_kv_up).reshape(B, S, MLA_HEADS, NOPE_DIM + V_DIM)
    k_nope, v = jnp.split(kv, [NOPE_DIM], axis=-1)
    k_rope = apply_rope(k_rope, cos, sin)
    return k_nope, k_rope, v

def causal_mla_attention(q_nope, q_rope, k_nope, k_rope, v):
    B, S, H, _ = q_nope.shape
    nb = S // ATTN_BLOCK
    scale = (NOPE_DIM + ROPE_DIM) ** -0.5
    key_pos = jnp.arange(S)

    def to_blocks(t):
        return t.reshape(B, nb, ATTN_BLOCK, *t.shape[2:]).swapaxes(0, 1)

    def one_block(args):
        qn, qr, start = args
        s = jnp.einsum('bqhd,bkhd->bhqk', qn, k_nope) + jnp.einsum('bqhr,bkr->bhqk', qr, k_rope)
        s = s.astype(jnp.float32) * scale
        q_pos = start + jnp.arange(ATTN_BLOCK)
        s = jnp.where(key_pos[None, :] <= q_pos[:, None], s, -jnp.inf)
        p = jax.nn.softmax(s, axis=-1).astype(v.dtype)
        return jnp.einsum('bhqk,bkhd->bqhd', p, v)

    starts = jnp.arange(nb, dtype=jnp.int32) * ATTN_BLOCK
    out = lax.map(one_block, (to_blocks(q_nope), to_blocks(q_rope), starts))
    return out.swapaxes(0, 1).reshape(B, S, H, V_DIM)

def mla_query_mixer(h, w_in, q_norm_g, w_q_up, w_out, k_nope, k_rope, v, cos, sin):
    B, S, _ = h.shape
    cq, gate = jnp.split(h @ w_in, [Q_LORA], axis=-1)
    q = (rmsnorm(cq, q_norm_g) @ w_q_up).reshape(B, S, MLA_HEADS, NOPE_DIM + ROPE_DIM)
    q_nope, q_rope = jnp.split(q, [NOPE_DIM], axis=-1)
    q_rope = apply_rope(q_rope, cos[:, None, :], sin[:, None, :])
    attn = causal_mla_attention(q_nope, q_rope, k_nope, k_rope, v).reshape(B, S, D_INNER)
    return (attn * jax.nn.silu(gate)) @ w_out

def setup_inputs(seed: int = 0) -> dict:
    key = jax.random.key(seed)
    ks = jax.random.split(key, 20)

    def w(k, shape, fan_in):
        return jax.random.normal(k, shape, jnp.float32) * fan_in ** -0.5

    def gain(k, shape):
        return 1.0 + 0.02 * jax.random.normal(k, shape, jnp.float32)

    hg_in_cols = 2 * HG_KEY_TOTAL + 2 * D_INNER
    return {
        "x": jax.random.normal(ks[0], (BATCH, SEQ, D_MODEL), jnp.float32),
        "norm_g": gain(ks[1], (DEPTH, D_MODEL)),
        "hg_w_in": w(ks[2], (N_A_LAYERS, D_MODEL, hg_in_cols), D_MODEL),
        "hg_g_norm": gain(ks[3], (N_A_LAYERS, HG_VAL_DIM)),
        "hg_w_out": w(ks[4], (N_A_LAYERS, D_INNER, D_MODEL), D_INNER),
        "hg_lb": 0.5 * jax.random.normal(ks[5], (DEPTH, HG_KEY_TOTAL), jnp.float32),
        "kv_in_norm_g": gain(ks[6], (D_MODEL,)),
        "w_kv_down": w(ks[7], (D_MODEL, KV_LORA + ROPE_DIM), D_MODEL),
        "kv_norm_g": gain(ks[8], (KV_LORA,)),
        "w_kv_up": w(ks[9], (KV_LORA, MLA_HEADS * (NOPE_DIM + V_DIM)), KV_LORA),
        "mla_w_in": w(ks[10], (N_B_LAYERS, D_MODEL, Q_LORA + D_INNER), D_MODEL),
        "mla_q_norm_g": gain(ks[11], (N_B_LAYERS, Q_LORA)),
        "mla_w_q_up": w(ks[12], (N_B_LAYERS, Q_LORA, MLA_HEADS * (NOPE_DIM + ROPE_DIM)), Q_LORA),
        "mla_w_out": w(ks[13], (N_B_LAYERS, D_INNER, D_MODEL), D_INNER),
        "final_norm_g": gain(ks[14], (D_MODEL,)),
    }

def reference(x, norm_g, hg_w_in, hg_g_norm, hg_w_out, hg_lb, kv_in_norm_g, w_kv_down, kv_norm_g,
              w_kv_up, mla_w_in, mla_q_norm_g, mla_w_q_up, mla_w_out, final_norm_g):
    S = x.shape[1]
    cos, sin = rope_tables(S)
    lower_bounds = jnp.cumsum(jax.nn.softmax(hg_lb.astype(jnp.float32), axis=0), axis=0)
    h = x
    k_nope = k_rope = v = None
    for layer in range(DEPTH):
        if layer < N_A_LAYERS:
            h = h + hgrn2_mixer(rmsnorm(h, norm_g[layer]), hg_w_in[layer], hg_g_norm[layer],
                                hg_w_out[layer], lower_bounds[layer])
        else:
            j = layer - N_A_LAYERS
            if j == 0:
                k_nope, k_rope, v = shared_mla_kv(h, kv_in_norm_g, w_kv_down, kv_norm_g, w_kv_up, cos, sin)
            h = h + mla_query_mixer(rmsnorm(h, norm_g[layer]), mla_w_in[j], mla_q_norm_g[j],
                                    mla_w_q_up[j], mla_w_out[j], k_nope, k_rope, v, cos, sin)
    return rmsnorm(h, final_norm_g)


_drawn_inputs = setup_inputs


def setup_inputs(seed=0):
    import zlib

    import numpy as np

    out = dict(_drawn_inputs(seed))
    spreads = {}
    factors = {'hg_g_norm': 5.983,
     'kv_in_norm_g': 8.0,
     'kv_norm_g': 8.0,
     'mla_q_norm_g': 8.0,
     'final_norm_g': 2.785}
    for name, (base, spread) in spreads.items():
        noise = np.random.default_rng([zlib.crc32(name.encode()), seed]).standard_normal(out[name].shape)
        drawn = base * np.exp(spread * noise) if base else spread * noise
        out[name] = __import__('jax').numpy.asarray(drawn.astype(out[name].dtype))
    for name, factor in factors.items():
        out[name] = (out[name] * factor).astype(out[name].dtype)
    return out
```

```python
import concourse.bass as bass
from concourse import mybir
from contextlib import ExitStack

TOKENS = 256
TILES = TOKENS // 128
D_MODEL = 2048
D_INNER = 4096
KEY_DIM = 128
HG_HEADS = 16
HG_VAL = 256
MLA_HEADS = 32
Q_LORA = 768
KV_LORA = 512
NOPE = 128
ROPE = 64
V_DIM = 128
EPS = 1e-6
ATT_SCALE = float(NOPE + ROPE) ** -0.5
MASKED = -1e30
SMALLEST_F = 1e-19

KT = D_MODEL // 128
KT_INNER = D_INNER // 128
KT_Q = Q_LORA // 128
KT_C = KV_LORA // 128
UNIT = 1024
UNIT_Q = 1152
RING = 4
AHEAD = 3

STEPS = 8
A_UNITS = 24
B_UNITS = 16
GROUPS = D_MODEL // 512
O_UNITS = KT_INNER // 2
C_UNITS = 10
CQ_UNITS = 12
A0 = 0
WO0 = A0 + STEPS * A_UNITS
KV0 = WO0 + GROUPS * O_UNITS
CQ0 = KV0 + C_UNITS
B0 = CQ0 + CQ_UNITS
OUT0 = B0 + STEPS * B_UNITS
UNITS = OUT0 + GROUPS * O_UNITS

LEVELS = 8
CONST_COLS = 128 + 128 + 256 + 256 + 384
LEVEL_COLS = (LEVELS + 1) * 128
MASK_COLS = 7 * 128
GAIN_COLS = 3 * KT + KT_C + KT_Q + 2 + 2 * HG_HEADS


def build(nc, w_a, w_o, w_kv, w_cq, w_bkv, w_bq, w_bg, w_out, x, consts, levels, masks, gains, final_g, out, h_store):
    fp32 = mybir.dt.float32
    f32r = mybir.dt.float32r
    ALU = mybir.AluOpType
    ACT = mybir.ActivationFunctionType
    AX = mybir.AxisListType
    ds = bass.ds

    ctx = ExitStack()
    with ctx:
        def sb(name, shape, dt=fp32, stack=ctx):
            return stack.enter_context(nc.sbuf_tensor(name, shape, dt))

        def sem(name):
            return ctx.enter_context(nc.semaphore(name))

        w_raw = sb("w_raw", [128, RING, UNIT_Q])
        w_hi = sb("w_hi", [128, RING, UNIT_Q], f32r)
        w_lo = sb("w_lo", [128, RING, UNIT_Q], f32r)
        aT_hi = sb("aT_hi", [128, KT_INNER, TOKENS], f32r)
        aT_lo = sb("aT_lo", [128, KT_INNER, TOKENS], f32r)
        nT_hi = sb("nT_hi", [128, KT, TOKENS], f32r)
        nT_lo = sb("nT_lo", [128, KT, TOKENS], f32r)
        const_sb = sb("const_sb", [128, CONST_COLS])
        gain_sb = sb("gain_sb", [128, GAIN_COLS])
        ident = const_sb[:, 0:128]
        rotate = const_sb[:, 128:256]
        cos_sb = const_sb[:, 256:512]
        sin_sb = const_sb[:, 512:768]
        causal = const_sb[:, 768:1152]
        g_hg = gain_sb[:, 0:KT]
        g_mla = gain_sb[:, KT:2 * KT]
        g_kvin = gain_sb[:, 2 * KT:3 * KT]
        g_c = gain_sb[:, 3 * KT:3 * KT + KT_C]
        g_q = gain_sb[:, 3 * KT + KT_C:3 * KT + KT_C + KT_Q]
        at = 3 * KT + KT_C + KT_Q
        g_o = gain_sb[:, at:at + 2]
        lb_in = gain_sb[:, at + 2:at + 2 + 2 * HG_HEADS]
        sums = sb("sums", [128, 16])
        rnorm = sb("rnorm", [128, 8])
        ms = sb("ms", [128, 8])
        minus_half = sb("minus_half", [128, 8])
        h_sums = sb("h_sums", [128, TILES])

        a_mem = ExitStack()
        h = sb("h", [128, TILES, D_MODEL], stack=a_mem)
        h_flat = h[:, :, :].rearrange("p t n -> p (t n)")
        decay = [h_flat[:, i * 1024:(i + 1) * 1024].rearrange("p (l t) -> p l t", l=LEVELS) for i in range(2)]
        k_dec = [h_flat[:, (2 + i) * 1024:(3 + i) * 1024].rearrange("p (l t) -> p l t", l=LEVELS) for i in range(2)]
        level_raw = sb("level_raw", [128, LEVEL_COLS], stack=a_mem)
        level_sb = sb("level_sb", [128, LEVEL_COLS], f32r, stack=a_mem)
        mask_sb = sb("mask_sb", [128, MASK_COLS], stack=a_mem)
        lb_tmp = sb("lb_tmp", [128, 3, HG_HEADS], stack=a_mem)
        lb = sb("lb", [128, HG_HEADS], stack=a_mem)
        one_lb = sb("one_lb", [128, HG_HEADS], stack=a_mem)
        qT = sb("qT", [128, 2 * TOKENS], stack=a_mem)
        kT = sb("kT", [128, 2 * TOKENS], stack=a_mem)
        logf = sb("logf", [128, 2 * TOKENS], stack=a_mem)
        g_hi = sb("g_hi", [128, 512], f32r, stack=a_mem)
        g_lo = sb("g_lo", [128, 512], f32r, stack=a_mem)
        att = sb("att", [128, 2, 3, 128], stack=a_mem)
        val = sb("val", [128, TILES, 512], stack=a_mem)
        gate = sb("gate", [128, TILES, 512], stack=a_mem)
        a_mem.close()

        b_mem = ExitStack()
        cT_hi = sb("cT_hi", [128, KT_C, TOKENS], f32r, stack=b_mem)
        cT_lo = sb("cT_lo", [128, KT_C, TOKENS], f32r, stack=b_mem)
        cqT_hi = sb("cqT_hi", [128, KT_Q, TOKENS], f32r, stack=b_mem)
        cqT_lo = sb("cqT_lo", [128, KT_Q, TOKENS], f32r, stack=b_mem)
        k_nope = sb("k_nope", [128, 4, TOKENS], stack=b_mem)
        q_nope = sb("q_nope", [128, 4, TOKENS], stack=b_mem)
        q_rope = sb("q_rope", [128, 2, TOKENS], stack=b_mem)
        rot_sb = sb("rot_sb", [128, 2, TOKENS], stack=b_mem)
        k_even = sb("k_even", [128, TOKENS], stack=b_mem)
        k_odd = sb("k_odd", [128, TOKENS], stack=b_mem)
        v_sb = sb("v_sb", [128, TILES, 512], stack=b_mem)
        prob = sb("prob", [128, 2, 384], stack=b_mem)
        probT = sb("probT", [128, 2, 384], stack=b_mem)
        gate_b = sb("gate_b", [128, TILES, 512], stack=b_mem)
        row_max = sb("row_max", [128, 2, TILES, 2], stack=b_mem)
        row_sum = sb("row_sum", [128, 2, 4], stack=b_mem)
        b_mem.close()
        q_flat = k_nope[:, :, :].rearrange("p h t -> p (h t)")
        c_nat = q_flat.rearrange("p (t n) -> p t n", t=TILES)
        cq_nat = [v_sb[:, :, :].rearrange("p t n -> p (t n)")[:, 0:Q_LORA],
                  gate_b[:, :, :].rearrange("p t n -> p (t n)")[:, 0:Q_LORA]]

        f_mem = ExitStack()
        h_fin = sb("h_fin", [128, TILES, D_MODEL], stack=f_mem)
        final_sb = sb("final_sb", [128, D_MODEL], stack=f_mem)
        f_mem.close()

        ps = ctx.enter_context(nc.psum_tensor("ps", [128, 8 * 512], fp32))

        def bank(b, n=1):
            return ps[:, b * 512:(b + n) * 512]

        raw_ready = [sem(f"raw_ready{i}") for i in range(RING)]
        x_ready = sem("x_ready")
        const_ready = sem("const_ready")
        x_again = sem("x_again")
        h_stored = sem("h_stored")
        h_back = sem("h_back")
        out_stored = sem("out_stored")
        hi_ready = sem("hi_ready")
        lo_ready = sem("lo_ready")
        unit_done = sem("unit_done")
        sq_done = sem("sq_done")
        mean_done = sem("mean_done")
        norm_ready = sem("norm_ready")
        scaled = sem("scaled")
        turned = sem("turned")
        n_hi = sem("n_hi")
        n_lo = sem("n_lo")
        half_ready = sem("half_ready")
        lb_step = sem("lb_step")
        lb_exp = sem("lb_exp")
        level_ready = sem("level_ready")
        sig_ready = sem("sig_ready")
        sig_clamped = sem("sig_clamped")
        logf_ready = sem("logf_ready")
        q_ready = sem("q_ready")
        k_ready = sem("k_ready")
        gturn_done = sem("gturn_done")
        ghi_ready = sem("ghi_ready")
        glo_ready = sem("glo_ready")
        range_done = sem("range_done")
        decay_ready = sem("decay_ready")
        kdec_ready = sem("kdec_ready")
        qdec_ready = sem("qdec_ready")
        score_done = sem("score_done")
        masked = sem("masked")
        att_ready = sem("att_ready")
        cross_ready = sem("cross_ready")
        val_ready = sem("val_ready")
        o_done = sem("o_done")
        o_sq = sem("o_sq")
        o_ms = sem("o_ms")
        o_norm = sem("o_norm")
        gsig_ready = sem("gsig_ready")
        silu_ready = sem("silu_ready")
        y_ready = sem("y_ready")
        yturn_done = sem("yturn_done")
        y_hi = sem("y_hi")
        y_lo = sem("y_lo")
        h_ready = sem("h_ready")
        h_sq = sem("h_sq")
        h_sum = sem("h_sum")
        c_sq = sem("c_sq")
        c_ms = sem("c_ms")
        c_norm = sem("c_norm")
        c_scaled = sem("c_scaled")
        c_turned = sem("c_turned")
        c_hi = sem("c_hi")
        c_lo = sem("c_lo")
        kr_raw = sem("kr_raw")
        kr_rot = sem("kr_rot")
        kr_step = sem("kr_step")
        cq_sum = sem("cq_sum")
        kn_ready = sem("kn_ready")
        v_ready = sem("v_ready")
        qn_ready = sem("qn_ready")
        qr_raw = sem("qr_raw")
        qr_rot = sem("qr_rot")
        qr_step = sem("qr_step")
        s_done = sem("s_done")
        score_masked = sem("score_masked")
        max_ready = sem("max_ready")
        neg_ready = sem("neg_ready")
        p_ready = sem("p_ready")
        pturn_done = sem("pturn_done")
        pT_ready = sem("pT_ready")
        pv_done = sem("pv_done")
        inv_ready = sem("inv_ready")
        gbsig_ready = sem("gbsig_ready")
        bsilu_ready = sem("bsilu_ready")
        yb_ready = sem("yb_ready")
        ybturn_done = sem("ybturn_done")
        yb_hi = sem("yb_hi")
        yb_lo = sem("yb_lo")
        fin_norm = sem("fin_norm")
        fin_scaled = sem("fin_scaled")

        block = ctx.enter_context(nc.Block())

        def slot(base, n):
            return (base + n) % RING

        def known(v):
            return isinstance(v, int)

        def lo_part(dve, dst, src, gain, high):
            return dve.scalar_tensor_tensor(out=dst, in0=src, scalar=gain, in1=high.bitcast(fp32),
                                            op0=ALU.mult, op1=ALU.subtract)

        def b_cols(n):
            return UNIT_Q if 4 <= n % B_UNITS < 8 else UNIT

        def level_at(tile, level):
            return level if tile == 0 else (level - 1) % LEVELS

        STREAM_ORDER = [(b, w) for b in range(KT // 2) for w in range(2)]

        @block.sync
        def _(sp):
            sp.dma_start(h[:, :, :], x.rearrange("(t p) n -> p t n", p=128)).then_inc(x_ready, 16)
            sp.dma_start(const_sb[:, :], consts).then_inc(const_ready, 16)
            sp.dma_start(gain_sb[:, :], gains).then_inc(const_ready, 16)
            sp.dma_start(level_raw[:, :], levels).then_inc(const_ready, 16)
            sp.dma_start(mask_sb[:, :], masks).then_inc(const_ready, 16)

            def load(unit, s, src, cols):
                if not known(unit) or unit >= RING:
                    sp.wait_ge(lo_ready, unit - (RING - 1))
                sp.dma_start(w_raw[:, s, 0:cols], src).then_inc(raw_ready[s], 16)

            for n in range(RING):
                load(n, n, w_a[n], UNIT)
            with sp.Fori(1, STEPS * A_UNITS // RING) as i:
                for n in range(RING):
                    load(i * RING + n, n, w_a[i * RING + n], UNIT)
            for n in range(RING):
                load(WO0 + n, slot(WO0, n), w_o[n], UNIT)
            sp.wait_ge(score_done, 4 * STEPS)
            sp.wait_ge(att_ready, 4 * STEPS)
            sp.dma_start(h[:, :, :], x.rearrange("(t p) n -> p t n", p=128)).then_inc(x_again, 16)
            with sp.Fori(1, GROUPS * O_UNITS // RING) as i:
                for n in range(RING):
                    load(i * RING + (WO0 + n), n, w_o[i * RING + n], UNIT)
            for n in range(RING):
                load(KV0 + n, slot(KV0, n), w_kv[n], UNIT)
            sp.wait_ge(h_ready, GROUPS)
            sp.dma_start(h_store.rearrange("(t p) n -> p t n", p=128), h[:, :, :]).then_inc(h_stored, 16)
            for n in range(RING, C_UNITS):
                load(KV0 + n, slot(KV0, n), w_kv[n], UNIT)
            for n in range(CQ_UNITS):
                load(CQ0 + n, slot(CQ0, n), w_cq[n], UNIT)
            with sp.Fori(0, STEPS) as j:
                for n in range(B_UNITS):
                    src = w_bkv[j * 4 + n] if n < 4 else w_bq[j * 4 + (n - 4)] if n < 8 else w_bg[j * 8 + (n - 8)]
                    load(j * B_UNITS + (B0 + n), slot(B0, n), src, b_cols(n))
            for n in range(2 * RING):
                load(OUT0 + n, slot(OUT0, n), w_out[n], UNIT)
            sp.wait_ge(yb_lo, STEPS)
            sp.wait_ge(h_stored, 16)
            sp.dma_start(h_fin[:, :, :], h_store.rearrange("(t p) n -> p t n", p=128)).then_inc(h_back, 16)
            sp.dma_start(final_sb[:, :], final_g.partition_broadcast(128)).then_inc(h_back, 16)
            with sp.Fori(2, GROUPS * O_UNITS // RING) as i:
                for n in range(RING):
                    load(i * RING + (OUT0 + n), slot(OUT0, n), w_out[i * RING + n], UNIT)
            for part in range(4):
                tile, half = divmod(part, 2)
                sp.wait_ge(fin_scaled, part + 1)
                sp.dma_start(out[0, tile * 128:(tile + 1) * 128, half * 1024:(half + 1) * 1024],
                             h_fin[:, tile, half * 1024:(half + 1) * 1024]).then_inc(out_stored, 16)
            sp.wait_ge(out_stored, 4 * 16)

        @block.gpsimd
        def _(pool):
            pool.memset(minus_half[:, :], -0.5).then_inc(half_ready, 1)
            pool.wait_ge(half_ready, 1)

            def rsqrt(n, done):
                pool.tensor_tensor(rnorm[:, 0:n], ms[:, 0:n], minus_half[:, 0:n], ALU.pow).then_inc(done, 1)

            pool.wait_ge(mean_done, 1)
            rsqrt(TILES, norm_ready)

            def a_step(j, first):
                pool.wait_ge(k_ready, j + 1)
                for blk in range(4):
                    head, tile = divmod(blk, 2)
                    pool.wait_ge(decay_ready, j * 4 + (blk + 1))
                    if not first or blk >= 2:
                        pool.wait_ge(score_done, j * 4 + 2 * head)
                    cols = kT[:, head * TOKENS + tile * 128:head * TOKENS + tile * 128 + 128]
                    pool.tensor_tensor(k_dec[blk % 2], decay[blk % 2],
                                       cols[:, None, :].to_broadcast([128, LEVELS, 128]),
                                       ALU.mult).then_inc(kdec_ready, 1)
                pool.wait_ge(o_ms, j + 1)
                rsqrt(4, o_norm)

            a_step(0, True)
            with pool.Fori(1, STEPS) as j:
                a_step(j, False)

            pool.wait_ge(mean_done, 2)
            rsqrt(TILES, norm_ready)
            pool.wait_ge(c_ms, 1)
            pool.wait_ge(scaled, 2 * TILES)
            rsqrt(TILES, c_norm)
            pool.wait_ge(c_ms, 2)
            pool.wait_ge(c_scaled, TILES)
            rsqrt(TILES, c_norm)
            pool.wait_ge(mean_done, 3)
            rsqrt(TILES, fin_norm)

        @block.scalar
        def _(act):
            def split_hi(base, i, per, n, cols=UNIT):
                s = slot(base, n)
                turn = (base + n - s) // RING + 1
                act.wait_ge(raw_ready[s], i * (per // RING * 16) + 16 * turn)
                if not known(i) or base + i * per + n >= RING:
                    act.wait_ge(unit_done, i * per + (base + n - RING + 1))
                act.activation(w_hi[:, s, 0:cols], w_raw[:, s, 0:cols], ACT.Copy).then_inc(hi_ready, 1)

            def mean(n, src, width, done):
                act.activation(ms[:, 0:n], src, ACT.Copy, scale=1.0 / width, bias=EPS).then_inc(done, 1)

            act.wait_ge(x_ready, 16)
            for t in range(TILES):
                act.activation(bank(4 * t, 4), h[:, t, :], ACT.Square, accum_out=sums[:, t:t + 1]).then_inc(sq_done, 1)
            act.wait_ge(sq_done, TILES)
            mean(TILES, sums[:, 0:TILES], D_MODEL, mean_done)
            for n in range(AHEAD):
                split_hi(A0, 0, A_UNITS, n)
            act.wait_ge(lb_step, 3)
            act.activation(lb_tmp[:, 0:2, :], lb_tmp[:, 0:2, :], ACT.Exp).then_inc(lb_exp, 1)

            for kt in range(KT):
                act.wait_ge(turned, kt // 2 + 1)
                act.activation(nT_hi[:, kt, :], ps[:, kt * TOKENS:(kt + 1) * TOKENS], ACT.Copy,
                               scale=g_hg[:, kt:kt + 1]).then_inc(n_hi, 1)

            def y_out(jp):
                def gate_sigmoid():
                    act.wait_ge(unit_done, jp * A_UNITS + A_UNITS)
                    act.activation(gate[:, :, :].rearrange("p t n -> p (t n)"), bank(4, 2),
                                   ACT.Sigmoid).then_inc(gsig_ready, 1)

                def turned_hi():
                    act.wait_ge(yturn_done, jp + 1)
                    for c in range(4):
                        last = act.activation(aT_hi[:, ds(jp * 4 + c, 1), :], ps[:, 4 * 512 + c * 256:4 * 512 + (c + 1) * 256],
                                              ACT.Copy, scale=g_o[:, c % 2:c % 2 + 1])
                    last.then_inc(y_hi, 1)
                return gate_sigmoid, turned_hi

            def a_step(j, first):
                if not first:
                    gate_sigmoid, turned_hi = y_out(j - 1)
                for n in range(A_UNITS):
                    split_hi(A0, j, A_UNITS, n + AHEAD)
                    if n == 0 and not first:
                        gate_sigmoid()
                    if n == 2 and not first:
                        turned_hi()
                    if n == 7:
                        act.wait_ge(unit_done, j * A_UNITS + 8)
                        act.activation(logf[:, :], bank(1), ACT.Sigmoid).then_inc(sig_ready, 1)
                        act.activation(kT[:, :], bank(1), ACT.Sigmoid, scale=-1.0).then_inc(sig_ready, 1)
                        act.wait_ge(sig_clamped, j + 1)
                        if first:
                            act.wait_ge(lb_step, 7)
                        for e in range(2):
                            head = logf[:, e * TOKENS:(e + 1) * TOKENS]
                            act.activation(head, head, ACT.Ln, scale=one_lb[:, ds(j * 2 + e, 1)],
                                           bias=lb[:, ds(j * 2 + e, 1)]).then_inc(logf_ready, 1)
                    if n == 9:
                        act.wait_ge(gturn_done, j + 1)
                        act.activation(g_hi[:, :], bank(6), ACT.Copy).then_inc(ghi_ready, 1)
                    if n in (11, 12, 14, 16):
                        blk = (11, 12, 14, 16).index(n)
                        act.wait_ge(range_done, j * 4 + (blk + 1))
                        if not first or blk >= 2:
                            act.wait_ge(att_ready, j * 4 + (blk - 1))
                        act.activation(decay[blk % 2].rearrange("p l t -> p (l t)"), bank(0, 2),
                                       ACT.Exp).then_inc(decay_ready, 1)
                    if n in (15, 19):
                        head = (15, 19).index(n)
                        act.wait_ge(masked, j * 4 + (2 * head + 2))
                        act.activation(att[:, head, 2, :], ps[:, 6 * 512 + 7 * 128:8 * 512], ACT.Copy).then_inc(cross_ready, 1)
                    if n == 17:
                        act.wait_ge(unit_done, j * A_UNITS + 16)
                        act.activation(val[:, :, :].rearrange("p t n -> p (t n)"), bank(2, 2), ACT.Copy).then_inc(val_ready, 1)
                    if n == 21:
                        act.wait_ge(o_done, j + 1)
                        for i in range(4):
                            last = act.activation(ps[:, i * 256:(i + 1) * 256], ps[:, 6 * 512 + i * 256:6 * 512 + (i + 1) * 256],
                                                  ACT.Square, accum_out=sums[:, i:i + 1])
                        last.then_inc(o_sq, 1)
                        act.wait_ge(o_sq, j + 1)
                        mean(4, sums[:, 0:4], HG_VAL, o_ms)

            a_step(0, True)
            with act.Fori(1, STEPS) as j:
                a_step(j, False)

            def h_squares(g, stream, done):
                act.wait_ge(h_ready, done)
                for t in range(TILES):
                    act.activation(bank(6 + t), stream[:, t, g * 512:(g + 1) * 512], ACT.Square,
                                   accum_out=sums[:, 8 + 4 * t + g:9 + 4 * t + g]).then_inc(h_sq, 1)

            gate_sigmoid, turned_hi = y_out(STEPS - 1)
            for g in range(GROUPS):
                for n in range(O_UNITS):
                    split_hi(WO0, g, O_UNITS, n + AHEAD)
                    if g == 0 and n == 0:
                        gate_sigmoid()
                    if g == 0 and n == 2:
                        turned_hi()
                    if g and n == 1:
                        h_squares(g - 1, h, g)
            h_squares(GROUPS - 1, h, GROUPS)
            act.wait_ge(h_sum, 1)
            mean(TILES, h_sums[:, :], D_MODEL, mean_done)

            def stream_hi(batch, which):
                dst, gain = ((aT_hi, g_kvin), (nT_hi, g_mla))[which]
                act.wait_ge(turned, KT // 2 + batch + 1)
                for kt in (2 * batch, 2 * batch + 1):
                    act.activation(dst[:, kt, :], ps[:, kt * TOKENS:(kt + 1) * TOKENS], ACT.Copy,
                                   scale=gain[:, kt:kt + 1]).then_inc(n_hi, 1)
            for batch, which in STREAM_ORDER:
                stream_hi(batch, which)

            for n in range(C_UNITS + CQ_UNITS):
                split_hi(KV0, 0, 0, n + AHEAD)
                if n == 7:
                    act.wait_ge(unit_done, KV0 + 8)
                    act.wait_ge(n_lo, 3 * KT)
                    for t in range(TILES):
                        act.activation(bank(5 + t), bank(t), ACT.Square, accum_out=sums[:, t:t + 1]).then_inc(c_sq, 1)
                    act.wait_ge(c_sq, 2)
                    mean(TILES, sums[:, 0:TILES], KV_LORA, c_ms)
                if n == 9:
                    act.wait_ge(unit_done, KV0 + C_UNITS)
                    act.activation(rot_sb[:, 0, :], bank(2)[:, 0:TOKENS], ACT.Copy).then_inc(kr_raw, 1)
                if n == 11:
                    act.wait_ge(c_turned, 1)
                    for kt in range(KT_C):
                        act.activation(cT_hi[:, kt, :], ps[:, kt * TOKENS:(kt + 1) * TOKENS], ACT.Copy,
                                       scale=g_c[:, kt:kt + 1]).then_inc(c_hi, 1)
            act.wait_ge(unit_done, B0)
            for t in range(TILES):
                act.wait_ge(kr_step, 6)
                act.wait_ge(c_sq, 2 + 2 * t)
                act.activation(bank(7), bank(3 + t), ACT.Square, accum_out=sums[:, 2 + 2 * t:3 + 2 * t]).then_inc(c_sq, 1)
                act.activation(bank(2)[:, 0:256], bank(5 + t)[:, 0:256], ACT.Square, accum_out=sums[:, 3 + 2 * t:4 + 2 * t]).then_inc(c_sq, 1)
            act.wait_ge(cq_sum, 1)
            mean(TILES, sums[:, 6:8], Q_LORA, c_ms)

            def yb_out(jp):
                def gate_sigmoid():
                    act.wait_ge(unit_done, jp * B_UNITS + (B0 + B_UNITS))
                    act.activation(gate_b[:, :, :].rearrange("p t n -> p (t n)"), bank(2, 2),
                                   ACT.Sigmoid).then_inc(gbsig_ready, 1)

                def turned_hi():
                    act.wait_ge(ybturn_done, jp + 1)
                    act.activation(aT_hi[:, ds(jp * 4, 4), :].rearrange("p c t -> p (c t)"), bank(6, 2), ACT.Copy).then_inc(yb_hi, 1)
                return gate_sigmoid, turned_hi

            def b_step(j, first):
                if not first:
                    gate_sigmoid, turned_hi = yb_out(j - 1)
                for n in range(B_UNITS):
                    split_hi(B0, j, B_UNITS, n + AHEAD, b_cols(n + AHEAD))
                    if n == 0 and not first:
                        gate_sigmoid()
                    if n == 1:
                        act.wait_ge(unit_done, j * B_UNITS + (B0 + 2))
                        act.activation(k_nope[:, :, :].rearrange("p h t -> p (h t)"), bank(0, 2), ACT.Copy).then_inc(kn_ready, 1)
                        if first:
                            act.wait_ge(c_turned, 2)
                            for kt in range(KT_Q):
                                act.activation(cqT_hi[:, kt, :], ps[:, 5 * 512 + kt * TOKENS:5 * 512 + (kt + 1) * TOKENS],
                                               ACT.Copy, scale=g_q[:, kt:kt + 1]).then_inc(c_hi, 1)
                    if n == 2 and not first:
                        turned_hi()
                    if n == 7:
                        act.wait_ge(unit_done, j * B_UNITS + (B0 + 8))
                        act.activation(q_rope[:, :, :].rearrange("p h t -> p (h t)"), bank(0), ACT.Copy).then_inc(qr_raw, 1)
                    if n in (12, 14):
                        pair = (12, 14).index(n)
                        act.wait_ge(pturn_done, j * 2 + (pair + 1))
                        act.activation(probT[:, :, :], bank(4 + 2 * pair, 2).rearrange("p (i n) -> p i n", i=2)[:, :, 0:384],
                                       ACT.Copy).then_inc(pT_ready, 1)
                    if n in (10, 12):
                        pair = (10, 12).index(n)
                        act.wait_ge(neg_ready, j * 2 + (pair + 1))
                        for i in range(2):
                            for t in range(TILES):
                                cols = prob[:, i, 128 * t:128 + 256 * t]
                                last = act.activation(cols, cols, ACT.Exp, scale=ATT_SCALE, bias=row_max[:, pair, t, i:i + 1],
                                                      accum_out=row_sum[:, pair, 2 * i + t:2 * i + t + 1])
                        last.then_inc(p_ready, 1)

            b_step(0, True)
            with act.Fori(1, STEPS) as j:
                b_step(j, False)

            gate_sigmoid, turned_hi = yb_out(STEPS - 1)
            for g in range(GROUPS):
                for n in range(O_UNITS):
                    if g * O_UNITS + n + AHEAD < GROUPS * O_UNITS:
                        split_hi(OUT0, g, O_UNITS, n + AHEAD)
                    if g == 0 and n == 0:
                        gate_sigmoid()
                    if g == 0 and n == 2:
                        turned_hi()
                    if g and n == 1:
                        h_squares(g - 1, h_fin, GROUPS + g)
            h_squares(GROUPS - 1, h_fin, 2 * GROUPS)
            act.wait_ge(h_sum, 2)
            mean(TILES, h_sums[:, :], D_MODEL, mean_done)

        @block.vector
        def _(dve):
            def split_lo(base, i, per, n, cols=UNIT):
                s = slot(base, n)
                dve.wait_ge(hi_ready, i * per + (base + n + 1))
                dve.tensor_tensor(w_lo[:, s, 0:cols], w_raw[:, s, 0:cols], w_hi[:, s, 0:cols].bitcast(fp32),
                                  ALU.subtract).then_inc(lo_ready, 1)

            dve.wait_ge(const_ready, 4 * 16)
            dve.tensor_tensor(lb_tmp[:, 2, :], lb_in[:, 0:HG_HEADS], lb_in[:, HG_HEADS:], ALU.max).then_inc(lb_step, 1)
            dve.wait_ge(lb_step, 1)
            for layer in range(2):
                dve.tensor_tensor(lb_tmp[:, layer, :], lb_in[:, layer * HG_HEADS:(layer + 1) * HG_HEADS],
                                  lb_tmp[:, 2, :], ALU.subtract).then_inc(lb_step, 1)
            dve.tensor_copy(level_sb[:, :], level_raw[:, :]).then_inc(level_ready, 1)
            dve.wait_ge(norm_ready, 1)
            for t in range(TILES):
                dve.tensor_scalar(h[:, t, :], h[:, t, :], rnorm[:, t:t + 1], None, ALU.mult).then_inc(scaled, 1)
            for n in range(AHEAD):
                split_lo(A0, 0, A_UNITS, n)
            dve.wait_ge(lb_exp, 1)
            dve.tensor_tensor(lb_tmp[:, 2, :], lb_tmp[:, 0, :], lb_tmp[:, 1, :], ALU.add).then_inc(lb_step, 1)
            dve.wait_ge(lb_step, 4)
            dve.reciprocal(lb_tmp[:, 2, :], lb_tmp[:, 2, :]).then_inc(lb_step, 1)
            dve.wait_ge(lb_step, 5)
            dve.tensor_tensor(lb[:, :], lb_tmp[:, 0, :], lb_tmp[:, 2, :], ALU.mult).then_inc(lb_step, 1)
            dve.wait_ge(lb_step, 6)
            dve.tensor_scalar(one_lb[:, :], lb[:, :], -1.0, 1.0, ALU.mult, ALU.add).then_inc(lb_step, 1)
            for kt in range(KT):
                dve.wait_ge(n_hi, kt // 2 * 2 + 2)
                lo_part(dve, nT_lo[:, kt, :], ps[:, kt * TOKENS:(kt + 1) * TOKENS], g_hg[:, kt:kt + 1],
                        nT_hi[:, kt, :]).then_inc(n_lo, 1)

            def y_out(jp):
                def gated():
                    dve.wait_ge(gsig_ready, jp + 1)
                    flat = gate[:, :, :].rearrange("p t n -> p (t n)")
                    dve.tensor_tensor(flat, bank(4, 2), flat, ALU.mult).then_inc(silu_ready, 1)
                    dve.wait_ge(silu_ready, jp + 1)
                    dve.wait_ge(o_norm, jp + 1)
                    for t in range(TILES):
                        for e in range(2):
                            cols = gate[:, t, e * HG_VAL:(e + 1) * HG_VAL]
                            i = 2 * t + e
                            last = dve.scalar_tensor_tensor(
                                out=cols, in0=ps[:, 6 * 512 + i * HG_VAL:6 * 512 + (i + 1) * HG_VAL],
                                scalar=rnorm[:, i:i + 1], in1=cols, op0=ALU.mult, op1=ALU.mult)
                    last.then_inc(y_ready, 1)

                def turned_lo():
                    dve.wait_ge(y_hi, jp + 1)
                    for c in range(4):
                        last = lo_part(dve, aT_lo[:, ds(jp * 4 + c, 1), :], ps[:, 4 * 512 + c * 256:4 * 512 + (c + 1) * 256],
                                       g_o[:, c % 2:c % 2 + 1], aT_hi[:, ds(jp * 4 + c, 1), :])
                    last.then_inc(y_lo, 1)
                return gated, turned_lo

            def a_step(j, first):
                def q_decay(blk):
                    head, tile = divmod(blk, 2)
                    dve.wait_ge(kdec_ready, j * 4 + (blk + 1))
                    cols = qT[:, head * TOKENS + tile * 128:head * TOKENS + tile * 128 + 128]
                    dve.tensor_tensor(decay[blk % 2], decay[blk % 2], cols[:, None, :].to_broadcast([128, LEVELS, 128]),
                                      ALU.mult).then_inc(qdec_ready, 1)

                def mask_scores(blk):
                    head, tile = divmod(blk, 2)
                    dve.wait_ge(score_done, j * 4 + (blk + 1))
                    d = decay[blk % 2]
                    dve.tensor_tensor(d[:, 0:7, :], ps[:, 6 * 512:6 * 512 + MASK_COLS].rearrange("p (l t) -> p l t", l=7),
                                      mask_sb[:, :].rearrange("p (l t) -> p l t", l=7), ALU.mult).then_inc(masked, 1)
                    dve.wait_ge(masked, j * 4 + (blk + 1))
                    dve.tensor_reduce(att[:, head, tile, :], d[:, 0:7, :].rearrange("p l t -> p t l"), AX.X,
                                      ALU.add).then_inc(att_ready, 1)

                if not first:
                    gated, turned_lo = y_out(j - 1)
                for n in range(A_UNITS):
                    split_lo(A0, j, A_UNITS, n + AHEAD)
                    if n == 0 and not first:
                        gated()
                    if n == 2 and not first:
                        turned_lo()
                    if n == 7:
                        dve.wait_ge(unit_done, j * A_UNITS + 8)
                        dve.tensor_copy(qT[:, :], bank(0)).then_inc(q_ready, 1)
                        dve.wait_ge(sig_ready, j * 2 + 1)
                        dve.tensor_scalar(logf[:, :], logf[:, :], SMALLEST_F, None, ALU.max).then_inc(sig_clamped, 1)
                        dve.wait_ge(sig_ready, j * 2 + 2)
                        if first:
                            dve.wait_ge(lb_step, 7)
                        for e in range(2):
                            head = kT[:, e * TOKENS:(e + 1) * TOKENS]
                            last = dve.tensor_scalar(head, head, one_lb[:, ds(j * 2 + e, 1)], None, ALU.mult)
                        last.then_inc(k_ready, 1)
                    if n == 9:
                        dve.wait_ge(ghi_ready, j + 1)
                        dve.tensor_tensor(g_lo[:, :], bank(6), g_hi[:, :].bitcast(fp32), ALU.subtract).then_inc(glo_ready, 1)
                    if n in (11, 12, 14, 16):
                        q_decay((11, 12, 14, 16).index(n))
                    if n in (13, 15, 17, 19):
                        mask_scores((13, 15, 17, 19).index(n))

            a_step(0, True)
            with dve.Fori(1, STEPS) as j:
                a_step(j, False)

            def residual(g, stream, banks, done):
                dve.wait_ge(unit_done, done)
                cols = stream[:, :, g * 512:(g + 1) * 512]
                dve.tensor_tensor(cols, bank(banks, 2).rearrange("p (t n) -> p t n", t=TILES), cols,
                                  ALU.add).then_inc(h_ready, 1)

            def stream_sum(squares, done):
                dve.wait_ge(h_sq, squares)
                dve.tensor_reduce(h_sums[:, :], sums[:, 8:16].rearrange("p (t g) -> p t g", t=TILES), AX.X,
                                  ALU.add).then_inc(h_sum, 1)

            gated, turned_lo = y_out(STEPS - 1)
            for g in range(GROUPS):
                for n in range(O_UNITS):
                    split_lo(WO0, g, O_UNITS, n + AHEAD)
                    if g == 0 and n == 0:
                        gated()
                    if g == 0 and n == 2:
                        turned_lo()
                    if g and n == 0:
                        if g == 1:
                            dve.wait_ge(x_again, 16)
                        residual(g - 1, h, 2 * ((g - 1) % 2), WO0 + g * O_UNITS)
            residual(GROUPS - 1, h, 2 * ((GROUPS - 1) % 2), KV0)
            stream_sum(TILES * GROUPS, 1)
            dve.wait_ge(norm_ready, 2)
            dve.wait_ge(h_stored, 16)
            for t in range(TILES):
                dve.tensor_scalar(h[:, t, :], h[:, t, :], rnorm[:, t:t + 1], None, ALU.mult).then_inc(scaled, 1)
            for batch, which in STREAM_ORDER:
                hi, lo, gain = ((aT_hi, aT_lo, g_kvin), (nT_hi, nT_lo, g_mla))[which]
                for e in range(2):
                    kt = 2 * batch + e
                    dve.wait_ge(n_hi, KT + 4 * batch + 4)
                    lo_part(dve, lo[:, kt, :], ps[:, kt * TOKENS:(kt + 1) * TOKENS], gain[:, kt:kt + 1],
                            hi[:, kt, :]).then_inc(n_lo, 1)

            for n in range(C_UNITS + CQ_UNITS):
                split_lo(KV0, 0, 0, n + AHEAD)
                if n == 7:
                    dve.wait_ge(c_norm, 1)
                    for t in range(TILES):
                        dve.tensor_scalar(c_nat[:, t, :], bank(t), rnorm[:, t:t + 1], None, ALU.mult).then_inc(c_scaled, 1)
                    dve.memset(k_even[:, :], 0.0).then_inc(kr_step, 1)
                    dve.memset(k_odd[:, :], 0.0).then_inc(kr_step, 1)
                if n == 11:
                    for kt in range(KT_C):
                        dve.wait_ge(c_hi, kt // 2 * 2 + 2)
                        lo_part(dve, cT_lo[:, kt, :], ps[:, kt * TOKENS:(kt + 1) * TOKENS], g_c[:, kt:kt + 1],
                                cT_hi[:, kt, :]).then_inc(c_lo, 1)
                    dve.wait_ge(kr_rot, 1)
                    dve.tensor_tensor(rot_sb[:, 1, :], bank(2)[:, 256:512], sin_sb, ALU.mult).then_inc(kr_step, 1)
                    dve.tensor_tensor(rot_sb[:, 0, :], rot_sb[:, 0, :], cos_sb, ALU.mult).then_inc(kr_step, 1)
                    dve.wait_ge(kr_step, 4)
                    dve.tensor_tensor(k_even[0:64, :], rot_sb[0:64, 0, :], rot_sb[0:64, 1, :], ALU.add).then_inc(kr_step, 1)
                    dve.tensor_tensor(k_odd[64:128, :], rot_sb[64:128, 0, :], rot_sb[64:128, 1, :], ALU.add).then_inc(kr_step, 1)
            dve.wait_ge(c_sq, 6)
            dve.tensor_reduce(sums[:, 6:8], sums[:, 2:6].rearrange("p (t g) -> p t g", t=TILES), AX.X,
                              ALU.add).then_inc(cq_sum, 1)
            dve.wait_ge(c_norm, 2)
            for t in range(TILES):
                dve.tensor_scalar(cq_nat[t][:, 0:512], bank(3 + t), rnorm[:, t:t + 1], None, ALU.mult).then_inc(c_scaled, 1)
                dve.tensor_scalar(cq_nat[t][:, 512:Q_LORA], bank(5 + t)[:, 0:256], rnorm[:, t:t + 1], None,
                                  ALU.mult).then_inc(c_scaled, 1)

            def yb_out(jp):
                def gated():
                    dve.wait_ge(gbsig_ready, jp + 1)
                    flat = gate_b[:, :, :].rearrange("p t n -> p (t n)")
                    dve.tensor_tensor(flat, bank(2, 2), flat, ALU.mult).then_inc(bsilu_ready, 1)
                    dve.wait_ge(bsilu_ready, jp + 1)
                    dve.wait_ge(inv_ready, jp + 1)
                    dve.wait_ge(pv_done, jp * 2 + 2)
                    for pair in range(2):
                        for i in range(2):
                            for t in range(TILES):
                                m = 2 * pair + i
                                cols = gate_b[:, t, m * V_DIM:(m + 1) * V_DIM]
                                at = (4 + pair) * 512 + (2 * i + t) * V_DIM
                                last = dve.scalar_tensor_tensor(
                                    out=cols, in0=ps[:, at:at + V_DIM], scalar=row_sum[:, pair, 2 * i + t:2 * i + t + 1],
                                    in1=cols, op0=ALU.mult, op1=ALU.mult)
                    last.then_inc(yb_ready, 1)

                def turned_lo():
                    dve.wait_ge(yb_hi, jp + 1)
                    dve.tensor_tensor(aT_lo[:, ds(jp * 4, 4), :].rearrange("p c t -> p (c t)"), bank(6, 2),
                                      aT_hi[:, ds(jp * 4, 4), :].rearrange("p c t -> p (c t)").bitcast(fp32),
                                      ALU.subtract).then_inc(yb_lo, 1)
                return gated, turned_lo

            def b_step(j, first):
                def row_maxima(pair):
                    dve.wait_ge(s_done, j * 2 + (pair + 1))
                    if pair:
                        dve.wait_ge(pturn_done, j * 2 + 1)
                    dve.tensor_tensor(prob[:, :, :], bank(4 + 2 * pair, 2).rearrange("p (i n) -> p i n", i=2)[:, :, 0:384],
                                      causal[:, None, :].to_broadcast([128, 2, 384]), ALU.add).then_inc(score_masked, 1)
                    dve.wait_ge(score_masked, j * 2 + (pair + 1))
                    for t in range(TILES):
                        last = dve.tensor_reduce(row_max[:, pair, t, :], prob[:, :, 128 * t:128 + 256 * t], AX.X, ALU.max)
                    last.then_inc(max_ready, 1)
                    dve.wait_ge(max_ready, j * 2 + (pair + 1))
                    dve.tensor_scalar(row_max[:, pair, :, :], row_max[:, pair, :, :], -ATT_SCALE, None,
                                      ALU.mult).then_inc(neg_ready, 1)

                if not first:
                    gated, turned_lo = yb_out(j - 1)
                for n in range(B_UNITS):
                    split_lo(B0, j, B_UNITS, n + AHEAD, b_cols(n + AHEAD))
                    if n == 0 and not first:
                        gated()
                    if n == 1 and first:
                        for kt in range(KT_Q):
                            dve.wait_ge(c_hi, KT_C + KT_Q)
                            lo_part(dve, cqT_lo[:, kt, :], ps[:, 5 * 512 + kt * TOKENS:5 * 512 + (kt + 1) * TOKENS],
                                    g_q[:, kt:kt + 1], cqT_hi[:, kt, :]).then_inc(c_lo, 1)
                    if n == 2 and not first:
                        turned_lo()
                    if n == 3:
                        dve.wait_ge(unit_done, j * B_UNITS + (B0 + 4))
                        dve.tensor_copy(v_sb[:, :, :].rearrange("p t n -> p (t n)"), bank(2, 2)).then_inc(v_ready, 1)
                    if n == 7:
                        dve.wait_ge(unit_done, j * B_UNITS + (B0 + 8))
                        dve.tensor_copy(q_nope[:, :, :].rearrange("p h t -> p (h t)"), bank(4, 2)).then_inc(qn_ready, 1)
                    if n == 8:
                        dve.wait_ge(qr_rot, j + 1)
                        dve.tensor_tensor(rot_sb[:, :, :], bank(1).rearrange("p (i t) -> p i t", i=2),
                                          sin_sb[:, None, :].to_broadcast([128, 2, TOKENS]), ALU.mult).then_inc(qr_step, 1)
                        dve.tensor_tensor(q_rope[:, :, :], q_rope[:, :, :],
                                          cos_sb[:, None, :].to_broadcast([128, 2, TOKENS]), ALU.mult).then_inc(qr_step, 1)
                        dve.wait_ge(qr_step, j * 3 + 2)
                        dve.tensor_tensor(q_rope[:, :, :], q_rope[:, :, :], rot_sb[:, :, :], ALU.add).then_inc(qr_step, 1)
                    if n in (10, 12):
                        row_maxima((10, 12).index(n))
                    if n == 15:
                        dve.wait_ge(p_ready, j * 2 + 2)
                        dve.reciprocal(row_sum[:, :, :], row_sum[:, :, :]).then_inc(inv_ready, 1)

            b_step(0, True)
            with dve.Fori(1, STEPS) as j:
                b_step(j, False)

            gated, turned_lo = yb_out(STEPS - 1)
            for g in range(GROUPS):
                for n in range(O_UNITS):
                    if g * O_UNITS + n + AHEAD < GROUPS * O_UNITS:
                        split_lo(OUT0, g, O_UNITS, n + AHEAD)
                    if g == 0 and n == 0:
                        gated()
                    if g == 0 and n == 2:
                        turned_lo()
                    if g and n == 0:
                        if g == 1:
                            dve.wait_ge(h_back, 2 * 16)
                        residual(g - 1, h_fin, 2 * ((g - 1) % 2), OUT0 + g * O_UNITS)
            residual(GROUPS - 1, h_fin, 2 * ((GROUPS - 1) % 2), UNITS)
            stream_sum(2 * TILES * GROUPS, 2)
            dve.wait_ge(fin_norm, 1)
            for part in range(4):
                t, half = divmod(part, 2)
                cols = h_fin[:, t, half * 1024:(half + 1) * 1024]
                dve.scalar_tensor_tensor(out=cols, in0=cols, scalar=rnorm[:, t:t + 1],
                                         in1=final_sb[:, half * 1024:(half + 1) * 1024],
                                         op0=ALU.mult, op1=ALU.mult).then_inc(fin_scaled, 1)

        @block.tensor
        def _(pe):
            def natural(base, i, per, n, xT, kts, cols, banks, first, last):
                s = slot(base, n)
                pe.wait_ge(lo_ready, i * per + (base + n + 1))
                for e, kt in enumerate(kts):
                    w = slice(e * cols, (e + 1) * cols)
                    for t in range(TILES):
                        acc = bank(banks[t])[:, 0:cols]
                        tile = slice(t * 128, (t + 1) * 128)
                        pe.matmul(acc, xT[0][:, kt, tile], w_hi[:, s, w], start=first and e == 0, stop=False)
                        pe.matmul(acc, xT[0][:, kt, tile], w_lo[:, s, w], start=False, stop=False)
                        mm = pe.matmul(acc, xT[1][:, kt, tile], w_hi[:, s, w], start=False,
                                       stop=last and e == len(kts) - 1)
                return mm.then_inc(unit_done, 1)

            def turned_out(base, i, per, n, xT, parts):
                s = slot(base, n)
                pe.wait_ge(lo_ready, i * per + (base + n + 1))
                for place, kt, at, first, last in parts:
                    w = slice(place * 128, (place + 1) * 128)
                    acc = ps[:, at:at + TOKENS]
                    pe.matmul(acc, w_hi[:, s, w], xT[0][:, kt, :], start=first, stop=False, skip_group_check=True)
                    pe.matmul(acc, w_hi[:, s, w], xT[1][:, kt, :], start=False, stop=False, skip_group_check=True)
                    mm = pe.matmul(acc, w_lo[:, s, w], xT[0][:, kt, :], start=False, stop=last, skip_group_check=True)
                return mm.then_inc(unit_done, 1)

            nT = (nT_hi, nT_lo)
            aT = (aT_hi, aT_lo)
            cT = (cT_hi, cT_lo)
            cqT = (cqT_hi, cqT_lo)

            def turn_stream(wait):
                pe.wait_ge(scaled, wait)
                for kt in range(KT):
                    for t in range(TILES):
                        mm = pe.transpose(ps[:, kt * TOKENS + t * 128:kt * TOKENS + (t + 1) * 128],
                                          h[:, t, kt * 128:(kt + 1) * 128], ident)
                    if kt % 2:
                        mm.then_inc(turned, 1)

            pe.wait_ge(const_ready, 4 * 16)
            turn_stream(TILES)

            def turn_y(src, first_bank, done):
                for c in range(4):
                    for t in range(TILES):
                        at = first_bank * 512 + c * TOKENS + t * 128
                        mm = pe.transpose(ps[:, at:at + 128], src[:, t, c * 128:(c + 1) * 128], ident)
                mm.then_inc(done, 1)

            def a_step(j, first):
                def ranges(blk):
                    head, tile = divmod(blk, 2)
                    if blk == 0:
                        pe.wait_ge(glo_ready, j + 1)
                        pe.wait_ge(q_ready, j + 1)
                        if first:
                            pe.wait_ge(level_ready, 1)
                    else:
                        pe.wait_ge(decay_ready, j * 4 + blk)
                    g = slice(blk * 128, (blk + 1) * 128)
                    for half in range(2):
                        lev = level_sb[:, tile * 128 + half * 512:tile * 128 + (half + 1) * 512]
                        pe.matmul(bank(half), g_hi[:, g], lev, start=True, stop=False)
                        mm = pe.matmul(bank(half), g_lo[:, g], lev, start=False, stop=True)
                    mm.then_inc(range_done, 1)

                def scores(blk):
                    head, tile = divmod(blk, 2)
                    pe.wait_ge(qdec_ready, j * 4 + (blk + 1))
                    if blk:
                        pe.wait_ge(masked, j * 4 + blk)
                        if blk == 2:
                            pe.wait_ge(cross_ready, j * 2 + 1)
                    kd, qd = k_dec[tile], decay[tile]

                    def at(i, rows=slice(0, 128), cols=slice(0, 128)):
                        start = 6 * 512 + i * 128
                        return ps[rows, start + cols.start:start + cols.stop]

                    low, high, every = slice(0, 64), slice(64, 128), slice(0, 128)
                    l64, l32 = level_at(tile, 1), level_at(tile, 2)
                    pe.matmul(at(0, every, low), kd[:, l32, every], qd[:, l32, low], start=True, stop=True)
                    pe.matmul(at(0, low, high), kd[:, l64, low], qd[:, l64, high], start=True, stop=True)
                    pe.matmul(at(0, high, high), kd[:, l32, high], qd[:, l32, high], start=True, stop=True)
                    for i in range(5):
                        lev = level_at(tile, 3 + i)
                        pe.matmul(at(1 + i), kd[:, lev, :], qd[:, lev, :], start=True, stop=True)
                    own = slice(head * TOKENS + tile * 128, head * TOKENS + tile * 128 + 128)
                    mm = pe.matmul(at(6), kT[:, own], qT[:, own], start=True, stop=True)
                    if tile:
                        mm = pe.matmul(at(7), k_dec[0][:, level_at(0, 0), :], decay[1][:, level_at(1, 0), :],
                                       start=True, stop=True)
                    mm.then_inc(score_done, 1)

                for n in range(A_UNITS):
                    u = n % 8
                    kts = (2 * u, 2 * u + 1)
                    if n < 8:
                        if first:
                            pe.wait_ge(n_lo, max(2 * u + 2, 4))
                        elif n == 0:
                            pe.wait_ge(o_sq, j)
                        parts = [(4 * e + m, kts[e], m * TOKENS, u == 0 and e == 0 and m % 2 == 0, u == 7 and e == 1)
                                 for e in range(2) for m in range(4)]
                        turned_out(A0, j, A_UNITS, n, nT, parts)
                    elif n < 16:
                        if n == 8 and not first:
                            pe.wait_ge(val_ready, j)
                        natural(A0, j, A_UNITS, n, nT, kts, 512, (2, 3), u == 0, u == 7)
                    else:
                        if n == 16 and not first:
                            pe.wait_ge(y_lo, j)
                        natural(A0, j, A_UNITS, n, nT, kts, 512, (4, 5), u == 0, u == 7)
                    if n == 2 and not first:
                        pe.wait_ge(y_ready, j)
                        turn_y(gate, 4, yturn_done)
                    if n == 9:
                        pe.wait_ge(logf_ready, j * 2 + 2)
                        for i in range(4):
                            mm = pe.transpose(bank(6)[:, i * 128:(i + 1) * 128], logf[:, i * 128:(i + 1) * 128], ident)
                        mm.then_inc(gturn_done, 1)
                    if n in (11, 12, 14, 16):
                        ranges((11, 12, 14, 16).index(n))
                    if n in (13, 15, 17, 19):
                        scores((13, 15, 17, 19).index(n))
                    if n == 21:
                        pe.wait_ge(att_ready, j * 4 + 4)
                        pe.wait_ge(cross_ready, j * 2 + 2)
                        pe.wait_ge(val_ready, j + 1)
                        for e in range(2):
                            v = slice(e * HG_VAL, (e + 1) * HG_VAL)
                            pe.matmul(bank(6)[:, v], att[:, e, 0, :], val[:, 0, v], start=True, stop=True)
                            pe.matmul(bank(7)[:, v], att[:, e, 2, :], val[:, 0, v], start=True, stop=False)
                            mm = pe.matmul(bank(7)[:, v], att[:, e, 1, :], val[:, 1, v], start=False, stop=True)
                        mm.then_inc(o_done, 1)

            a_step(0, True)
            with pe.Fori(1, STEPS) as j:
                a_step(j, False)

            def project(base, h_before, y_count, extra, turn):
                for g in range(GROUPS):
                    for n in range(O_UNITS):
                        if g == 0 and n == 0:
                            extra(0)
                        if g == 1 and n == 0:
                            extra(1)
                        if g >= 2 and n == 0:
                            pe.wait_ge(h_ready, h_before + g - 1)
                        if g == 0 and n == O_UNITS - 2:
                            pe.wait_ge(y_count, STEPS)
                        b = 2 * (g % 2)
                        natural(base, g, O_UNITS, n, aT, (2 * n, 2 * n + 1), 512, (b, b + 1), n == 0, n == O_UNITS - 1)
                        if g == 0 and n == 2:
                            turn()

            def wo_banks(g):
                if g == 0:
                    pe.wait_ge(o_sq, STEPS)
                else:
                    pe.wait_ge(val_ready, STEPS)

            def wo_turn():
                pe.wait_ge(y_ready, STEPS)
                turn_y(gate, 4, yturn_done)

            project(WO0, 0, y_lo, wo_banks, wo_turn)

            turn_stream(2 * TILES)
            def rotated(dst, src):
                return pe.matmul(dst, rotate, src, start=True, stop=True)

            for n in range(C_UNITS + CQ_UNITS):
                if n < 8:
                    pe.wait_ge(n_lo, KT + 4 * max(2, n + 1))
                    natural(KV0, 0, 0, n, aT, (2 * n, 2 * n + 1), 512, (0, 1), n == 0, n == 7)
                elif n < C_UNITS:
                    if n == 8:
                        pe.wait_ge(n_lo, 3 * KT)
                    turned_out(KV0, 0, 0, n, aT, [(e, 8 * (n - 8) + e, 2 * 512, n == 8 and e == 0, n == 9 and e == 7)
                                                  for e in range(8)])
                elif n < C_UNITS + 8:
                    u = n - C_UNITS
                    natural(KV0, 0, 0, n, nT, (2 * u, 2 * u + 1), 512, (3, 4), u == 0, u == 7)
                else:
                    u = n - C_UNITS - 8
                    if u == 0:
                        pe.wait_ge(c_sq, 2)
                    natural(KV0, 0, 0, n, nT, range(4 * u, 4 * u + 4), 256, (5, 6), u == 0, u == 3)
                if n == 11:
                    pe.wait_ge(c_scaled, 2)
                    for kt in range(KT_C):
                        for t in range(TILES):
                            at = kt * TOKENS + t * 128
                            mm = pe.transpose(ps[:, at:at + 128], c_nat[:, t, kt * 128:(kt + 1) * 128], ident)
                    mm.then_inc(c_turned, 1)
                    pe.wait_ge(kr_raw, 1)
                    rotated(bank(2)[:, 256:512], rot_sb[:, 0, :]).then_inc(kr_rot, 1)

            def b_step(j, first):
                def head_scores(pair):
                    for i in range(2):
                        m = 2 * pair + i
                        key = (k_even, k_odd)[i]
                        for t in range(TILES):
                            q = slice(t * 128, (t + 1) * 128)
                            keys = slice(0, (t + 1) * 128)
                            at = (4 + 2 * pair + i) * 512 + 128 * t
                            acc = ps[:, at:at + (t + 1) * 128]
                            pe.matmul(acc, q_nope[:, m, q], k_nope[:, m, keys], start=True, stop=False)
                            mm = pe.matmul(acc, q_rope[:, pair, q], key[:, keys], start=False, stop=True)
                    mm.then_inc(s_done, 1)

                def turn_probs(pair):
                    pe.wait_ge(p_ready, j * 2 + (pair + 1))
                    for i in range(2):
                        for c in range(3):
                            at = (4 + 2 * pair + i) * 512 + c * 128
                            mm = pe.transpose(ps[:, at:at + 128], prob[:, i, c * 128:(c + 1) * 128], ident)
                    mm.then_inc(pturn_done, 1)

                def weigh_values(pair):
                    pe.wait_ge(pT_ready, j * 2 + (pair + 1))
                    for i in range(2):
                        v = slice((2 * pair + i) * V_DIM, (2 * pair + i + 1) * V_DIM)
                        at = (4 + pair) * 512 + i * 256
                        pe.matmul(ps[:, at:at + 128], probT[:, i, 0:128], v_sb[:, 0, v], start=True, stop=True)
                        pe.matmul(ps[:, at + 128:at + 256], probT[:, i, 128:256], v_sb[:, 0, v], start=True, stop=False)
                        mm = pe.matmul(ps[:, at + 128:at + 256], probT[:, i, 256:384], v_sb[:, 1, v], start=False, stop=True)
                    mm.then_inc(pv_done, 1)

                for n in range(B_UNITS):
                    if n < 2:
                        if first and n == 0:
                            pe.wait_ge(c_lo, KT_C)
                        parts = [(4 * e + m, 2 * n + e, m * TOKENS, n == 0 and e == 0 and m % 2 == 0, n == 1 and e == 1)
                                 for e in range(2) for m in range(4)]
                        turned_out(B0, j, B_UNITS, n, cT, parts)
                    elif n < 4:
                        if n == 2:
                            if first:
                                pe.wait_ge(c_scaled, 6)
                            else:
                                pe.wait_ge(bsilu_ready, j)
                        natural(B0, j, B_UNITS, n, cT, (2 * (n - 2), 2 * (n - 2) + 1), 512, (2, 3), n == 2, n == 3)
                    elif n < 8:
                        if n == 4:
                            pe.wait_ge(kn_ready, j + 1)
                            if first:
                                pe.wait_ge(c_lo, KT_C + KT_Q)
                            else:
                                pe.wait_ge(yb_ready, j)
                        parts = []
                        for place in range(9):
                            kt, m = divmod((n - 4) * 9 + place, 6)
                            at = (4 * 512 + m * TOKENS) if m < 4 else (m - 4) * TOKENS
                            parts.append((place, kt, at, kt == 0 and m % 2 == 0, kt == KT_Q - 1))
                        turned_out(B0, j, B_UNITS, n, cqT, parts)
                    else:
                        if n == 8:
                            pe.wait_ge(v_ready, j + 1)
                        u = n - 8
                        natural(B0, j, B_UNITS, n, nT, (2 * u, 2 * u + 1), 512, (2, 3), u == 0, u == 7)
                    if n == 0 and first:
                        pe.wait_ge(c_scaled, 6)
                        for kt in range(KT_Q):
                            for t in range(TILES):
                                at = 5 * 512 + kt * TOKENS + t * 128
                                mm = pe.transpose(ps[:, at:at + 128], cq_nat[t][:, kt * 128:(kt + 1) * 128], ident)
                        mm.then_inc(c_turned, 1)
                    if n == 2 and not first:
                        pe.wait_ge(yb_ready, j)
                        turn_y(gate_b, 6, ybturn_done)
                    if n == 8:
                        pe.wait_ge(qr_raw, j + 1)
                        rotated(bank(1), q_rope[:, :, :].rearrange("p i t -> p (i t)")).then_inc(qr_rot, 1)
                    if n == 10:
                        pe.wait_ge(qn_ready, j + 1)
                        pe.wait_ge(qr_step, j * 3 + 3)
                        if first:
                            pe.wait_ge(kr_step, 6)
                        head_scores(0)
                    if n == 12:
                        turn_probs(0)
                        if not first:
                            pe.wait_ge(yb_lo, j)
                        head_scores(1)
                    if n == 13:
                        weigh_values(0)
                    if n == 14:
                        turn_probs(1)
                    if n == 15:
                        weigh_values(1)

            b_step(0, True)
            with pe.Fori(1, STEPS) as j:
                b_step(j, False)

            def out_banks(g):
                if g == 1:
                    pe.wait_ge(bsilu_ready, STEPS)

            def out_turn():
                pe.wait_ge(yb_ready, STEPS)
                turn_y(gate_b, 6, ybturn_done)

            project(OUT0, GROUPS, yb_lo, out_banks, out_turn)


def level_matrices():
    import numpy as np
    s, t = np.arange(128)[:, None], np.arange(128)[None, :]
    mats = [(s > t)]
    for m in (64, 32, 16, 8, 4, 2, 1):
        mid = t // (2 * m) * (2 * m) + m
        mats.append(np.where(t >= mid, (s >= mid) & (s <= t), (s > t) & (s < mid)))
    mats.append(s <= t)
    return np.ascontiguousarray(np.concatenate(mats, axis=1).astype(np.float32))


def score_masks():
    import numpy as np
    s, t = np.arange(128)[:, None], np.arange(128)[None, :]
    before, differ = s < t, s ^ t
    masks = [before & (differ >= 32)]
    for m in (16, 8, 4, 2, 1):
        masks.append(before & (differ >= m) & (differ < 2 * m))
    masks.append(s == t)
    return np.ascontiguousarray(np.concatenate(masks, axis=1).astype(np.float32))


def constants():
    import numpy as np
    rot = np.zeros((128, 128), np.float32)
    for b in (0, 64):
        for i in range(32):
            rot[b + 32 + i, b + i] = -1.0
            rot[b + i, b + 32 + i] = 1.0
    pos = np.arange(TOKENS, dtype=np.float32)
    freq = (np.float32(10000.0) ** (-np.arange(0, ROPE, 2, dtype=np.float32) / np.float32(ROPE))).astype(np.float32)
    ang = np.tile((pos[:, None] * freq[None, :]).astype(np.float32).T, (4, 1))
    q, k = np.arange(128)[:, None], np.arange(128)[None, :]
    own = np.where(k <= q, 0.0, MASKED)
    causal = np.concatenate([own, np.zeros((128, 128)), own], axis=1)
    parts = [np.eye(128), rot, np.cos(ang), np.sin(ang), causal]
    return np.ascontiguousarray(np.concatenate([p.astype(np.float32) for p in parts], axis=1))


def units(w, rows_per_unit, cols):
    import numpy as np
    k, n = w.shape
    a = w.reshape(k // (128 * rows_per_unit), rows_per_unit, 128, n // cols, cols)
    return np.ascontiguousarray(a.transpose(3, 0, 2, 1, 4)).reshape(n // cols, -1, 128, rows_per_unit * cols)


def by_column(v):
    return v.reshape(-1, 128).T


def kernel(x, norm_g, hg_w_in, hg_g_norm, hg_w_out, hg_lb, kv_in_norm_g, w_kv_down, kv_norm_g,
           w_kv_up, mla_w_in, mla_q_norm_g, mla_w_q_up, mla_w_out, final_norm_g):
    import numpy as np
    import concourse.bacc as bacc
    from concourse import mybir
    from concourse.bass_utils import run_bass_kernel_spmd

    a = {k: np.asarray(v) for k, v in dict(
        x=x, norm_g=norm_g, w_in=hg_w_in, g_norm=hg_g_norm, w_o=hg_w_out, lb=hg_lb, kvin=kv_in_norm_g,
        kv=w_kv_down, kvn=kv_norm_g, up=w_kv_up, mw=mla_w_in, qn=mla_q_norm_g, qup=mla_w_q_up,
        mo=mla_w_out, fin=final_norm_g).items()}
    w_in = a["w_in"][0]
    key = HG_HEADS * KEY_DIM
    q, f = (w_in[:, i * key:(i + 1) * key].reshape(D_MODEL, STEPS, 256) for i in range(2))
    qf = np.concatenate([q, f], axis=2).reshape(D_MODEL, STEPS * 512)
    parts = [qf, w_in[:, 2 * key:2 * key + D_INNER], w_in[:, 2 * key + D_INNER:]]
    w_a = np.stack([units(p, 2, 512) for p in parts], axis=1).reshape(STEPS * A_UNITS, 128, UNIT)
    w_o = units(a["w_o"][0], 2, 512).reshape(-1, 128, UNIT)
    rope2 = np.concatenate([a["kv"][:, KV_LORA:]] * 2, axis=1)
    w_kv = np.concatenate([units(a["kv"][:, :KV_LORA], 2, 512).reshape(-1, 128, UNIT),
                           units(rope2, 8, 128).reshape(-1, 128, UNIT)])
    mw = a["mw"][0]
    w_cq = np.concatenate([units(mw[:, :512], 2, 512).reshape(-1, 128, UNIT),
                           units(mw[:, 512:Q_LORA], 4, 256).reshape(-1, 128, UNIT)])
    up = a["up"].reshape(KV_LORA, STEPS, 4, 2, 128)
    w_bkv = np.stack([units(up[:, :, :, i].reshape(KV_LORA, -1), 2, 512) for i in range(2)],
                     axis=1).reshape(-1, 128, UNIT)
    qup = a["qup"][0].reshape(Q_LORA, STEPS, 4, NOPE + ROPE)
    qcols = np.concatenate([qup[..., :NOPE].reshape(Q_LORA, STEPS, -1), qup[..., NOPE:].reshape(Q_LORA, STEPS, -1)], axis=2)
    w_bq = qcols.reshape(KT_Q, 128, STEPS, 6, 128).transpose(2, 0, 3, 1, 4).reshape(STEPS, 4, 9, 128, 128)
    w_bq = np.ascontiguousarray(w_bq.transpose(0, 1, 3, 2, 4)).reshape(-1, 128, UNIT_Q)
    w_bg = units(mw[:, Q_LORA:], 2, 512).reshape(-1, 128, UNIT)
    w_out = units(a["mo"][0], 2, 512).reshape(-1, 128, UNIT)
    gains = np.ascontiguousarray(np.concatenate(
        [by_column(v) for v in (a["norm_g"][0], a["norm_g"][1], a["kvin"], a["kvn"], a["qn"][0], a["g_norm"][0],
                                a["lb"][0], a["lb"][1])], axis=1))
    arrays = dict(w_a=w_a, w_o=w_o, w_kv=w_kv, w_cq=w_cq, w_bkv=w_bkv, w_bq=w_bq, w_bg=w_bg, w_out=w_out,
                  x=a["x"][0], consts=constants(), levels=level_matrices(), masks=score_masks(), gains=gains,
                  final_g=a["fin"].reshape(1, -1))
    arrays = {k: np.ascontiguousarray(v) for k, v in arrays.items()}

    nc = bacc.Bacc("TRN2", target_bir_lowering=False, num_devices=1)
    args = {k: nc.dram_tensor(k, v.shape, mybir.dt.from_np(v.dtype), kind="ExternalInput").ap()
            for k, v in arrays.items()}
    args["out"] = nc.dram_tensor("out", (1, TOKENS, D_MODEL), mybir.dt.float32, kind="ExternalOutput").ap()
    args["h_store"] = nc.dram_tensor("h_store", (TOKENS, D_MODEL), mybir.dt.float32, kind="Internal").ap()
    build(nc, **args)
    r = run_bass_kernel_spmd(nc, [arrays], core_ids=[0])
    return r.results[0]["out"]
```

```python
import concourse.bass as bass
from concourse import mybir
from contextlib import ExitStack

TOKENS = 256
TILES = TOKENS // 128
D_MODEL = 2048
D_INNER = 4096
KEY_DIM = 128
HG_HEADS = 16
HG_VAL = 256
MLA_HEADS = 32
Q_LORA = 768
KV_LORA = 512
NOPE = 128
ROPE = 64
V_DIM = 128
EPS = 1e-6
ATT_SCALE = float(NOPE + ROPE) ** -0.5
MASKED = -1e30
SMALLEST_F = 1e-19

KT = D_MODEL // 128
KT_INNER = D_INNER // 128
KT_Q = Q_LORA // 128
KT_C = KV_LORA // 128
UNIT = 1024
UNIT_Q = 1152
RING = 4
AHEAD = 3

STEPS = 8
A_UNITS = 24
B_UNITS = 16
GROUPS = D_MODEL // 512
O_UNITS = KT_INNER // 2
C_UNITS = 10
CQ_UNITS = 12
A0 = 0
WO0 = A0 + STEPS * A_UNITS
KV0 = WO0 + GROUPS * O_UNITS
CQ0 = KV0 + C_UNITS
B0 = CQ0 + CQ_UNITS
OUT0 = B0 + STEPS * B_UNITS
UNITS = OUT0 + GROUPS * O_UNITS

LEVELS = 8
SCORES_AT = (16, 17, 18, 19)
OUT_AT = 21
CONST_COLS = 128 + 128 + 256 + 256 + 384
LEVEL_COLS = 64
MASK_COLS = (LEVELS - 1) * LEVEL_COLS + 128
PAIR = 2 * TOKENS
GAIN_COLS = 3 * KT + KT_C + KT_Q + 2 + 2 * HG_HEADS


def build(nc, w_a, w_o, w_kv, w_cq, w_bkv, w_bq, w_bg, w_out, x, consts, masks, gains, final_g, out, h_store):
    fp32 = mybir.dt.float32
    f32r = mybir.dt.float32r
    ALU = mybir.AluOpType
    ACT = mybir.ActivationFunctionType
    AX = mybir.AxisListType
    ds = bass.ds

    ctx = ExitStack()
    with ctx:
        def sb(name, shape, dt=fp32, stack=ctx):
            return stack.enter_context(nc.sbuf_tensor(name, shape, dt))

        def sem(name):
            return ctx.enter_context(nc.semaphore(name))

        w_raw = sb("w_raw", [128, RING, UNIT_Q])
        w_hi = sb("w_hi", [128, RING, UNIT_Q], f32r)
        w_lo = sb("w_lo", [128, RING, UNIT_Q], f32r)
        aT_hi = sb("aT_hi", [128, KT_INNER, TOKENS], f32r)
        aT_lo = sb("aT_lo", [128, KT_INNER, TOKENS], f32r)
        nT_hi = sb("nT_hi", [128, KT, TOKENS], f32r)
        nT_lo = sb("nT_lo", [128, KT, TOKENS], f32r)
        const_sb = sb("const_sb", [128, CONST_COLS])
        gain_sb = sb("gain_sb", [128, GAIN_COLS])
        ident = const_sb[:, 0:128]
        rotate = const_sb[:, 128:256]
        cos_sb = const_sb[:, 256:512]
        sin_sb = const_sb[:, 512:768]
        causal = const_sb[:, 768:1152]
        g_hg = gain_sb[:, 0:KT]
        g_mla = gain_sb[:, KT:2 * KT]
        g_kvin = gain_sb[:, 2 * KT:3 * KT]
        g_c = gain_sb[:, 3 * KT:3 * KT + KT_C]
        g_q = gain_sb[:, 3 * KT + KT_C:3 * KT + KT_C + KT_Q]
        at = 3 * KT + KT_C + KT_Q
        g_o = gain_sb[:, at:at + 2]
        lb_in = gain_sb[:, at + 2:at + 2 + 2 * HG_HEADS]
        sums = sb("sums", [128, 16])
        rnorm = sb("rnorm", [128, 8])
        ms = sb("ms", [128, 8])
        minus_half = sb("minus_half", [128, 8])
        h_sums = sb("h_sums", [128, TILES])

        a_mem = ExitStack()
        h = sb("h", [128, TILES, D_MODEL], stack=a_mem)
        h_flat = h[:, :, :].rearrange("p t n -> p (t n)")
        qk_dec = h_flat.rearrange("p (l t) -> p l t", l=LEVELS)
        mask_sb = sb("mask_sb", [128, MASK_COLS], stack=a_mem)
        lb_tmp = sb("lb_tmp", [128, 3, HG_HEADS], stack=a_mem)
        lb = sb("lb", [128, HG_HEADS], stack=a_mem)
        one_lb = sb("one_lb", [128, HG_HEADS], stack=a_mem)
        qT = sb("qT", [128, 2 * TOKENS], stack=a_mem)
        kT = sb("kT", [128, 2 * TOKENS], stack=a_mem)
        logf = sb("logf", [128, 2 * TOKENS], stack=a_mem)
        behind = sb("behind", [128, 2 * TOKENS], stack=a_mem)
        att = sb("att", [128, 4, MASK_COLS], stack=a_mem)
        cross = sb("cross", [128, 2, 128], stack=a_mem)
        val = sb("val", [128, TILES, 512], stack=a_mem)
        gate = sb("gate", [128, TILES, 512], stack=a_mem)
        a_mem.close()

        b_mem = ExitStack()
        cT_hi = sb("cT_hi", [128, KT_C, TOKENS], f32r, stack=b_mem)
        cT_lo = sb("cT_lo", [128, KT_C, TOKENS], f32r, stack=b_mem)
        cqT_hi = sb("cqT_hi", [128, KT_Q, TOKENS], f32r, stack=b_mem)
        cqT_lo = sb("cqT_lo", [128, KT_Q, TOKENS], f32r, stack=b_mem)
        k_nope = sb("k_nope", [128, 4, TOKENS], stack=b_mem)
        q_nope = sb("q_nope", [128, 4, TOKENS], stack=b_mem)
        q_rope = sb("q_rope", [128, 2, TOKENS], stack=b_mem)
        rot_sb = sb("rot_sb", [128, 2, TOKENS], stack=b_mem)
        k_even = sb("k_even", [128, TOKENS], stack=b_mem)
        k_odd = sb("k_odd", [128, TOKENS], stack=b_mem)
        v_sb = sb("v_sb", [128, TILES, 512], stack=b_mem)
        prob = sb("prob", [128, 2, 384], stack=b_mem)
        probT = sb("probT", [128, 2, 384], stack=b_mem)
        gate_b = sb("gate_b", [128, TILES, 512], stack=b_mem)
        row_max = sb("row_max", [128, 2, TILES, 2], stack=b_mem)
        row_sum = sb("row_sum", [128, 2, 4], stack=b_mem)
        b_mem.close()
        q_flat = k_nope[:, :, :].rearrange("p h t -> p (h t)")
        c_nat = q_flat.rearrange("p (t n) -> p t n", t=TILES)
        cq_nat = [v_sb[:, :, :].rearrange("p t n -> p (t n)")[:, 0:Q_LORA],
                  gate_b[:, :, :].rearrange("p t n -> p (t n)")[:, 0:Q_LORA]]

        f_mem = ExitStack()
        h_fin = sb("h_fin", [128, TILES, D_MODEL], stack=f_mem)
        final_sb = sb("final_sb", [128, D_MODEL], stack=f_mem)
        f_mem.close()

        ps = ctx.enter_context(nc.psum_tensor("ps", [128, 8 * 512], fp32))

        def bank(b, n=1):
            return ps[:, b * 512:(b + n) * 512]

        raw_ready = [sem(f"raw_ready{i}") for i in range(RING)]
        x_ready = sem("x_ready")
        const_ready = sem("const_ready")
        x_again = [sem(f"x_again{g}") for g in range(GROUPS)]
        h_stored = sem("h_stored")
        h_back = [sem(f"h_back{g}") for g in range(GROUPS)]
        gain_back = sem("gain_back")
        out_stored = sem("out_stored")
        hi_ready = sem("hi_ready")
        lo_ready = sem("lo_ready")
        unit_done = sem("unit_done")
        sq_done = sem("sq_done")
        mean_done = sem("mean_done")
        norm_ready = sem("norm_ready")
        scaled = sem("scaled")
        turned = sem("turned")
        n_hi = sem("n_hi")
        n_lo = sem("n_lo")
        half_ready = sem("half_ready")
        lb_step = sem("lb_step")
        lb_exp = sem("lb_exp")
        sig_ready = sem("sig_ready")
        sig_clamped = sem("sig_clamped")
        logf_ready = sem("logf_ready")
        q_ready = sem("q_ready")
        k_ready = sem("k_ready")
        behind_clear = sem("behind_clear")
        behind_added = sem("behind_added")
        range_ready = sem("range_ready")
        decay_ready = sem("decay_ready")
        qk_ready = sem("qk_ready")
        att_step = sem("att_step")
        cross_ready = sem("cross_ready")
        score_done = sem("score_done")
        att_ready = sem("att_ready")
        val_ready = sem("val_ready")
        o_done = sem("o_done")
        o_sq = sem("o_sq")
        o_ms = sem("o_ms")
        o_norm = sem("o_norm")
        gsig_ready = sem("gsig_ready")
        silu_ready = sem("silu_ready")
        y_ready = sem("y_ready")
        yturn_done = sem("yturn_done")
        y_hi = sem("y_hi")
        y_lo = sem("y_lo")
        h_ready = sem("h_ready")
        h_sq = sem("h_sq")
        h_sum = sem("h_sum")
        c_sq = sem("c_sq")
        c_ms = sem("c_ms")
        c_norm = sem("c_norm")
        c_scaled = sem("c_scaled")
        c_turned = sem("c_turned")
        c_hi = sem("c_hi")
        c_lo = sem("c_lo")
        kr_raw = sem("kr_raw")
        kr_rot = sem("kr_rot")
        kr_step = sem("kr_step")
        cq_sum = sem("cq_sum")
        kn_ready = sem("kn_ready")
        v_ready = sem("v_ready")
        qn_ready = sem("qn_ready")
        qr_raw = sem("qr_raw")
        qr_rot = sem("qr_rot")
        qr_step = sem("qr_step")
        s_done = sem("s_done")
        score_masked = sem("score_masked")
        max_ready = sem("max_ready")
        neg_ready = sem("neg_ready")
        p_ready = sem("p_ready")
        pturn_done = sem("pturn_done")
        pT_ready = sem("pT_ready")
        pv_done = sem("pv_done")
        inv_ready = sem("inv_ready")
        gbsig_ready = sem("gbsig_ready")
        bsilu_ready = sem("bsilu_ready")
        yb_ready = sem("yb_ready")
        ybturn_done = sem("ybturn_done")
        yb_hi = sem("yb_hi")
        yb_lo = sem("yb_lo")
        fin_norm = sem("fin_norm")
        fin_scaled = sem("fin_scaled")

        block = ctx.enter_context(nc.Block())

        def slot(base, n):
            return (base + n) % RING

        def known(v):
            return isinstance(v, int)

        def lo_part(dve, dst, src, gain, high):
            return dve.scalar_tensor_tensor(out=dst, in0=src, scalar=gain, in1=high.bitcast(fp32),
                                            op0=ALU.mult, op1=ALU.subtract)

        def b_cols(n):
            return UNIT_Q if 4 <= n % B_UNITS < 8 else UNIT

        def halves(ap, level):
            m = 1 << level
            v = ap.rearrange("p (b i m) -> p b i m", i=2, m=m)
            return v[:, :, 0, :], v[:, :, 1, :]

        STREAM_ORDER = [(b, w) for b in range(KT // 2) for w in range(2)]

        @block.sync
        def _(sp):
            sp.dma_start(h[:, :, :], x.rearrange("(t p) n -> p t n", p=128)).then_inc(x_ready, 16)
            sp.dma_start(const_sb[:, :], consts).then_inc(const_ready, 16)
            sp.dma_start(gain_sb[:, :], gains).then_inc(const_ready, 16)
            sp.dma_start(mask_sb[:, :], masks).then_inc(const_ready, 16)

            def load(unit, s, src, cols):
                if not known(unit) or unit >= RING:
                    sp.wait_ge(lo_ready, unit - (RING - 1))
                sp.dma_start(w_raw[:, s, 0:cols], src).then_inc(raw_ready[s], 16)

            for n in range(RING):
                load(n, n, w_a[n], UNIT)
            with sp.Fori(1, STEPS * A_UNITS // RING) as i:
                for n in range(RING):
                    load(i * RING + n, n, w_a[i * RING + n], UNIT)
            for n in range(RING):
                load(WO0 + n, slot(WO0, n), w_o[n], UNIT)
            sp.wait_ge(score_done, 4 * STEPS)
            for i in range(1, GROUPS * O_UNITS // RING):
                if i <= GROUPS:
                    cols = slice((i - 1) * 512, i * 512)
                    sp.dma_start(h[:, :, cols], x.rearrange("(t p) n -> p t n", p=128)[:, :, cols]).then_inc(x_again[i - 1], 16)
                for n in range(RING):
                    load(WO0 + i * RING + n, n, w_o[i * RING + n], UNIT)
            for n in range(RING):
                load(KV0 + n, slot(KV0, n), w_kv[n], UNIT)
            sp.wait_ge(h_ready, GROUPS)
            sp.dma_start(h_store.rearrange("(t p) n -> p t n", p=128), h[:, :, :]).then_inc(h_stored, 16)
            for n in range(RING, C_UNITS):
                load(KV0 + n, slot(KV0, n), w_kv[n], UNIT)
            for n in range(CQ_UNITS):
                load(CQ0 + n, slot(CQ0, n), w_cq[n], UNIT)
            with sp.Fori(0, STEPS) as j:
                for n in range(B_UNITS):
                    src = w_bkv[j * 4 + n] if n < 4 else w_bq[j * 4 + (n - 4)] if n < 8 else w_bg[j * 8 + (n - 8)]
                    load(j * B_UNITS + (B0 + n), slot(B0, n), src, b_cols(n))
            for n in range(2 * RING):
                load(OUT0 + n, slot(OUT0, n), w_out[n], UNIT)
            sp.wait_ge(yb_lo, STEPS)
            sp.wait_ge(h_stored, 16)
            for i in range(2, GROUPS * O_UNITS // RING):
                if i < 2 + GROUPS:
                    cols = slice((i - 2) * 512, (i - 1) * 512)
                    sp.dma_start(h_fin[:, :, cols], h_store.rearrange("(t p) n -> p t n", p=128)[:, :, cols]).then_inc(h_back[i - 2], 16)
                if i == 2 + GROUPS:
                    sp.dma_start(final_sb[:, :], final_g.partition_broadcast(128)).then_inc(gain_back, 16)
                for n in range(RING):
                    load(OUT0 + i * RING + n, slot(OUT0, n), w_out[i * RING + n], UNIT)
            for part in range(4):
                tile, half = divmod(part, 2)
                sp.wait_ge(fin_scaled, part + 1)
                sp.dma_start(out[0, tile * 128:(tile + 1) * 128, half * 1024:(half + 1) * 1024],
                             h_fin[:, tile, half * 1024:(half + 1) * 1024]).then_inc(out_stored, 16)
            sp.wait_ge(out_stored, 4 * 16)

        @block.gpsimd
        def _(pool):
            pool.memset(minus_half[:, :], -0.5).then_inc(half_ready, 1)
            pool.wait_ge(half_ready, 1)

            def rsqrt(n, done):
                pool.tensor_tensor(rnorm[:, 0:n], ms[:, 0:n], minus_half[:, 0:n], ALU.pow).then_inc(done, 1)

            pool.wait_ge(mean_done, 1)
            rsqrt(TILES, norm_ready)

            def a_step(j):
                pool.memset(behind[:, :], 0.0).then_inc(behind_clear, 1)
                pool.wait_ge(behind_clear, j + 1)
                for level in range(LEVELS - 1):
                    pool.wait_ge(decay_ready, j * LEVELS + (level + 1))
                    m = 1 << level
                    to_first, _ = halves(behind[:, :], level)
                    f_first, f_second = halves(logf[:, :], level)
                    shape = [128, PAIR // (2 * m), m]
                    pool.tensor_tensor(to_first, to_first, f_second[:, :, m - 1:m].to_broadcast(shape),
                                       ALU.add).then_inc(behind_added, 1)
                    pool.wait_ge(behind_added, j * (LEVELS - 1) + (level + 1))
                    pool.tensor_tensor(f_second, f_second, f_first[:, :, m - 1:m].to_broadcast(shape),
                                       ALU.add).then_inc(range_ready, 1)
                    if level < LEVELS - 2:
                        pool.wait_ge(range_ready, j * (LEVELS - 1) + (level + 1))
                pool.wait_ge(o_ms, j + 1)
                rsqrt(4, o_norm)

            with pool.Fori(0, STEPS) as j:
                a_step(j)

            pool.wait_ge(mean_done, 2)
            rsqrt(TILES, norm_ready)
            pool.wait_ge(c_ms, 1)
            pool.wait_ge(scaled, 2 * TILES)
            rsqrt(TILES, c_norm)
            pool.wait_ge(c_ms, 2)
            pool.wait_ge(c_scaled, TILES)
            rsqrt(TILES, c_norm)
            pool.wait_ge(mean_done, 3)
            rsqrt(TILES, fin_norm)

        @block.scalar
        def _(act):
            def split_hi(base, i, per, n, cols=UNIT):
                s = slot(base, n)
                turn = (base + n - s) // RING + 1
                act.wait_ge(raw_ready[s], i * (per // RING * 16) + 16 * turn)
                if not known(i) or base + i * per + n >= RING:
                    act.wait_ge(unit_done, i * per + (base + n - RING + 1))
                act.activation(w_hi[:, s, 0:cols], w_raw[:, s, 0:cols], ACT.Copy).then_inc(hi_ready, 1)

            def mean(n, src, width, done):
                act.activation(ms[:, 0:n], src, ACT.Copy, scale=1.0 / width, bias=EPS).then_inc(done, 1)

            act.wait_ge(x_ready, 16)
            for t in range(TILES):
                act.activation(bank(4 * t, 4), h[:, t, :], ACT.Square, accum_out=sums[:, t:t + 1]).then_inc(sq_done, 1)
            act.wait_ge(sq_done, TILES)
            mean(TILES, sums[:, 0:TILES], D_MODEL, mean_done)
            for n in range(AHEAD):
                split_hi(A0, 0, A_UNITS, n)
            act.wait_ge(lb_step, 3)
            act.activation(lb_tmp[:, 0:2, :], lb_tmp[:, 0:2, :], ACT.Exp).then_inc(lb_exp, 1)

            for kt in range(KT):
                act.wait_ge(turned, kt // 2 + 1)
                act.activation(nT_hi[:, kt, :], ps[:, kt * TOKENS:(kt + 1) * TOKENS], ACT.Copy,
                               scale=g_hg[:, kt:kt + 1]).then_inc(n_hi, 1)

            def y_out(jp):
                def gate_sigmoid():
                    act.wait_ge(unit_done, jp * A_UNITS + A_UNITS)
                    act.activation(gate[:, :, :].rearrange("p t n -> p (t n)"), bank(4, 2),
                                   ACT.Sigmoid).then_inc(gsig_ready, 1)

                def turned_hi():
                    act.wait_ge(yturn_done, jp + 1)
                    for c in range(4):
                        last = act.activation(aT_hi[:, ds(jp * 4 + c, 1), :], ps[:, 4 * 512 + c * 256:4 * 512 + (c + 1) * 256],
                                              ACT.Copy, scale=g_o[:, c % 2:c % 2 + 1])
                    last.then_inc(y_hi, 1)
                return gate_sigmoid, turned_hi

            def a_step(j, first):
                if not first:
                    gate_sigmoid, turned_hi = y_out(j - 1)
                for n in range(A_UNITS):
                    split_hi(A0, j, A_UNITS, n + AHEAD)
                    if n == 0 and not first:
                        gate_sigmoid()
                    if n == 2 and not first:
                        turned_hi()
                    if n == 7:
                        act.wait_ge(unit_done, j * A_UNITS + 8)
                        act.activation(logf[:, :], bank(1), ACT.Sigmoid).then_inc(sig_ready, 1)
                        act.activation(kT[:, :], bank(1), ACT.Sigmoid, scale=-1.0).then_inc(sig_ready, 1)
                        act.wait_ge(sig_clamped, j + 1)
                        if first:
                            act.wait_ge(lb_step, 7)
                        for e in range(2):
                            head = logf[:, e * TOKENS:(e + 1) * TOKENS]
                            act.activation(head, head, ACT.Ln, scale=one_lb[:, ds(j * 2 + e, 1)],
                                           bias=lb[:, ds(j * 2 + e, 1)]).then_inc(logf_ready, 1)
                    if 8 <= n < 8 + LEVELS:
                        level = n - 8
                        if level == 0:
                            act.wait_ge(logf_ready, j * 2 + 2)
                            act.wait_ge(behind_clear, j + 1)
                        else:
                            act.wait_ge(range_ready, j * (LEVELS - 1) + level)
                        into = halves(qk_dec[:, level, :], level)
                        act.activation(into[0], halves(behind[:, :], level)[0], ACT.Exp)
                        act.activation(into[1], halves(logf[:, :], level)[1], ACT.Exp).then_inc(decay_ready, 1)
                    if n == 17:
                        act.wait_ge(unit_done, j * A_UNITS + 16)
                        act.activation(val[:, :, :].rearrange("p t n -> p (t n)"), bank(2, 2), ACT.Copy).then_inc(val_ready, 1)
                    if n == OUT_AT:
                        act.wait_ge(o_done, j + 1)
                        act.wait_ge(att_ready, j * 4 + 4)
                        for i in range(4):
                            last = act.activation(ps[:, i * 256:(i + 1) * 256], ps[:, 6 * 512 + i * 256:6 * 512 + (i + 1) * 256],
                                                  ACT.Square, accum_out=sums[:, i:i + 1])
                        last.then_inc(o_sq, 1)
                        act.wait_ge(o_sq, j + 1)
                        mean(4, sums[:, 0:4], HG_VAL, o_ms)

            a_step(0, True)
            with act.Fori(1, STEPS) as j:
                a_step(j, False)

            def h_squares(g, stream, done):
                act.wait_ge(h_ready, done)
                for t in range(TILES):
                    act.activation(bank(6 + t), stream[:, t, g * 512:(g + 1) * 512], ACT.Square,
                                   accum_out=sums[:, 8 + 4 * t + g:9 + 4 * t + g]).then_inc(h_sq, 1)

            gate_sigmoid, turned_hi = y_out(STEPS - 1)
            for g in range(GROUPS):
                for n in range(O_UNITS):
                    split_hi(WO0, g, O_UNITS, n + AHEAD)
                    if g == 0 and n == 0:
                        gate_sigmoid()
                    if g == 0 and n == 2:
                        turned_hi()
                    if g and n == 1:
                        h_squares(g - 1, h, g)
            h_squares(GROUPS - 1, h, GROUPS)
            act.wait_ge(h_sum, 1)
            mean(TILES, h_sums[:, :], D_MODEL, mean_done)

            def stream_hi(batch, which):
                dst, gain = ((aT_hi, g_kvin), (nT_hi, g_mla))[which]
                act.wait_ge(turned, KT // 2 + batch + 1)
                for kt in (2 * batch, 2 * batch + 1):
                    act.activation(dst[:, kt, :], ps[:, kt * TOKENS:(kt + 1) * TOKENS], ACT.Copy,
                                   scale=gain[:, kt:kt + 1]).then_inc(n_hi, 1)
            for batch, which in STREAM_ORDER:
                stream_hi(batch, which)

            for n in range(C_UNITS + CQ_UNITS):
                split_hi(KV0, 0, 0, n + AHEAD)
                if n == 7:
                    act.wait_ge(unit_done, KV0 + 8)
                    act.wait_ge(n_lo, 3 * KT)
                    for t in range(TILES):
                        act.activation(bank(5 + t), bank(t), ACT.Square, accum_out=sums[:, t:t + 1]).then_inc(c_sq, 1)
                    act.wait_ge(c_sq, 2)
                    mean(TILES, sums[:, 0:TILES], KV_LORA, c_ms)
                if n == 9:
                    act.wait_ge(unit_done, KV0 + C_UNITS)
                    act.activation(rot_sb[:, 0, :], bank(2)[:, 0:TOKENS], ACT.Copy).then_inc(kr_raw, 1)
                if n == 11:
                    act.wait_ge(c_turned, 1)
                    for kt in range(KT_C):
                        act.activation(cT_hi[:, kt, :], ps[:, kt * TOKENS:(kt + 1) * TOKENS], ACT.Copy,
                                       scale=g_c[:, kt:kt + 1]).then_inc(c_hi, 1)
            act.wait_ge(unit_done, B0)
            for t in range(TILES):
                act.wait_ge(kr_step, 6)
                act.wait_ge(c_sq, 2 + 2 * t)
                act.activation(bank(7), bank(3 + t), ACT.Square, accum_out=sums[:, 2 + 2 * t:3 + 2 * t]).then_inc(c_sq, 1)
                act.activation(bank(2)[:, 0:256], bank(5 + t)[:, 0:256], ACT.Square, accum_out=sums[:, 3 + 2 * t:4 + 2 * t]).then_inc(c_sq, 1)
            act.wait_ge(cq_sum, 1)
            mean(TILES, sums[:, 6:8], Q_LORA, c_ms)

            def yb_out(jp):
                def gate_sigmoid():
                    act.wait_ge(unit_done, jp * B_UNITS + (B0 + B_UNITS))
                    act.activation(gate_b[:, :, :].rearrange("p t n -> p (t n)"), bank(2, 2),
                                   ACT.Sigmoid).then_inc(gbsig_ready, 1)

                def turned_hi():
                    act.wait_ge(ybturn_done, jp + 1)
                    act.activation(aT_hi[:, ds(jp * 4, 4), :].rearrange("p c t -> p (c t)"), bank(6, 2), ACT.Copy).then_inc(yb_hi, 1)
                return gate_sigmoid, turned_hi

            def b_step(j, first):
                if not first:
                    gate_sigmoid, turned_hi = yb_out(j - 1)
                for n in range(B_UNITS):
                    split_hi(B0, j, B_UNITS, n + AHEAD, b_cols(n + AHEAD))
                    if n == 0 and not first:
                        gate_sigmoid()
                    if n == 1:
                        act.wait_ge(unit_done, j * B_UNITS + (B0 + 2))
                        act.activation(k_nope[:, :, :].rearrange("p h t -> p (h t)"), bank(0, 2), ACT.Copy).then_inc(kn_ready, 1)
                        if first:
                            act.wait_ge(c_turned, 2)
                            for kt in range(KT_Q):
                                act.activation(cqT_hi[:, kt, :], ps[:, 5 * 512 + kt * TOKENS:5 * 512 + (kt + 1) * TOKENS],
                                               ACT.Copy, scale=g_q[:, kt:kt + 1]).then_inc(c_hi, 1)
                    if n == 2 and not first:
                        turned_hi()
                    if n == 7:
                        act.wait_ge(unit_done, j * B_UNITS + (B0 + 8))
                        act.activation(q_rope[:, :, :].rearrange("p h t -> p (h t)"), bank(0), ACT.Copy).then_inc(qr_raw, 1)
                    if n in (12, 14):
                        pair = (12, 14).index(n)
                        act.wait_ge(pturn_done, j * 2 + (pair + 1))
                        act.activation(probT[:, :, :], bank(4 + 2 * pair, 2).rearrange("p (i n) -> p i n", i=2)[:, :, 0:384],
                                       ACT.Copy).then_inc(pT_ready, 1)
                    if n in (10, 12):
                        pair = (10, 12).index(n)
                        act.wait_ge(neg_ready, j * 2 + (pair + 1))
                        for i in range(2):
                            for t in range(TILES):
                                cols = prob[:, i, 128 * t:128 + 256 * t]
                                last = act.activation(cols, cols, ACT.Exp, scale=ATT_SCALE, bias=row_max[:, pair, t, i:i + 1],
                                                      accum_out=row_sum[:, pair, 2 * i + t:2 * i + t + 1])
                        last.then_inc(p_ready, 1)

            b_step(0, True)
            with act.Fori(1, STEPS) as j:
                b_step(j, False)

            gate_sigmoid, turned_hi = yb_out(STEPS - 1)
            for g in range(GROUPS):
                for n in range(O_UNITS):
                    if g * O_UNITS + n + AHEAD < GROUPS * O_UNITS:
                        split_hi(OUT0, g, O_UNITS, n + AHEAD)
                    if g == 0 and n == 0:
                        gate_sigmoid()
                    if g == 0 and n == 2:
                        turned_hi()
                    if g and n == 1:
                        h_squares(g - 1, h_fin, GROUPS + g)
            h_squares(GROUPS - 1, h_fin, 2 * GROUPS)
            act.wait_ge(h_sum, 2)
            mean(TILES, h_sums[:, :], D_MODEL, mean_done)

        @block.vector
        def _(dve):
            def split_lo(base, i, per, n, cols=UNIT):
                s = slot(base, n)
                dve.wait_ge(hi_ready, i * per + (base + n + 1))
                dve.tensor_tensor(w_lo[:, s, 0:cols], w_raw[:, s, 0:cols], w_hi[:, s, 0:cols].bitcast(fp32),
                                  ALU.subtract).then_inc(lo_ready, 1)

            dve.wait_ge(const_ready, 3 * 16)
            dve.tensor_tensor(lb_tmp[:, 2, :], lb_in[:, 0:HG_HEADS], lb_in[:, HG_HEADS:], ALU.max).then_inc(lb_step, 1)
            dve.wait_ge(lb_step, 1)
            for layer in range(2):
                dve.tensor_tensor(lb_tmp[:, layer, :], lb_in[:, layer * HG_HEADS:(layer + 1) * HG_HEADS],
                                  lb_tmp[:, 2, :], ALU.subtract).then_inc(lb_step, 1)
            dve.wait_ge(norm_ready, 1)
            for t in range(TILES):
                dve.tensor_scalar(h[:, t, :], h[:, t, :], rnorm[:, t:t + 1], None, ALU.mult).then_inc(scaled, 1)
            for n in range(AHEAD):
                split_lo(A0, 0, A_UNITS, n)
            dve.wait_ge(lb_exp, 1)
            dve.tensor_tensor(lb_tmp[:, 2, :], lb_tmp[:, 0, :], lb_tmp[:, 1, :], ALU.add).then_inc(lb_step, 1)
            dve.wait_ge(lb_step, 4)
            dve.reciprocal(lb_tmp[:, 2, :], lb_tmp[:, 2, :]).then_inc(lb_step, 1)
            dve.wait_ge(lb_step, 5)
            dve.tensor_tensor(lb[:, :], lb_tmp[:, 0, :], lb_tmp[:, 2, :], ALU.mult).then_inc(lb_step, 1)
            dve.wait_ge(lb_step, 6)
            dve.tensor_scalar(one_lb[:, :], lb[:, :], -1.0, 1.0, ALU.mult, ALU.add).then_inc(lb_step, 1)
            for kt in range(KT):
                dve.wait_ge(n_hi, kt // 2 * 2 + 2)
                lo_part(dve, nT_lo[:, kt, :], ps[:, kt * TOKENS:(kt + 1) * TOKENS], g_hg[:, kt:kt + 1],
                        nT_hi[:, kt, :]).then_inc(n_lo, 1)

            def y_out(jp):
                def gated():
                    dve.wait_ge(gsig_ready, jp + 1)
                    flat = gate[:, :, :].rearrange("p t n -> p (t n)")
                    dve.tensor_tensor(flat, bank(4, 2), flat, ALU.mult).then_inc(silu_ready, 1)
                    dve.wait_ge(silu_ready, jp + 1)
                    dve.wait_ge(o_norm, jp + 1)
                    for t in range(TILES):
                        for e in range(2):
                            cols = gate[:, t, e * HG_VAL:(e + 1) * HG_VAL]
                            i = 2 * t + e
                            last = dve.scalar_tensor_tensor(
                                out=cols, in0=ps[:, 6 * 512 + i * HG_VAL:6 * 512 + (i + 1) * HG_VAL],
                                scalar=rnorm[:, i:i + 1], in1=cols, op0=ALU.mult, op1=ALU.mult)
                    last.then_inc(y_ready, 1)

                def turned_lo():
                    dve.wait_ge(y_hi, jp + 1)
                    for c in range(4):
                        last = lo_part(dve, aT_lo[:, ds(jp * 4 + c, 1), :], ps[:, 4 * 512 + c * 256:4 * 512 + (c + 1) * 256],
                                       g_o[:, c % 2:c % 2 + 1], aT_hi[:, ds(jp * 4 + c, 1), :])
                    last.then_inc(y_lo, 1)
                return gated, turned_lo

            def a_step(j, first):
                def decayed(level):
                    dve.wait_ge(decay_ready, j * LEVELS + (level + 1))
                    if level == 0:
                        dve.wait_ge(k_ready, j + 1)
                    first_half, second_half = halves(qk_dec[:, level, :], level)
                    dve.tensor_tensor(first_half, first_half, halves(kT[:, :], level)[0], ALU.mult)
                    dve.tensor_tensor(second_half, second_half, halves(qT[:, :], level)[1], ALU.mult).then_inc(qk_ready, 1)

                def take_scores(blk):
                    head, tile = divmod(blk, 2)
                    base = (6, 0)[tile] * 512
                    dve.wait_ge(score_done, j * 4 + (blk + 1))
                    whole = att[:, blk, :]
                    dve.tensor_tensor(whole, ps[:, base:base + MASK_COLS], mask_sb[:, :], ALU.mult).then_inc(att_step, 1)
                    for level in range(LEVELS - 1):
                        dve.wait_ge(att_step, j * (4 * (LEVELS - 1)) + (blk * (LEVELS - 1) + level + 1))
                        at = 128 + level * LEVEL_COLS
                        into = halves(whole[:, 0:128], level)[1]
                        new = whole[:, at:at + LEVEL_COLS].rearrange("p (b m) -> p b m", m=1 << level)
                        dve.tensor_tensor(into, into, new, ALU.add).then_inc(
                            att_step if level < LEVELS - 2 else att_ready, 1)
                    if tile:
                        dve.tensor_copy(cross[:, head, :], ps[:, base + 640:base + 768]).then_inc(cross_ready, 1)

                if not first:
                    gated, turned_lo = y_out(j - 1)
                for n in range(A_UNITS):
                    split_lo(A0, j, A_UNITS, n + AHEAD)
                    if n == 0 and not first:
                        gated()
                    if n == 2 and not first:
                        turned_lo()
                    if n == 7:
                        dve.wait_ge(unit_done, j * A_UNITS + 8)
                        dve.tensor_copy(qT[:, :], bank(0)).then_inc(q_ready, 1)
                        dve.wait_ge(sig_ready, j * 2 + 1)
                        dve.tensor_scalar(logf[:, :], logf[:, :], SMALLEST_F, None, ALU.max).then_inc(sig_clamped, 1)
                        dve.wait_ge(sig_ready, j * 2 + 2)
                        if first:
                            dve.wait_ge(lb_step, 7)
                        for e in range(2):
                            head = kT[:, e * TOKENS:(e + 1) * TOKENS]
                            last = dve.tensor_scalar(head, head, one_lb[:, ds(j * 2 + e, 1)], None, ALU.mult)
                        last.then_inc(k_ready, 1)
                    if 8 <= n < 8 + LEVELS:
                        decayed(n - 8)
                    if n in SCORES_AT:
                        take_scores(SCORES_AT.index(n))

            a_step(0, True)
            with dve.Fori(1, STEPS) as j:
                a_step(j, False)

            def residual(g, stream, loaded, banks, done):
                dve.wait_ge(loaded, 16)
                dve.wait_ge(unit_done, done)
                cols = stream[:, :, g * 512:(g + 1) * 512]
                dve.tensor_tensor(cols, bank(banks, 2).rearrange("p (t n) -> p t n", t=TILES), cols,
                                  ALU.add).then_inc(h_ready, 1)

            def stream_sum(squares, done):
                dve.wait_ge(h_sq, squares)
                dve.tensor_reduce(h_sums[:, :], sums[:, 8:16].rearrange("p (t g) -> p t g", t=TILES), AX.X,
                                  ALU.add).then_inc(h_sum, 1)

            gated, turned_lo = y_out(STEPS - 1)
            for g in range(GROUPS):
                for n in range(O_UNITS):
                    split_lo(WO0, g, O_UNITS, n + AHEAD)
                    if g == 0 and n == 0:
                        gated()
                    if g == 0 and n == 2:
                        turned_lo()
                    if g and n == 0:
                        residual(g - 1, h, x_again[g - 1], 2 * ((g - 1) % 2), WO0 + g * O_UNITS)
            residual(GROUPS - 1, h, x_again[GROUPS - 1], 2 * ((GROUPS - 1) % 2), KV0)
            stream_sum(TILES * GROUPS, 1)
            dve.wait_ge(norm_ready, 2)
            dve.wait_ge(h_stored, 16)
            for t in range(TILES):
                dve.tensor_scalar(h[:, t, :], h[:, t, :], rnorm[:, t:t + 1], None, ALU.mult).then_inc(scaled, 1)
            for batch, which in STREAM_ORDER:
                hi, lo, gain = ((aT_hi, aT_lo, g_kvin), (nT_hi, nT_lo, g_mla))[which]
                for e in range(2):
                    kt = 2 * batch + e
                    dve.wait_ge(n_hi, KT + 4 * batch + 4)
                    lo_part(dve, lo[:, kt, :], ps[:, kt * TOKENS:(kt + 1) * TOKENS], gain[:, kt:kt + 1],
                            hi[:, kt, :]).then_inc(n_lo, 1)

            for n in range(C_UNITS + CQ_UNITS):
                split_lo(KV0, 0, 0, n + AHEAD)
                if n == 7:
                    dve.wait_ge(c_norm, 1)
                    for t in range(TILES):
                        dve.tensor_scalar(c_nat[:, t, :], bank(t), rnorm[:, t:t + 1], None, ALU.mult).then_inc(c_scaled, 1)
                    dve.memset(k_even[:, :], 0.0).then_inc(kr_step, 1)
                    dve.memset(k_odd[:, :], 0.0).then_inc(kr_step, 1)
                if n == 11:
                    for kt in range(KT_C):
                        dve.wait_ge(c_hi, kt // 2 * 2 + 2)
                        lo_part(dve, cT_lo[:, kt, :], ps[:, kt * TOKENS:(kt + 1) * TOKENS], g_c[:, kt:kt + 1],
                                cT_hi[:, kt, :]).then_inc(c_lo, 1)
                    dve.wait_ge(kr_rot, 1)
                    dve.tensor_tensor(rot_sb[:, 1, :], bank(2)[:, 256:512], sin_sb, ALU.mult).then_inc(kr_step, 1)
                    dve.tensor_tensor(rot_sb[:, 0, :], rot_sb[:, 0, :], cos_sb, ALU.mult).then_inc(kr_step, 1)
                    dve.wait_ge(kr_step, 4)
                    dve.tensor_tensor(k_even[0:64, :], rot_sb[0:64, 0, :], rot_sb[0:64, 1, :], ALU.add).then_inc(kr_step, 1)
                    dve.tensor_tensor(k_odd[64:128, :], rot_sb[64:128, 0, :], rot_sb[64:128, 1, :], ALU.add).then_inc(kr_step, 1)
            dve.wait_ge(c_sq, 6)
            dve.tensor_reduce(sums[:, 6:8], sums[:, 2:6].rearrange("p (t g) -> p t g", t=TILES), AX.X,
                              ALU.add).then_inc(cq_sum, 1)
            dve.wait_ge(c_norm, 2)
            for t in range(TILES):
                dve.tensor_scalar(cq_nat[t][:, 0:512], bank(3 + t), rnorm[:, t:t + 1], None, ALU.mult).then_inc(c_scaled, 1)
                dve.tensor_scalar(cq_nat[t][:, 512:Q_LORA], bank(5 + t)[:, 0:256], rnorm[:, t:t + 1], None,
                                  ALU.mult).then_inc(c_scaled, 1)

            def yb_out(jp):
                def gated():
                    dve.wait_ge(gbsig_ready, jp + 1)
                    flat = gate_b[:, :, :].rearrange("p t n -> p (t n)")
                    dve.tensor_tensor(flat, bank(2, 2), flat, ALU.mult).then_inc(bsilu_ready, 1)
                    dve.wait_ge(bsilu_ready, jp + 1)
                    dve.wait_ge(inv_ready, jp + 1)
                    dve.wait_ge(pv_done, jp * 2 + 2)
                    for pair in range(2):
                        for i in range(2):
                            for t in range(TILES):
                                m = 2 * pair + i
                                cols = gate_b[:, t, m * V_DIM:(m + 1) * V_DIM]
                                at = (4 + pair) * 512 + (2 * i + t) * V_DIM
                                last = dve.scalar_tensor_tensor(
                                    out=cols, in0=ps[:, at:at + V_DIM], scalar=row_sum[:, pair, 2 * i + t:2 * i + t + 1],
                                    in1=cols, op0=ALU.mult, op1=ALU.mult)
                    last.then_inc(yb_ready, 1)

                def turned_lo():
                    dve.wait_ge(yb_hi, jp + 1)
                    dve.tensor_tensor(aT_lo[:, ds(jp * 4, 4), :].rearrange("p c t -> p (c t)"), bank(6, 2),
                                      aT_hi[:, ds(jp * 4, 4), :].rearrange("p c t -> p (c t)").bitcast(fp32),
                                      ALU.subtract).then_inc(yb_lo, 1)
                return gated, turned_lo

            def b_step(j, first):
                def row_maxima(pair):
                    dve.wait_ge(s_done, j * 2 + (pair + 1))
                    if pair:
                        dve.wait_ge(pturn_done, j * 2 + 1)
                    dve.tensor_tensor(prob[:, :, :], bank(4 + 2 * pair, 2).rearrange("p (i n) -> p i n", i=2)[:, :, 0:384],
                                      causal[:, None, :].to_broadcast([128, 2, 384]), ALU.add).then_inc(score_masked, 1)
                    dve.wait_ge(score_masked, j * 2 + (pair + 1))
                    for t in range(TILES):
                        last = dve.tensor_reduce(row_max[:, pair, t, :], prob[:, :, 128 * t:128 + 256 * t], AX.X, ALU.max)
                    last.then_inc(max_ready, 1)
                    dve.wait_ge(max_ready, j * 2 + (pair + 1))
                    dve.tensor_scalar(row_max[:, pair, :, :], row_max[:, pair, :, :], -ATT_SCALE, None,
                                      ALU.mult).then_inc(neg_ready, 1)

                if not first:
                    gated, turned_lo = yb_out(j - 1)
                for n in range(B_UNITS):
                    split_lo(B0, j, B_UNITS, n + AHEAD, b_cols(n + AHEAD))
                    if n == 0 and not first:
                        gated()
                    if n == 1 and first:
                        for kt in range(KT_Q):
                            dve.wait_ge(c_hi, KT_C + KT_Q)
                            lo_part(dve, cqT_lo[:, kt, :], ps[:, 5 * 512 + kt * TOKENS:5 * 512 + (kt + 1) * TOKENS],
                                    g_q[:, kt:kt + 1], cqT_hi[:, kt, :]).then_inc(c_lo, 1)
                    if n == 2 and not first:
                        turned_lo()
                    if n == 3:
                        dve.wait_ge(unit_done, j * B_UNITS + (B0 + 4))
                        dve.tensor_copy(v_sb[:, :, :].rearrange("p t n -> p (t n)"), bank(2, 2)).then_inc(v_ready, 1)
                    if n == 7:
                        dve.wait_ge(unit_done, j * B_UNITS + (B0 + 8))
                        dve.tensor_copy(q_nope[:, :, :].rearrange("p h t -> p (h t)"), bank(4, 2)).then_inc(qn_ready, 1)
                    if n == 8:
                        dve.wait_ge(qr_rot, j + 1)
                        dve.tensor_tensor(rot_sb[:, :, :], bank(1).rearrange("p (i t) -> p i t", i=2),
                                          sin_sb[:, None, :].to_broadcast([128, 2, TOKENS]), ALU.mult).then_inc(qr_step, 1)
                        dve.tensor_tensor(q_rope[:, :, :], q_rope[:, :, :],
                                          cos_sb[:, None, :].to_broadcast([128, 2, TOKENS]), ALU.mult).then_inc(qr_step, 1)
                        dve.wait_ge(qr_step, j * 3 + 2)
                        dve.tensor_tensor(q_rope[:, :, :], q_rope[:, :, :], rot_sb[:, :, :], ALU.add).then_inc(qr_step, 1)
                    if n in (10, 12):
                        row_maxima((10, 12).index(n))
                    if n == 15:
                        dve.wait_ge(p_ready, j * 2 + 2)
                        dve.reciprocal(row_sum[:, :, :], row_sum[:, :, :]).then_inc(inv_ready, 1)

            b_step(0, True)
            with dve.Fori(1, STEPS) as j:
                b_step(j, False)

            gated, turned_lo = yb_out(STEPS - 1)
            for g in range(GROUPS):
                for n in range(O_UNITS):
                    if g * O_UNITS + n + AHEAD < GROUPS * O_UNITS:
                        split_lo(OUT0, g, O_UNITS, n + AHEAD)
                    if g == 0 and n == 0:
                        gated()
                    if g == 0 and n == 2:
                        turned_lo()
                    if g and n == 0:
                        residual(g - 1, h_fin, h_back[g - 1], 2 * ((g - 1) % 2), OUT0 + g * O_UNITS)
            residual(GROUPS - 1, h_fin, h_back[GROUPS - 1], 2 * ((GROUPS - 1) % 2), UNITS)
            stream_sum(2 * TILES * GROUPS, 2)
            dve.wait_ge(fin_norm, 1)
            dve.wait_ge(gain_back, 16)
            for part in range(4):
                t, half = divmod(part, 2)
                cols = h_fin[:, t, half * 1024:(half + 1) * 1024]
                dve.scalar_tensor_tensor(out=cols, in0=cols, scalar=rnorm[:, t:t + 1],
                                         in1=final_sb[:, half * 1024:(half + 1) * 1024],
                                         op0=ALU.mult, op1=ALU.mult).then_inc(fin_scaled, 1)

        @block.tensor
        def _(pe):
            def natural(base, i, per, n, xT, kts, cols, banks, first, last):
                s = slot(base, n)
                pe.wait_ge(lo_ready, i * per + (base + n + 1))
                for e, kt in enumerate(kts):
                    w = slice(e * cols, (e + 1) * cols)
                    for t in range(TILES):
                        acc = bank(banks[t])[:, 0:cols]
                        tile = slice(t * 128, (t + 1) * 128)
                        pe.matmul(acc, xT[0][:, kt, tile], w_hi[:, s, w], start=first and e == 0, stop=False)
                        pe.matmul(acc, xT[0][:, kt, tile], w_lo[:, s, w], start=False, stop=False)
                        mm = pe.matmul(acc, xT[1][:, kt, tile], w_hi[:, s, w], start=False,
                                       stop=last and e == len(kts) - 1)
                return mm.then_inc(unit_done, 1)

            def turned_out(base, i, per, n, xT, parts):
                s = slot(base, n)
                pe.wait_ge(lo_ready, i * per + (base + n + 1))
                for place, kt, at, first, last in parts:
                    w = slice(place * 128, (place + 1) * 128)
                    acc = ps[:, at:at + TOKENS]
                    pe.matmul(acc, w_hi[:, s, w], xT[0][:, kt, :], start=first, stop=False, skip_group_check=True)
                    pe.matmul(acc, w_hi[:, s, w], xT[1][:, kt, :], start=False, stop=False, skip_group_check=True)
                    mm = pe.matmul(acc, w_lo[:, s, w], xT[0][:, kt, :], start=False, stop=last, skip_group_check=True)
                return mm.then_inc(unit_done, 1)

            nT = (nT_hi, nT_lo)
            aT = (aT_hi, aT_lo)
            cT = (cT_hi, cT_lo)
            cqT = (cqT_hi, cqT_lo)

            def turn_stream(wait):
                pe.wait_ge(scaled, wait)
                for kt in range(KT):
                    for t in range(TILES):
                        mm = pe.transpose(ps[:, kt * TOKENS + t * 128:kt * TOKENS + (t + 1) * 128],
                                          h[:, t, kt * 128:(kt + 1) * 128], ident)
                    if kt % 2:
                        mm.then_inc(turned, 1)

            pe.wait_ge(const_ready, 3 * 16)
            turn_stream(TILES)

            def turn_y(src, first_bank, done):
                for c in range(4):
                    for t in range(TILES):
                        at = first_bank * 512 + c * TOKENS + t * 128
                        mm = pe.transpose(ps[:, at:at + 128], src[:, t, c * 128:(c + 1) * 128], ident)
                mm.then_inc(done, 1)

            def a_step(j, first):
                def scores(blk):
                    head, tile = divmod(blk, 2)
                    base = (6, 0)[tile] * 512
                    if blk == 0:
                        pe.wait_ge(qk_ready, j * LEVELS + (LEVELS - 1))
                    if blk == 1:
                        pe.wait_ge(qk_ready, j * LEVELS + LEVELS)
                    if blk >= 2:
                        pe.wait_ge(att_ready, j * 4 + (blk - 1))
                        if tile:
                            pe.wait_ge(cross_ready, j * 2 + 1)
                    own = slice(head * TOKENS + tile * 128, head * TOKENS + tile * 128 + 128)
                    for level in range(LEVELS - 1):
                        at = base + 128 + level * LEVEL_COLS
                        both = qk_dec[:, level, own]
                        out_cols = ps[:, at:at + LEVEL_COLS].rearrange("p (b m) -> p b m", m=1 << level)
                        pe.matmul(out_cols, both, halves(both, level)[1], start=True, stop=True)
                    mm = pe.matmul(ps[:, base:base + 128], kT[:, own], qT[:, own], start=True, stop=True)
                    if tile:
                        tile0, tile1 = halves(qk_dec[:, LEVELS - 1, head * TOKENS:(head + 1) * TOKENS], LEVELS - 1)
                        mm = pe.matmul(ps[:, base + 640:base + 768], tile0.rearrange("p b m -> p (b m)"),
                                       tile1.rearrange("p b m -> p (b m)"), start=True, stop=True)
                    mm.then_inc(score_done, 1)

                for n in range(A_UNITS):
                    u = n % 8
                    kts = (2 * u, 2 * u + 1)
                    if n < 8:
                        if first:
                            pe.wait_ge(n_lo, max(2 * u + 2, 4))
                        elif n == 0:
                            pe.wait_ge(o_sq, j)
                        parts = [(4 * e + m, kts[e], m * TOKENS, u == 0 and e == 0 and m % 2 == 0, u == 7 and e == 1)
                                 for e in range(2) for m in range(4)]
                        turned_out(A0, j, A_UNITS, n, nT, parts)
                    elif n < 16:
                        if n == 8 and not first:
                            pe.wait_ge(val_ready, j)
                        natural(A0, j, A_UNITS, n, nT, kts, 512, (2, 3), u == 0, u == 7)
                    else:
                        if n == 16 and not first:
                            pe.wait_ge(y_lo, j)
                        natural(A0, j, A_UNITS, n, nT, kts, 512, (4, 5), u == 0, u == 7)
                    if n == 2 and not first:
                        pe.wait_ge(y_ready, j)
                        turn_y(gate, 4, yturn_done)
                    if n in SCORES_AT:
                        scores(SCORES_AT.index(n))
                    if n == OUT_AT:
                        pe.wait_ge(att_ready, j * 4 + 4)
                        pe.wait_ge(cross_ready, j * 2 + 2)
                        pe.wait_ge(val_ready, j + 1)
                        for e in range(2):
                            v = slice(e * HG_VAL, (e + 1) * HG_VAL)
                            pe.matmul(bank(6)[:, v], att[:, 2 * e, 0:128], val[:, 0, v], start=True, stop=True)
                            pe.matmul(bank(7)[:, v], cross[:, e, :], val[:, 0, v], start=True, stop=False)
                            mm = pe.matmul(bank(7)[:, v], att[:, 2 * e + 1, 0:128], val[:, 1, v], start=False, stop=True)
                        mm.then_inc(o_done, 1)

            a_step(0, True)
            with pe.Fori(1, STEPS) as j:
                a_step(j, False)

            def project(base, h_before, y_count, extra, turn):
                for g in range(GROUPS):
                    for n in range(O_UNITS):
                        if g == 0 and n == 0:
                            extra(0)
                        if g == 1 and n == 0:
                            extra(1)
                        if g >= 2 and n == 0:
                            pe.wait_ge(h_ready, h_before + g - 1)
                        if g == 0 and n == O_UNITS - 2:
                            pe.wait_ge(y_count, STEPS)
                        b = 2 * (g % 2)
                        natural(base, g, O_UNITS, n, aT, (2 * n, 2 * n + 1), 512, (b, b + 1), n == 0, n == O_UNITS - 1)
                        if g == 0 and n == 2:
                            turn()

            def wo_banks(g):
                if g == 0:
                    pe.wait_ge(o_sq, STEPS)
                else:
                    pe.wait_ge(val_ready, STEPS)

            def wo_turn():
                pe.wait_ge(y_ready, STEPS)
                turn_y(gate, 4, yturn_done)

            project(WO0, 0, y_lo, wo_banks, wo_turn)

            turn_stream(2 * TILES)
            def rotated(dst, src):
                return pe.matmul(dst, rotate, src, start=True, stop=True)

            for n in range(C_UNITS + CQ_UNITS):
                if n < 8:
                    pe.wait_ge(n_lo, KT + 4 * max(2, n + 1))
                    natural(KV0, 0, 0, n, aT, (2 * n, 2 * n + 1), 512, (0, 1), n == 0, n == 7)
                elif n < C_UNITS:
                    if n == 8:
                        pe.wait_ge(n_lo, 3 * KT)
                    turned_out(KV0, 0, 0, n, aT, [(e, 8 * (n - 8) + e, 2 * 512, n == 8 and e == 0, n == 9 and e == 7)
                                                  for e in range(8)])
                elif n < C_UNITS + 8:
                    u = n - C_UNITS
                    natural(KV0, 0, 0, n, nT, (2 * u, 2 * u + 1), 512, (3, 4), u == 0, u == 7)
                else:
                    u = n - C_UNITS - 8
                    if u == 0:
                        pe.wait_ge(c_sq, 2)
                    natural(KV0, 0, 0, n, nT, range(4 * u, 4 * u + 4), 256, (5, 6), u == 0, u == 3)
                if n == 11:
                    pe.wait_ge(c_scaled, 2)
                    for kt in range(KT_C):
                        for t in range(TILES):
                            at = kt * TOKENS + t * 128
                            mm = pe.transpose(ps[:, at:at + 128], c_nat[:, t, kt * 128:(kt + 1) * 128], ident)
                    mm.then_inc(c_turned, 1)
                    pe.wait_ge(kr_raw, 1)
                    rotated(bank(2)[:, 256:512], rot_sb[:, 0, :]).then_inc(kr_rot, 1)

            def b_step(j, first):
                def head_scores(pair):
                    for i in range(2):
                        m = 2 * pair + i
                        key = (k_even, k_odd)[i]
                        for t in range(TILES):
                            q = slice(t * 128, (t + 1) * 128)
                            keys = slice(0, (t + 1) * 128)
                            at = (4 + 2 * pair + i) * 512 + 128 * t
                            acc = ps[:, at:at + (t + 1) * 128]
                            pe.matmul(acc, q_nope[:, m, q], k_nope[:, m, keys], start=True, stop=False)
                            mm = pe.matmul(acc, q_rope[:, pair, q], key[:, keys], start=False, stop=True)
                    mm.then_inc(s_done, 1)

                def turn_probs(pair):
                    pe.wait_ge(p_ready, j * 2 + (pair + 1))
                    for i in range(2):
                        for c in range(3):
                            at = (4 + 2 * pair + i) * 512 + c * 128
                            mm = pe.transpose(ps[:, at:at + 128], prob[:, i, c * 128:(c + 1) * 128], ident)
                    mm.then_inc(pturn_done, 1)

                def weigh_values(pair):
                    pe.wait_ge(pT_ready, j * 2 + (pair + 1))
                    for i in range(2):
                        v = slice((2 * pair + i) * V_DIM, (2 * pair + i + 1) * V_DIM)
                        at = (4 + pair) * 512 + i * 256
                        pe.matmul(ps[:, at:at + 128], probT[:, i, 0:128], v_sb[:, 0, v], start=True, stop=True)
                        pe.matmul(ps[:, at + 128:at + 256], probT[:, i, 128:256], v_sb[:, 0, v], start=True, stop=False)
                        mm = pe.matmul(ps[:, at + 128:at + 256], probT[:, i, 256:384], v_sb[:, 1, v], start=False, stop=True)
                    mm.then_inc(pv_done, 1)

                for n in range(B_UNITS):
                    if n < 2:
                        if first and n == 0:
                            pe.wait_ge(c_lo, KT_C)
                        parts = [(4 * e + m, 2 * n + e, m * TOKENS, n == 0 and e == 0 and m % 2 == 0, n == 1 and e == 1)
                                 for e in range(2) for m in range(4)]
                        turned_out(B0, j, B_UNITS, n, cT, parts)
                    elif n < 4:
                        if n == 2:
                            if first:
                                pe.wait_ge(c_scaled, 6)
                            else:
                                pe.wait_ge(bsilu_ready, j)
                        natural(B0, j, B_UNITS, n, cT, (2 * (n - 2), 2 * (n - 2) + 1), 512, (2, 3), n == 2, n == 3)
                    elif n < 8:
                        if n == 4:
                            pe.wait_ge(kn_ready, j + 1)
                            if first:
                                pe.wait_ge(c_lo, KT_C + KT_Q)
                            else:
                                pe.wait_ge(yb_ready, j)
                        parts = []
                        for place in range(9):
                            kt, m = divmod((n - 4) * 9 + place, 6)
                            at = (4 * 512 + m * TOKENS) if m < 4 else (m - 4) * TOKENS
                            parts.append((place, kt, at, kt == 0 and m % 2 == 0, kt == KT_Q - 1))
                        turned_out(B0, j, B_UNITS, n, cqT, parts)
                    else:
                        if n == 8:
                            pe.wait_ge(v_ready, j + 1)
                        u = n - 8
                        natural(B0, j, B_UNITS, n, nT, (2 * u, 2 * u + 1), 512, (2, 3), u == 0, u == 7)
                    if n == 0 and first:
                        pe.wait_ge(c_scaled, 6)
                        for kt in range(KT_Q):
                            for t in range(TILES):
                                at = 5 * 512 + kt * TOKENS + t * 128
                                mm = pe.transpose(ps[:, at:at + 128], cq_nat[t][:, kt * 128:(kt + 1) * 128], ident)
                        mm.then_inc(c_turned, 1)
                    if n == 2 and not first:
                        pe.wait_ge(yb_ready, j)
                        turn_y(gate_b, 6, ybturn_done)
                    if n == 8:
                        pe.wait_ge(qr_raw, j + 1)
                        rotated(bank(1), q_rope[:, :, :].rearrange("p i t -> p (i t)")).then_inc(qr_rot, 1)
                    if n == 10:
                        pe.wait_ge(qn_ready, j + 1)
                        pe.wait_ge(qr_step, j * 3 + 3)
                        if first:
                            pe.wait_ge(kr_step, 6)
                        head_scores(0)
                    if n == 12:
                        turn_probs(0)
                        if not first:
                            pe.wait_ge(yb_lo, j)
                        head_scores(1)
                    if n == 13:
                        weigh_values(0)
                    if n == 14:
                        turn_probs(1)
                    if n == 15:
                        weigh_values(1)

            b_step(0, True)
            with pe.Fori(1, STEPS) as j:
                b_step(j, False)

            def out_banks(g):
                if g == 1:
                    pe.wait_ge(bsilu_ready, STEPS)

            def out_turn():
                pe.wait_ge(yb_ready, STEPS)
                turn_y(gate_b, 6, ybturn_done)

            project(OUT0, GROUPS, yb_lo, out_banks, out_turn)


def score_masks():
    import numpy as np
    s, t = np.arange(128)[:, None], np.arange(128)[None, :]
    masks = [s == t]
    for level in range(LEVELS - 1):
        own = t[:, (t[0] >> level) & 1 == 1]
        masks.append((s < own) & ((s ^ own) >> level == 1))
    return np.ascontiguousarray(np.concatenate(masks, axis=1).astype(np.float32))


def constants():
    import numpy as np
    rot = np.zeros((128, 128), np.float32)
    for b in (0, 64):
        for i in range(32):
            rot[b + 32 + i, b + i] = -1.0
            rot[b + i, b + 32 + i] = 1.0
    pos = np.arange(TOKENS, dtype=np.float32)
    freq = (np.float32(10000.0) ** (-np.arange(0, ROPE, 2, dtype=np.float32) / np.float32(ROPE))).astype(np.float32)
    ang = np.tile((pos[:, None] * freq[None, :]).astype(np.float32).T, (4, 1))
    q, k = np.arange(128)[:, None], np.arange(128)[None, :]
    own = np.where(k <= q, 0.0, MASKED)
    causal = np.concatenate([own, np.zeros((128, 128)), own], axis=1)
    parts = [np.eye(128), rot, np.cos(ang), np.sin(ang), causal]
    return np.ascontiguousarray(np.concatenate([p.astype(np.float32) for p in parts], axis=1))


def units(w, rows_per_unit, cols):
    import numpy as np
    k, n = w.shape
    a = w.reshape(k // (128 * rows_per_unit), rows_per_unit, 128, n // cols, cols)
    return np.ascontiguousarray(a.transpose(3, 0, 2, 1, 4)).reshape(n // cols, -1, 128, rows_per_unit * cols)


def by_column(v):
    return v.reshape(-1, 128).T


def kernel(x, norm_g, hg_w_in, hg_g_norm, hg_w_out, hg_lb, kv_in_norm_g, w_kv_down, kv_norm_g,
           w_kv_up, mla_w_in, mla_q_norm_g, mla_w_q_up, mla_w_out, final_norm_g):
    import numpy as np
    import concourse.bacc as bacc
    from concourse import mybir
    from concourse.bass_utils import run_bass_kernel_spmd

    a = {k: np.asarray(v) for k, v in dict(
        x=x, norm_g=norm_g, w_in=hg_w_in, g_norm=hg_g_norm, w_o=hg_w_out, lb=hg_lb, kvin=kv_in_norm_g,
        kv=w_kv_down, kvn=kv_norm_g, up=w_kv_up, mw=mla_w_in, qn=mla_q_norm_g, qup=mla_w_q_up,
        mo=mla_w_out, fin=final_norm_g).items()}
    w_in = a["w_in"][0]
    key = HG_HEADS * KEY_DIM
    q, f = (w_in[:, i * key:(i + 1) * key].reshape(D_MODEL, STEPS, 256) for i in range(2))
    qf = np.concatenate([q, f], axis=2).reshape(D_MODEL, STEPS * 512)
    parts = [qf, w_in[:, 2 * key:2 * key + D_INNER], w_in[:, 2 * key + D_INNER:]]
    w_a = np.stack([units(p, 2, 512) for p in parts], axis=1).reshape(STEPS * A_UNITS, 128, UNIT)
    w_o = units(a["w_o"][0], 2, 512).reshape(-1, 128, UNIT)
    rope2 = np.concatenate([a["kv"][:, KV_LORA:]] * 2, axis=1)
    w_kv = np.concatenate([units(a["kv"][:, :KV_LORA], 2, 512).reshape(-1, 128, UNIT),
                           units(rope2, 8, 128).reshape(-1, 128, UNIT)])
    mw = a["mw"][0]
    w_cq = np.concatenate([units(mw[:, :512], 2, 512).reshape(-1, 128, UNIT),
                           units(mw[:, 512:Q_LORA], 4, 256).reshape(-1, 128, UNIT)])
    up = a["up"].reshape(KV_LORA, STEPS, 4, 2, 128)
    w_bkv = np.stack([units(up[:, :, :, i].reshape(KV_LORA, -1), 2, 512) for i in range(2)],
                     axis=1).reshape(-1, 128, UNIT)
    qup = a["qup"][0].reshape(Q_LORA, STEPS, 4, NOPE + ROPE)
    qcols = np.concatenate([qup[..., :NOPE].reshape(Q_LORA, STEPS, -1), qup[..., NOPE:].reshape(Q_LORA, STEPS, -1)], axis=2)
    w_bq = qcols.reshape(KT_Q, 128, STEPS, 6, 128).transpose(2, 0, 3, 1, 4).reshape(STEPS, 4, 9, 128, 128)
    w_bq = np.ascontiguousarray(w_bq.transpose(0, 1, 3, 2, 4)).reshape(-1, 128, UNIT_Q)
    w_bg = units(mw[:, Q_LORA:], 2, 512).reshape(-1, 128, UNIT)
    w_out = units(a["mo"][0], 2, 512).reshape(-1, 128, UNIT)
    gains = np.ascontiguousarray(np.concatenate(
        [by_column(v) for v in (a["norm_g"][0], a["norm_g"][1], a["kvin"], a["kvn"], a["qn"][0], a["g_norm"][0],
                                a["lb"][0], a["lb"][1])], axis=1))
    arrays = dict(w_a=w_a, w_o=w_o, w_kv=w_kv, w_cq=w_cq, w_bkv=w_bkv, w_bq=w_bq, w_bg=w_bg, w_out=w_out,
                  x=a["x"][0], consts=constants(), masks=score_masks(), gains=gains,
                  final_g=a["fin"].reshape(1, -1))
    arrays = {k: np.ascontiguousarray(v) for k, v in arrays.items()}

    nc = bacc.Bacc("TRN2", target_bir_lowering=False, num_devices=1)
    args = {k: nc.dram_tensor(k, v.shape, mybir.dt.from_np(v.dtype), kind="ExternalInput").ap()
            for k, v in arrays.items()}
    args["out"] = nc.dram_tensor("out", (1, TOKENS, D_MODEL), mybir.dt.float32, kind="ExternalOutput").ap()
    args["h_store"] = nc.dram_tensor("h_store", (TOKENS, D_MODEL), mybir.dt.float32, kind="Internal").ap()
    build(nc, **args)
    r = run_bass_kernel_spmd(nc, [arrays], core_ids=[0])
    return r.results[0]["out"]
```

```python
import concourse.bass as bass
from concourse import mybir
from contextlib import ExitStack

TOKENS = 256
TILES = TOKENS // 128
D_MODEL = 2048
D_INNER = 4096
KEY_DIM = 128
HG_HEADS = 16
HG_VAL = 256
Q_LORA = 768
KV_LORA = 512
NOPE = 128
ROPE = 64
V_DIM = 128
EPS = 1e-6
ATT_SCALE = float(NOPE + ROPE) ** -0.5
MASKED = -1e30
SMALLEST_F = 1e-19

KT = D_MODEL // 128
KT_INNER = D_INNER // 128
KT_Q = Q_LORA // 128
KT_C = KV_LORA // 128
UNIT = 1024
UNIT_Q = 1152
RING = 4
AHEAD = 3

STEPS = 8
A_UNITS = 24
B_UNITS = 16
GROUPS = D_MODEL // 512
O_UNITS = KT_INNER // 2
KV_UNITS = 8
CQ_UNITS = 12
ROPE_UNITS = 2
C_UNITS = KV_UNITS + CQ_UNITS + ROPE_UNITS
A0 = 0
WO0 = A0 + STEPS * A_UNITS
KV0 = WO0 + GROUPS * O_UNITS
B0 = KV0 + C_UNITS
OUT0 = B0 + STEPS * B_UNITS
UNITS = OUT0 + GROUPS * O_UNITS

LEVELS = 8
LEVELS_AT = 9
SCORES_AT = (18, 19)
OUT_AT = 22
CONST_COLS = 128 + 128 + 256 + 256 + 384
LEVEL_COLS = (LEVELS - 1) * 128
MASK_COLS = LEVEL_COLS + 2 * 128
PAIR = 2 * TOKENS
GAIN_COLS = 3 * KT + KT_C + KT_Q + 2 + 2 * HG_HEADS


def build(nc, w_a, w_o, w_c, w_bkv, w_bq, w_bg, w_out, x, consts, masks, gains, final_g, out, h_store):
    fp32 = mybir.dt.float32
    f32r = mybir.dt.float32r
    ALU = mybir.AluOpType
    ACT = mybir.ActivationFunctionType
    AX = mybir.AxisListType
    ds = bass.ds

    ctx = ExitStack()
    with ctx:
        def sb(name, shape, dt=fp32, stack=ctx):
            return stack.enter_context(nc.sbuf_tensor(name, shape, dt))

        def sem(name):
            return ctx.enter_context(nc.semaphore(name))

        w_raw = sb("w_raw", [128, RING, UNIT_Q])
        w_hi = sb("w_hi", [128, RING, UNIT_Q], f32r)
        w_lo = sb("w_lo", [128, RING, UNIT_Q], f32r)
        aT_hi = sb("aT_hi", [128, KT_INNER, TOKENS], f32r)
        aT_lo = sb("aT_lo", [128, KT_INNER, TOKENS], f32r)
        nT_hi = sb("nT_hi", [128, KT, TOKENS], f32r)
        nT_lo = sb("nT_lo", [128, KT, TOKENS], f32r)
        const_sb = sb("const_sb", [128, CONST_COLS])
        gain_sb = sb("gain_sb", [128, GAIN_COLS])
        ident = const_sb[:, 0:128]
        rotate = const_sb[:, 128:256]
        cos_sb = const_sb[:, 256:512]
        sin_sb = const_sb[:, 512:768]
        causal = const_sb[:, 768:1152]
        g_hg = gain_sb[:, 0:KT]
        g_mla = gain_sb[:, KT:2 * KT]
        g_kvin = gain_sb[:, 2 * KT:3 * KT]
        g_c = gain_sb[:, 3 * KT:3 * KT + KT_C]
        g_q = gain_sb[:, 3 * KT + KT_C:3 * KT + KT_C + KT_Q]
        at = 3 * KT + KT_C + KT_Q
        g_o = gain_sb[:, at:at + 2]
        lb_in = gain_sb[:, at + 2:at + 2 + 2 * HG_HEADS]
        sums = sb("sums", [128, 16])
        rnorm = sb("rnorm", [128, 8])
        ms = sb("ms", [128, 8])
        r_x = sb("r_x", [128, TILES])
        r_h = sb("r_h", [128, TILES])
        r_h2 = sb("r_h2", [128, 3, TILES])
        ones = sb("ones", [128, 128])
        diag = sb("diag", [128, TOKENS])
        row_factor = sb("row_factor", [128, TOKENS])
        minus_half = sb("minus_half", [128, 8])
        h_sums = sb("h_sums", [128, TILES])

        a_mem = ExitStack()
        h = sb("h", [128, TILES, D_MODEL], stack=a_mem)
        h_flat = h[:, :, :].rearrange("p t n -> p (t n)")
        qk_dec = h_flat.rearrange("p (l e r t) -> p l e r t", l=LEVELS, e=2, r=2)
        mask_sb = sb("mask_sb", [128, MASK_COLS], stack=a_mem)
        lb_tmp = sb("lb_tmp", [128, 3, HG_HEADS], stack=a_mem)
        lb = sb("lb", [128, HG_HEADS], stack=a_mem)
        one_lb = sb("one_lb", [128, HG_HEADS], stack=a_mem)
        kq = sb("kq", [128, 2 * PAIR], stack=a_mem)
        ranges = sb("ranges", [128, 2 * PAIR], stack=a_mem)
        levels_mem = ExitStack()
        level_scores = sb("level_scores", [128, LEVEL_COLS], stack=levels_mem)
        levels_mem.close()
        att_lo = sb("att_lo", [128, 2, TILES, 128], f32r, stack=a_mem)
        cross_lo = sb("cross_lo", [128, 2, 128], f32r, stack=a_mem)
        sb("levels_rest", [128, LEVEL_COLS - (2 * TILES + 2) * 128], stack=a_mem)
        both_tiles = sb("both_tiles", [128, 2, 128], stack=a_mem)
        att = ranges[:, 0:512].rearrange("p (e t n) -> p e t n", e=2, t=TILES)
        cross_own = sb("cross_own", [128, 2 * 128 + 2 * TILES], stack=a_mem)
        cross_whole = cross_own[:, 0:256].rearrange("p (e n) -> p e n", e=2)
        own = cross_own[:, 256:256 + 2 * TILES]
        att_hi = sb("att_hi", [128, 2, TILES, 128], f32r, stack=a_mem)
        cross_hi = sb("cross_hi", [128, 2, 128], f32r, stack=a_mem)
        val_hi = sb("val_hi", [128, TILES, 512], f32r, stack=a_mem)
        val_lo = sb("val_lo", [128, TILES, 512], f32r, stack=a_mem)
        gate = sb("gate", [128, TILES, 512], stack=a_mem)
        a_mem.close()

        b_mem = ExitStack()
        cT_hi = sb("cT_hi", [128, KT_C, TOKENS], f32r, stack=b_mem)
        cT_lo = sb("cT_lo", [128, KT_C, TOKENS], f32r, stack=b_mem)
        cqT_hi = sb("cqT_hi", [128, KT_Q, TOKENS], f32r, stack=b_mem)
        cqT_lo = sb("cqT_lo", [128, KT_Q, TOKENS], f32r, stack=b_mem)
        k_nope = sb("k_nope", [128, 4, TOKENS], stack=b_mem)
        q_nope = sb("q_nope", [128, 4, TOKENS], stack=b_mem)
        q_rope = sb("q_rope", [128, 2, TOKENS], stack=b_mem)
        rot_sb = sb("rot_sb", [128, 2, TOKENS], stack=b_mem)
        k_even = sb("k_even", [128, TOKENS], stack=b_mem)
        k_odd = sb("k_odd", [128, TOKENS], stack=b_mem)
        v_sb = sb("v_sb", [128, TILES, 512], stack=b_mem)
        prob = sb("prob", [128, 2, 384], stack=b_mem)
        probT = sb("probT", [128, 2, 384], stack=b_mem)
        gate_b = sb("gate_b", [128, TILES, 512], stack=b_mem)
        row_max = sb("row_max", [128, 2, TILES, 2], stack=b_mem)
        row_sum = sb("row_sum", [128, 2, 4], stack=b_mem)
        b_mem.close()
        q_flat = k_nope[:, :, :].rearrange("p h t -> p (h t)")
        c_nat = q_flat.rearrange("p (t n) -> p t n", t=TILES)
        cq_nat = [v_sb[:, :, :].rearrange("p t n -> p (t n)")[:, 0:Q_LORA],
                  gate_b[:, :, :].rearrange("p t n -> p (t n)")[:, 0:Q_LORA]]

        f_mem = ExitStack()
        h_fin = sb("h_fin", [128, TILES, D_MODEL], stack=f_mem)
        final_sb = sb("final_sb", [128, D_MODEL], stack=f_mem)
        f_mem.close()

        ps = ctx.enter_context(nc.psum_tensor("ps", [128, 8 * 512], fp32))

        def bank(b, n=1):
            return ps[:, b * 512:(b + n) * 512]

        raw_ready = [sem(f"raw_ready{i}") for i in range(RING)]
        x_ready = [sem(f"x_ready{g}") for g in range(GROUPS)]
        x_first = sem("x_first")
        ident_ready = sem("ident_ready")
        gain_ready = sem("gain_ready")
        const_ready = sem("const_ready")
        x_again = [sem(f"x_again{g}") for g in range(GROUPS)]
        h_stored = sem("h_stored")
        h_back = [sem(f"h_back{g}") for g in range(GROUPS)]
        gain_back = sem("gain_back")
        out_stored = sem("out_stored")
        hi_ready = sem("hi_ready")
        lo_ready = sem("lo_ready")
        unit_done = sem("unit_done")
        tile_done = sem("tile_done")
        sq_done = sem("sq_done")
        mean_done = sem("mean_done")
        norm_ready = sem("norm_ready")
        diag_ready = sem("diag_ready")
        factor_done = sem("factor_done")
        factor_ready = sem("factor_ready")
        square_ready = sem("square_ready")
        f_ready = sem("f_ready")
        turned = sem("turned")
        n_hi = sem("n_hi")
        n_lo = sem("n_lo")
        half_ready = sem("half_ready")
        lb_step = sem("lb_step")
        lb_exp = sem("lb_exp")
        sig_ready = sem("sig_ready")
        sig_clamped = sem("sig_clamped")
        logf_ready = sem("logf_ready")
        q_ready = sem("q_ready")
        k_ready = sem("k_ready")
        behind_clear = sem("behind_clear")
        behind_added = sem("behind_added")
        range_ready = sem("range_ready")
        decay_ready = sem("decay_ready")
        qk_ready = sem("qk_ready")
        own_ready = sem("own_ready")
        cross_done = sem("cross_done")
        masked_ready = sem("masked_ready")
        summed = sem("summed")
        parted = sem("parted")
        cross_ready = sem("cross_ready")
        score_done = sem("score_done")
        att_ready = sem("att_ready")
        val_ready = sem("val_ready")
        vlo_ready = sem("vlo_ready")
        own_added = sem("own_added")
        att_rounded = sem("att_rounded")
        o_done = sem("o_done")
        o_sq = sem("o_sq")
        o_ms = sem("o_ms")
        o_norm = sem("o_norm")
        gsig_ready = sem("gsig_ready")
        silu_ready = sem("silu_ready")
        y_ready = sem("y_ready")
        yturn_done = sem("yturn_done")
        y_hi = sem("y_hi")
        y_lo = sem("y_lo")
        stream_turned = sem("stream_turned")
        stream_hi = sem("stream_hi")
        stream_lo = sem("stream_lo")
        h_ready = sem("h_ready")
        h_sq = sem("h_sq")
        h_sum = sem("h_sum")
        c_sq = sem("c_sq")
        c_ms = sem("c_ms")
        c_norm = sem("c_norm")
        c_scaled = sem("c_scaled")
        c_turned = sem("c_turned")
        c_hi = sem("c_hi")
        c_lo = sem("c_lo")
        kr_raw = sem("kr_raw")
        kr_rot = sem("kr_rot")
        kr_step = sem("kr_step")
        cq_sum = sem("cq_sum")
        kn_ready = sem("kn_ready")
        v_ready = sem("v_ready")
        qn_ready = sem("qn_ready")
        qr_raw = sem("qr_raw")
        qr_rot = sem("qr_rot")
        qr_step = sem("qr_step")
        s_done = sem("s_done")
        score_masked = sem("score_masked")
        max_ready = sem("max_ready")
        neg_ready = sem("neg_ready")
        p_ready = sem("p_ready")
        pturn_done = sem("pturn_done")
        pT_ready = sem("pT_ready")
        pv_done = sem("pv_done")
        inv_ready = sem("inv_ready")
        gbsig_ready = sem("gbsig_ready")
        bsilu_ready = sem("bsilu_ready")
        yb_ready = sem("yb_ready")
        ybturn_done = sem("ybturn_done")
        yb_hi = sem("yb_hi")
        yb_lo = sem("yb_lo")
        fin_norm = sem("fin_norm")
        fin_scaled = sem("fin_scaled")

        block = ctx.enter_context(nc.Block())

        def slot(base, n):
            return (base + n) % RING

        def known(v):
            return isinstance(v, int)

        def lo_part(dve, dst, src, gain, high):
            return dve.scalar_tensor_tensor(out=dst, in0=src, scalar=gain, in1=high.bitcast(fp32),
                                            op0=ALU.mult, op1=ALU.subtract)

        def b_cols(n):
            return UNIT_Q if 4 <= n % B_UNITS < 8 else UNIT

        def half(ap, level, i):
            return ap.rearrange("p e (b i m) -> p e b i m", i=2, m=1 << level)[:, :, :, i, :]

        def q_side(mem, head=slice(0, 2)):
            return mem[:, :].rearrange("p (c e r n) -> p r e c n", c=2, e=2, r=2)[:, 1, head]

        def tile_side(mem, tile, side):
            return mem[:, :].rearrange("p (c e r n) -> p c r e n", c=2, e=2, r=2)[:, tile if side else 1 - tile, side]

        def tokens_half(tile, side, level):
            return half(tile_side(ranges, tile, side), level, side ^ tile)

        def last_token(ap, tile):
            m = ap.shape[-1]
            return ap[:, :, :, 0:1] if tile else ap[:, :, :, m - 1:m]

        def places(level, mem):
            dst = qk_dec[:, level].rearrange("p e r n -> p (e r) n")
            src = mem[:, :].rearrange("p (c x n) -> p c x n", c=2, n=128)
            if level == LEVELS - 1:
                return [(dst, src[:, 1])]
            return [(half(dst, level, 1 - c), half(src[:, c], level, 1 - c)) for c in range(2)]

        def unit_gains(unit):
            n = unit - KV0
            if 0 <= n < KV_UNITS:
                gain, rows, kt = g_kvin, 2, 2 * n
            elif KV_UNITS <= n < KV_UNITS + 8:
                gain, rows, kt = g_mla, 2, 2 * (n - KV_UNITS)
            elif KV_UNITS + 8 <= n < KV_UNITS + CQ_UNITS:
                gain, rows, kt = g_mla, 4, 4 * (n - KV_UNITS - 8)
            elif KV_UNITS + CQ_UNITS <= n < C_UNITS:
                gain, rows, kt = g_kvin, 8, 8 * (n - KV_UNITS - CQ_UNITS)
            elif B0 <= unit < OUT0 and (unit - B0) % B_UNITS >= 8:
                gain, rows, kt = g_mla, 2, 2 * ((unit - B0) % B_UNITS - 8)
            else:
                return None
            width = UNIT // rows
            return [(gain[:, kt + e:kt + e + 1], slice(e * width, (e + 1) * width)) for e in range(rows)]

        def unit_number(base, i, per, n):
            return base + i * per + n if known(i) else base + n

        def x_bank(pair):
            return 2 + pair % 6

        @block.sync
        def _(sp):
            x_rows = x.rearrange("(t p) n -> p t n", p=128)

            def load_x(g, done, cols=slice(0, 512)):
                cols = slice(g * 512 + cols.start, g * 512 + cols.stop)
                sp.dma_start(h[:, :, cols], x_rows[:, :, cols]).then_inc(done, 16)

            def load(unit, s, src, cols):
                if not known(unit) or unit >= RING:
                    sp.wait_ge(lo_ready, unit - (RING - 1))
                sp.dma_start(w_raw[:, s, 0:cols], src).then_inc(raw_ready[s], 16)

            sp.dma_start(ident, consts[:, 0:128]).then_inc(ident_ready, 16)
            load_x(0, x_first, slice(0, 256))
            load(0, 0, w_a[0], UNIT)
            sp.dma_start(gain_sb[:, :], gains).then_inc(gain_ready, 16)
            load_x(0, x_ready[0], slice(256, 512))
            for n in range(1, GROUPS):
                load_x(n, x_ready[n])
                load(n, n, w_a[n], UNIT)
            for n in range(RING, 2 * RING):
                load(n, n - RING, w_a[n], UNIT)
            sp.dma_start(const_sb[:, 128:], consts[:, 128:]).then_inc(const_ready, 16)
            sp.dma_start(mask_sb[:, :], masks).then_inc(const_ready, 16)
            with sp.Fori(2, STEPS * A_UNITS // RING) as i:
                for n in range(RING):
                    load(i * RING + n, n, w_a[i * RING + n], UNIT)
            for n in range(RING):
                load(WO0 + n, slot(WO0, n), w_o[n], UNIT)
            sp.wait_ge(cross_done, STEPS)
            def store_stream(g):
                sp.wait_ge(h_ready, TILES * (g + 1))
                cols = slice(g * 512, (g + 1) * 512)
                sp.dma_start(h_store.rearrange("(t p) n -> p t n", p=128)[:, :, cols], h[:, :, cols]).then_inc(h_stored, 16)

            for i in range(1, GROUPS * O_UNITS // RING):
                if i >= 6 and (i - 6) % 4 == 0:
                    store_stream((i - 6) // 4)
                if i <= GROUPS:
                    load_x(i - 1, x_again[i - 1])
                for n in range(RING):
                    load(WO0 + i * RING + n, n, w_o[i * RING + n], UNIT)
            for n in range(C_UNITS):
                load(KV0 + n, slot(KV0, n), w_c[n], UNIT)
                if n == RING:
                    store_stream(GROUPS - 1)
            with sp.Fori(0, STEPS) as j:
                for n in range(B_UNITS):
                    src = w_bkv[j * 4 + n] if n < 4 else w_bq[j * 4 + (n - 4)] if n < 8 else w_bg[j * 8 + (n - 8)]
                    load(j * B_UNITS + (B0 + n), slot(B0, n), src, b_cols(n))
            for n in range(2 * RING):
                load(OUT0 + n, slot(OUT0, n), w_out[n], UNIT)
            sp.wait_ge(yb_lo, STEPS)
            sp.wait_ge(h_stored, 16 * GROUPS)
            for i in range(2, GROUPS * O_UNITS // RING):
                if i < 2 + GROUPS:
                    cols = slice((i - 2) * 512, (i - 1) * 512)
                    sp.dma_start(h_fin[:, :, cols], h_store.rearrange("(t p) n -> p t n", p=128)[:, :, cols]).then_inc(h_back[i - 2], 16)
                if i == 2 + GROUPS:
                    sp.dma_start(final_sb[:, :], final_g.partition_broadcast(128)).then_inc(gain_back, 16)
                for n in range(RING):
                    load(OUT0 + i * RING + n, slot(OUT0, n), w_out[i * RING + n], UNIT)
            for part in range(TILES * GROUPS):
                tile, g = divmod(part, GROUPS)
                cols = slice(g * 512, (g + 1) * 512)
                sp.wait_ge(fin_scaled, part + 1)
                sp.dma_start(out[0, tile * 128:(tile + 1) * 128, cols], h_fin[:, tile, cols]).then_inc(out_stored, 16)
            sp.wait_ge(out_stored, TILES * GROUPS * 16)

        @block.gpsimd
        def _(pool):
            pool.memset(minus_half[:, :], -0.5).then_inc(half_ready, 1)
            pool.wait_ge(half_ready, 1)

            def rsqrt(dst, n, done):
                pool.tensor_tensor(dst[:, 0:n], ms[:, 0:n], minus_half[:, 0:n], ALU.pow).then_inc(done, 1)

            pool.wait_ge(mean_done, 1)
            rsqrt(r_x, TILES, norm_ready)

            def a_step(j):
                k_sides = ranges[:, :].rearrange("p (x r n) -> p r x n", r=2, n=128)[:, 0]
                pool.memset(k_sides, 0.0).then_inc(behind_clear, 1)
                pool.wait_ge(behind_clear, j + 1)
                for level in range(LEVELS - 1):
                    pool.wait_ge(decay_ready, j * LEVELS + (level + 1))
                    m = 1 << level
                    shape = [128, 2, 64 // m, m]
                    for tile in range(TILES):
                        to_end, to_token = tokens_half(tile, 0, level), tokens_half(tile, 1, level)
                        last = pool.tensor_tensor(to_end, to_end, last_token(to_token, tile).to_broadcast(shape), ALU.add)
                    last.then_inc(behind_added, 1)
                    pool.wait_ge(behind_added, j * (LEVELS - 1) + (level + 1))
                    for tile in range(TILES):
                        to_token = tokens_half(tile, 1, level)
                        earlier = half(tile_side(ranges, tile, 1), level, tile)
                        last = pool.tensor_tensor(to_token, to_token, last_token(earlier, tile).to_broadcast(shape), ALU.add)
                    last.then_inc(range_ready, 1)
                    if level < LEVELS - 2:
                        pool.wait_ge(range_ready, j * (LEVELS - 1) + (level + 1))
                pool.wait_ge(o_ms, j + 1)
                rsqrt(rnorm, 4, o_norm)

            with pool.Fori(0, STEPS) as j:
                a_step(j)

            pool.wait_ge(mean_done, 2)
            rsqrt(r_h, TILES, norm_ready)
            pool.wait_ge(c_ms, 2)
            pool.wait_ge(y_ready, STEPS)
            rsqrt(rnorm, TILES, c_norm)
            pool.wait_ge(c_ms, 4)
            pool.wait_ge(c_scaled, TILES)
            rsqrt(rnorm, TILES, c_norm)
            pool.wait_ge(mean_done, 3)
            rsqrt(rnorm, TILES, fin_norm)

        @block.scalar
        def _(act):
            def split_hi(base, i, per, n, cols=UNIT):
                s = slot(base, n)
                turn = (base + n - s) // RING + 1
                act.wait_ge(raw_ready[s], i * (per // RING * 16) + 16 * turn)
                if not known(i) or base + i * per + n >= RING:
                    act.wait_ge(unit_done, i * per + (base + n - RING + 1))
                for gain, at in unit_gains(unit_number(base, i, per, n)) or [(1.0, slice(0, cols))]:
                    last = act.activation(w_hi[:, s, at], w_raw[:, s, at], ACT.Copy, scale=gain)
                last.then_inc(hi_ready, 1)

            def mean(n, src, width, done):
                act.activation(ms[:, 0:n], src, ACT.Copy, scale=1.0 / width, bias=EPS).then_inc(done, 1)

            def c_mean(src, square, done):
                for t in range(TILES):
                    act.activation(ms[:, t:t + 1], src[:, t:t + 1], ACT.Copy, scale=r_h2[:, square, t:t + 1],
                                   bias=EPS).then_inc(done, 1)

            def x_hi(pair):
                act.wait_ge(turned, pair + 1)
                for e in range(2):
                    kt = 2 * pair + e
                    act.activation(nT_hi[:, kt, :], bank(x_bank(pair))[:, e * TOKENS:(e + 1) * TOKENS], ACT.Copy,
                                   scale=g_hg[:, kt:kt + 1]).then_inc(n_hi, 1)

            def x_squares(g):
                if g == 0:
                    act.wait_ge(x_first, 16)
                act.wait_ge(x_ready[g], 16)
                for t in range(TILES):
                    if g:
                        act.wait_ge(sq_done, TILES * g + t - 1)
                    act.activation((kq, level_scores)[t][:, 0:512], h[:, t, g * 512:(g + 1) * 512], ACT.Square,
                                   accum_out=sums[:, 8 + 4 * t + g:9 + 4 * t + g]).then_inc(sq_done, 1)

            split_hi(A0, 0, A_UNITS, 0)
            act.wait_ge(gain_ready, 16)
            x_hi(0)
            x_hi(1)
            for n in range(1, AHEAD):
                split_hi(A0, 0, A_UNITS, n)

            def y_out(jp):
                def gate_sigmoid():
                    act.wait_ge(unit_done, jp * A_UNITS + A_UNITS)
                    for t in range(TILES):
                        last = act.activation(gate[:, t, :], bank(4 + t), ACT.Sigmoid, scale=r_x[:, t:t + 1])
                    last.then_inc(gsig_ready, 1)

                def turned_hi():
                    act.wait_ge(yturn_done, jp + 1)
                    for c in range(4):
                        last = act.activation(aT_hi[:, ds(jp * 4 + c, 1), :], ps[:, 4 * 512 + c * 256:4 * 512 + (c + 1) * 256],
                                              ACT.Copy, scale=g_o[:, c % 2:c % 2 + 1])
                    last.then_inc(y_hi, 1)
                return gate_sigmoid, turned_hi

            def a_step(j, first):
                if not first:
                    gate_sigmoid, turned_hi = y_out(j - 1)
                for n in range(A_UNITS):
                    split_hi(A0, j, A_UNITS, n + AHEAD)
                    if first and n + 2 < KT // 2:
                        x_hi(n + 2)
                    if first and n == 3:
                        act.wait_ge(lb_step, 3)
                        act.activation(lb_tmp[:, 0:2, :], lb_tmp[:, 0:2, :], ACT.Exp).then_inc(lb_exp, 1)
                    if first and 2 <= n < 2 + GROUPS:
                        x_squares(n - 2)
                    if first and n == 6:
                        act.wait_ge(h_sum, 1)
                        mean(TILES, h_sums[:, :], D_MODEL, mean_done)
                    if n == 0 and not first:
                        gate_sigmoid()
                    if n == 2 and not first:
                        turned_hi()
                    if n == 7:
                        act.wait_ge(f_ready, j + 1)
                        for tile in range(TILES):
                            last = act.activation(tile_side(kq, tile, 0), tile_side(ranges, tile, 1), ACT.Sigmoid, scale=-1.0)
                        last.then_inc(sig_ready, 1)
                        act.wait_ge(sig_ready, j * 2 + 1)
                        act.activation(q_side(ranges), q_side(ranges), ACT.Sigmoid).then_inc(sig_ready, 1)
                    if n == 8:
                        act.wait_ge(sig_clamped, j + 1)
                        if first:
                            act.wait_ge(lb_step, 7)
                        for e in range(2):
                            head = q_side(ranges, e)
                            act.activation(head, head, ACT.Ln, scale=one_lb[:, ds(j * 2 + e, 1)],
                                           bias=lb[:, ds(j * 2 + e, 1)]).then_inc(logf_ready, 1)
                    if LEVELS_AT <= n < LEVELS_AT + LEVELS:
                        level = n - LEVELS_AT
                        if level == 0:
                            act.wait_ge(logf_ready, j * 2 + 2)
                            act.wait_ge(behind_clear, j + 1)
                        else:
                            act.wait_ge(range_ready, j * (LEVELS - 1) + level)
                        for into, tokens in places(level, ranges):
                            last = act.activation(into, tokens, ACT.Exp)
                        last.then_inc(decay_ready, 1)
                    if n == 17:
                        act.wait_ge(unit_done, j * A_UNITS + 16)
                        for t in range(TILES):
                            last = act.activation(val_hi[:, t, :], bank(2 + t), ACT.Copy, scale=r_x[:, t:t + 1])
                        last.then_inc(val_ready, 1)
                    if n == SCORES_AT[1]:
                        act.wait_ge(own_added, j + 1)
                        act.activation(att_hi[:, :, :, :], att[:, :, :, :], ACT.Copy)
                        act.activation(cross_hi[:, :, :].rearrange("p e n -> p (e n)"), cross_own[:, 0:256],
                                       ACT.Copy).then_inc(att_rounded, 1)
                    if n == OUT_AT:
                        act.wait_ge(o_done, j + 1)
                        act.wait_ge(att_ready, j + 1)
                        for i in range(4):
                            last = act.activation(ps[:, i * 256:(i + 1) * 256], ps[:, 6 * 512 + i * 256:6 * 512 + (i + 1) * 256],
                                                  ACT.Square, accum_out=sums[:, i:i + 1])
                        last.then_inc(o_sq, 1)
                        act.wait_ge(o_sq, j + 1)
                        mean(4, sums[:, 0:4], HG_VAL, o_ms)

            a_step(0, True)
            with act.Fori(1, STEPS) as j:
                a_step(j, False)

            def h_squares(g, stream, done):
                for t in range(TILES):
                    act.wait_ge(h_ready, TILES * (done - 1) + t + 1)
                    act.activation(bank(6 + t), stream[:, t, g * 512:(g + 1) * 512], ACT.Square,
                                   accum_out=sums[:, 8 + 4 * t + g:9 + 4 * t + g]).then_inc(h_sq, 1)

            def turned_stream_hi(g):
                act.wait_ge(stream_turned, g + 1)
                act.activation(nT_hi[:, 4 * g:4 * g + 4, :].rearrange("p c t -> p (c t)"), bank(4, 2),
                               ACT.Copy).then_inc(stream_hi, 1)

            gate_sigmoid, turned_hi = y_out(STEPS - 1)
            for g in range(GROUPS):
                for n in range(O_UNITS):
                    split_hi(WO0, g, O_UNITS, n + AHEAD)
                    if g == 0 and n == 0:
                        gate_sigmoid()
                    if g == 0 and n == 2:
                        turned_hi()
                    if g and n == 1:
                        h_squares(g - 1, h, g)
                    if g and n == 3:
                        turned_stream_hi(g - 1)

            for n in range(C_UNITS):
                split_hi(KV0, 0, 0, n + AHEAD)
                if n == 0:
                    h_squares(GROUPS - 1, h, GROUPS)
                if n == 1:
                    turned_stream_hi(GROUPS - 1)
                if n == 2:
                    act.wait_ge(h_sum, 2)
                    mean(TILES, h_sums[:, :], D_MODEL, mean_done)
                if n == 7:
                    act.wait_ge(unit_done, KV0 + 8)
                    act.wait_ge(stream_lo, GROUPS)
                    for t in range(TILES):
                        act.activation(bank(5 + t), bank(t), ACT.Square, accum_out=sums[:, t:t + 1]).then_inc(c_sq, 1)
                    act.wait_ge(c_sq, 2)
                    act.wait_ge(square_ready, 3)
                    c_mean(sums[:, 0:TILES], 1, c_ms)
                if n == 11:
                    act.wait_ge(c_turned, 1)
                    act.wait_ge(h_stored, 16 * GROUPS)
                    for kt in range(KT_C):
                        act.activation(cT_hi[:, kt, :], ps[:, kt * TOKENS:(kt + 1) * TOKENS], ACT.Copy,
                                       scale=g_c[:, kt:kt + 1]).then_inc(c_hi, 1)
                if n == KV_UNITS + CQ_UNITS - 1:
                    act.wait_ge(unit_done, KV0 + KV_UNITS + CQ_UNITS)
                    for t in range(TILES):
                        for i, src in enumerate((bank(3 + t), bank(5 + t)[:, 0:256])):
                            act.wait_ge(c_sq, 2 + 2 * t + i)
                            act.activation(bank(2)[:, 0:src.shape[1]], src, ACT.Square,
                                           accum_out=sums[:, 2 + 2 * t + i:3 + 2 * t + i]).then_inc(c_sq, 1)
                    act.wait_ge(cq_sum, 1)
                    c_mean(sums[:, 6:8], 2, c_ms)
            def yb_out(jp):
                def gate_sigmoid():
                    act.wait_ge(unit_done, jp * B_UNITS + (B0 + B_UNITS))
                    for t in range(TILES):
                        last = act.activation(gate_b[:, t, :], bank(2 + t), ACT.Sigmoid, scale=r_h[:, t:t + 1])
                    last.then_inc(gbsig_ready, 1)

                def turned_hi():
                    act.wait_ge(ybturn_done, jp + 1)
                    act.activation(aT_hi[:, ds(jp * 4, 4), :].rearrange("p c t -> p (c t)"), bank(6, 2), ACT.Copy).then_inc(yb_hi, 1)
                return gate_sigmoid, turned_hi

            def b_step(j, first):
                if not first:
                    gate_sigmoid, turned_hi = yb_out(j - 1)
                for n in range(B_UNITS):
                    split_hi(B0, j, B_UNITS, n + AHEAD, b_cols(n + AHEAD))
                    if n == 0 and not first:
                        gate_sigmoid()
                    if n == 1:
                        act.wait_ge(unit_done, j * B_UNITS + (B0 + 2))
                        act.activation(k_nope[:, :, :].rearrange("p h t -> p (h t)"), bank(0, 2), ACT.Copy).then_inc(kn_ready, 1)
                        if first:
                            act.wait_ge(c_turned, 2)
                            for kt in range(KT_Q):
                                act.activation(cqT_hi[:, kt, :], ps[:, 4 * 512 + kt * TOKENS:4 * 512 + (kt + 1) * TOKENS],
                                               ACT.Copy, scale=g_q[:, kt:kt + 1]).then_inc(c_hi, 1)
                    if n == 2 and not first:
                        turned_hi()
                    if n == 7:
                        act.wait_ge(unit_done, j * B_UNITS + (B0 + 8))
                        act.activation(q_rope[:, :, :].rearrange("p h t -> p (h t)"), bank(0), ACT.Copy).then_inc(qr_raw, 1)
                    if n in (12, 14):
                        pair = (12, 14).index(n)
                        act.wait_ge(pturn_done, j * 2 + (pair + 1))
                        act.activation(probT[:, :, :], bank(4 + 2 * pair, 2).rearrange("p (i n) -> p i n", i=2)[:, :, 0:384],
                                       ACT.Copy).then_inc(pT_ready, 1)
                    if n in (10, 12):
                        pair = (10, 12).index(n)
                        act.wait_ge(neg_ready, j * 2 + (pair + 1))
                        for i in range(2):
                            for t in range(TILES):
                                cols = prob[:, i, 128 * t:128 + 256 * t]
                                last = act.activation(cols, cols, ACT.Exp, scale=ATT_SCALE, bias=row_max[:, pair, t, i:i + 1],
                                                      accum_out=row_sum[:, pair, 2 * i + t:2 * i + t + 1])
                        last.then_inc(p_ready, 1)

            b_step(0, True)
            with act.Fori(1, STEPS) as j:
                b_step(j, False)

            gate_sigmoid, turned_hi = yb_out(STEPS - 1)
            for g in range(GROUPS):
                for n in range(O_UNITS):
                    if g * O_UNITS + n + AHEAD < GROUPS * O_UNITS:
                        split_hi(OUT0, g, O_UNITS, n + AHEAD)
                    if g == 0 and n == 0:
                        gate_sigmoid()
                    if g == 0 and n == 2:
                        turned_hi()
                    if g and n == 1:
                        h_squares(g - 1, h_fin, GROUPS + g)
            h_squares(GROUPS - 1, h_fin, 2 * GROUPS)
            act.wait_ge(h_sum, 3)
            mean(TILES, h_sums[:, :], D_MODEL, mean_done)

        @block.vector
        def _(dve):
            def split_lo(base, i, per, n, cols=UNIT):
                s = slot(base, n)
                dve.wait_ge(hi_ready, i * per + (base + n + 1))
                gains = unit_gains(unit_number(base, i, per, n))
                if gains is None:
                    last = dve.tensor_tensor(w_lo[:, s, 0:cols], w_raw[:, s, 0:cols], w_hi[:, s, 0:cols].bitcast(fp32),
                                             ALU.subtract)
                for gain, at in gains or []:
                    last = lo_part(dve, w_lo[:, s, at], w_raw[:, s, at], gain, w_hi[:, s, at])
                last.then_inc(lo_ready, 1)

            def x_lo(pair):
                dve.wait_ge(n_hi, 2 * pair + 2)
                for e in range(2):
                    kt = 2 * pair + e
                    lo_part(dve, nT_lo[:, kt, :], bank(x_bank(pair))[:, e * TOKENS:(e + 1) * TOKENS], g_hg[:, kt:kt + 1],
                            nT_hi[:, kt, :]).then_inc(n_lo, 1)

            def layer_logits():
                dve.tensor_tensor(lb_tmp[:, 2, :], lb_in[:, 0:HG_HEADS], lb_in[:, HG_HEADS:], ALU.max).then_inc(lb_step, 1)
                dve.wait_ge(lb_step, 1)
                for layer in range(2):
                    dve.tensor_tensor(lb_tmp[:, layer, :], lb_in[:, layer * HG_HEADS:(layer + 1) * HG_HEADS],
                                      lb_tmp[:, 2, :], ALU.subtract).then_inc(lb_step, 1)

            def lower_bounds():
                dve.wait_ge(lb_exp, 1)
                dve.tensor_tensor(lb_tmp[:, 2, :], lb_tmp[:, 0, :], lb_tmp[:, 1, :], ALU.add).then_inc(lb_step, 1)
                dve.wait_ge(lb_step, 4)
                dve.reciprocal(lb_tmp[:, 2, :], lb_tmp[:, 2, :]).then_inc(lb_step, 1)
                dve.wait_ge(lb_step, 5)
                dve.tensor_tensor(lb[:, :], lb_tmp[:, 0, :], lb_tmp[:, 2, :], ALU.mult).then_inc(lb_step, 1)
                dve.wait_ge(lb_step, 6)
                dve.tensor_scalar(one_lb[:, :], lb[:, :], -1.0, 1.0, ALU.mult, ALU.add).then_inc(lb_step, 1)

            def factor_diagonal(r, norm):
                dve.wait_ge(norm_ready, norm)
                for t in range(TILES):
                    last = dve.tensor_scalar(diag[:, t * 128:(t + 1) * 128], ident, r[:, t:t + 1], None, ALU.mult)
                last.then_inc(diag_ready, 1)

            def take_factor(b, norm):
                dve.wait_ge(factor_done, norm)
                dve.tensor_copy(row_factor[:, :], bank(b)[:, 0:TOKENS]).then_inc(factor_ready, 1)
                dve.wait_ge(factor_ready, norm)

            def by_factor(dst, src, heads):
                return dve.tensor_tensor(dst.rearrange("p (i t) -> p i t", i=heads), src.rearrange("p (i t) -> p i t", i=heads),
                                         row_factor[:, None, :].to_broadcast([128, heads, TOKENS]), ALU.mult)

            def stream_sum(squares_done, squares, done):
                dve.wait_ge(squares_done, squares)
                dve.tensor_reduce(h_sums[:, :], sums[:, 8:16].rearrange("p (t g) -> p t g", t=TILES), AX.X,
                                  ALU.add).then_inc(h_sum, 1)

            dve.memset(ones[:, :], 1.0)
            split_lo(A0, 0, A_UNITS, 0)
            dve.wait_ge(gain_ready, 16)
            x_lo(0)
            x_lo(1)
            for n in range(1, AHEAD):
                split_lo(A0, 0, A_UNITS, n)

            def y_out(jp):
                def gated():
                    dve.wait_ge(gsig_ready, jp + 1)
                    for t in range(TILES):
                        last = dve.scalar_tensor_tensor(out=gate[:, t, :], in0=bank(4 + t), scalar=r_x[:, t:t + 1],
                                                        in1=gate[:, t, :], op0=ALU.mult, op1=ALU.mult)
                    last.then_inc(silu_ready, 1)
                    dve.wait_ge(silu_ready, jp + 1)
                    dve.wait_ge(o_norm, jp + 1)
                    for t in range(TILES):
                        for e in range(2):
                            cols = gate[:, t, e * HG_VAL:(e + 1) * HG_VAL]
                            i = 2 * t + e
                            last = dve.scalar_tensor_tensor(
                                out=cols, in0=ps[:, 6 * 512 + i * HG_VAL:6 * 512 + (i + 1) * HG_VAL],
                                scalar=rnorm[:, i:i + 1], in1=cols, op0=ALU.mult, op1=ALU.mult)
                    last.then_inc(y_ready, 1)

                def turned_lo():
                    dve.wait_ge(y_hi, jp + 1)
                    for c in range(4):
                        last = lo_part(dve, aT_lo[:, ds(jp * 4 + c, 1), :], ps[:, 4 * 512 + c * 256:4 * 512 + (c + 1) * 256],
                                       g_o[:, c % 2:c % 2 + 1], aT_hi[:, ds(jp * 4 + c, 1), :])
                    last.then_inc(y_lo, 1)
                return gated, turned_lo

            def a_step(j, first):
                def decayed(level):
                    dve.wait_ge(decay_ready, j * LEVELS + (level + 1))
                    if level == 0:
                        dve.wait_ge(q_ready, j + 1)
                        dve.wait_ge(k_ready, j + 1)
                    for into, tokens in places(level, kq):
                        last = dve.tensor_tensor(into, into, tokens, ALU.mult)
                    last.then_inc(qk_ready, 1)

                def take_scores(head):
                    base = (6, 0)[head] * 512
                    dve.wait_ge(score_done, j * 2 + (head + 1))
                    if head or not first:
                        dve.wait_ge(summed, j * 2 + head)
                    dve.tensor_tensor(level_scores[:, :], ps[:, base:base + LEVEL_COLS], mask_sb[:, 0:LEVEL_COLS],
                                      ALU.mult).then_inc(masked_ready, 1)
                    dve.wait_ge(masked_ready, j * 2 + (head + 1))
                    dve.tensor_reduce(both_tiles[:, head, :], level_scores[:, :].rearrange("p (l t) -> p t l", l=LEVELS - 1),
                                      AX.X, ALU.add).then_inc(summed, 1)
                    dve.wait_ge(summed, j * 2 + (head + 1))
                    dve.tensor_tensor(att[:, head, :, :], both_tiles[:, head, None, :].to_broadcast([128, TILES, 128]),
                                      mask_sb[:, LEVEL_COLS:].rearrange("p (t n) -> p t n", t=TILES),
                                      ALU.mult).then_inc(parted, 1)

                def add_own():
                    dve.wait_ge(cross_done, j + 1)
                    dve.tensor_copy(cross_own[:, :], bank(2)[:, 0:256 + 2 * TILES]).then_inc(cross_ready, 1)
                    dve.wait_ge(cross_ready, j + 1)
                    dve.wait_ge(parted, j * 2 + 2)
                    for head in range(2):
                        for tile in range(TILES):
                            i = TILES * head + tile
                            scores = att[:, head, tile, :]
                            last = dve.scalar_tensor_tensor(out=scores, in0=ident, scalar=own[:, i:i + 1], in1=scores,
                                                            op0=ALU.mult, op1=ALU.add)
                    last.then_inc(own_added, 1)
                    dve.wait_ge(att_rounded, j + 1)
                    for lo, whole, high in ((att_lo[:, :, :, :], att[:, :, :, :], att_hi[:, :, :, :]),
                                            (cross_lo[:, :, :], cross_whole, cross_hi[:, :, :])):
                        last = dve.tensor_tensor(lo, whole, high.bitcast(fp32), ALU.subtract)
                    last.then_inc(att_ready, 1)

                if not first:
                    gated, turned_lo = y_out(j - 1)
                for n in range(A_UNITS):
                    split_lo(A0, j, A_UNITS, n + AHEAD)
                    if first and n + 2 < KT // 2:
                        x_lo(n + 2)
                    if first and n == 2:
                        layer_logits()
                    if first and n == 4:
                        lower_bounds()
                    if first and n == 5:
                        stream_sum(sq_done, TILES * GROUPS, 1)
                    if first and n == 6:
                        factor_diagonal(r_x, 1)
                    if n == 0 and not first:
                        gated()
                    if n == 2 and not first:
                        turned_lo()
                    if n == 7:
                        dve.wait_ge(unit_done, j * A_UNITS + 8)
                        if first:
                            take_factor(6, 1)
                        for mem, b, done in ((ranges, 1, f_ready), (kq, 0, q_ready)):
                            dve.tensor_tensor(q_side(mem), bank(b).rearrange("p (e t n) -> p e t n", e=2, t=TILES),
                                              row_factor[:, :].rearrange("p (t n) -> p t n", t=TILES)[:, None]
                                              .to_broadcast([128, 2, TILES, 128]), ALU.mult).then_inc(done, 1)
                    if n == 8:
                        dve.wait_ge(sig_ready, j * 2 + 2)
                        dve.tensor_scalar(q_side(ranges), q_side(ranges), SMALLEST_F, None, ALU.max).then_inc(sig_clamped, 1)
                        if first:
                            dve.wait_ge(lb_step, 7)
                        for e in range(2):
                            head = kq[:, :].rearrange("p (c e r n) -> p e r c n", c=2, e=2, r=2)[:, e, 0]
                            last = dve.tensor_scalar(head, head, one_lb[:, ds(j * 2 + e, 1)], None, ALU.mult)
                        last.then_inc(k_ready, 1)
                    if LEVELS_AT <= n < LEVELS_AT + LEVELS:
                        decayed(n - LEVELS_AT)
                    if n == LEVELS_AT + LEVELS:
                        dve.wait_ge(qk_ready, j * LEVELS + LEVELS)
                        for tile in range(TILES):
                            k_mem = tile_side(kq, tile, 0)
                            last = dve.tensor_tensor(k_mem, k_mem, tile_side(kq, tile, 1), ALU.mult)
                        last.then_inc(own_ready, 1)
                    if n in SCORES_AT:
                        if first:
                            dve.wait_ge(const_ready, 2 * 16)
                        take_scores(SCORES_AT.index(n))
                    if n == 17:
                        dve.wait_ge(val_ready, j + 1)
                        for t in range(TILES):
                            last = lo_part(dve, val_lo[:, t, :], bank(2 + t), r_x[:, t:t + 1], val_hi[:, t, :])
                        last.then_inc(vlo_ready, 1)
                    if n == SCORES_AT[1]:
                        add_own()

            a_step(0, True)
            with dve.Fori(1, STEPS) as j:
                a_step(j, False)

            def residual(g, stream, loaded, banks, done, last=0):
                dve.wait_ge(loaded, 16)
                for t in range(TILES):
                    if t == 0 and last:
                        dve.wait_ge(tile_done, last)
                    else:
                        dve.wait_ge(unit_done, done)
                    cols = stream[:, t, g * 512:(g + 1) * 512]
                    dve.tensor_tensor(cols, bank(banks + t), cols, ALU.add).then_inc(h_ready, 1)

            def turned_stream_lo(g):
                dve.wait_ge(stream_hi, g + 1)
                dve.tensor_tensor(nT_lo[:, 4 * g:4 * g + 4, :].rearrange("p c t -> p (c t)"), bank(4, 2),
                                  nT_hi[:, 4 * g:4 * g + 4, :].rearrange("p c t -> p (c t)").bitcast(fp32),
                                  ALU.subtract).then_inc(stream_lo, 1)

            gated, turned_lo = y_out(STEPS - 1)
            for g in range(GROUPS):
                for n in range(O_UNITS):
                    split_lo(WO0, g, O_UNITS, n + AHEAD)
                    if g == 0 and n == 0:
                        gated()
                    if g == 0 and n == 2:
                        turned_lo()
                    if g and n == 0:
                        residual(g - 1, h, x_again[g - 1], 2 * ((g - 1) % 2), WO0 + g * O_UNITS)
                    if g and n == 3:
                        turned_stream_lo(g - 1)
            for n in range(C_UNITS):
                split_lo(KV0, 0, 0, n + AHEAD)
                if n == 0:
                    residual(GROUPS - 1, h, x_again[GROUPS - 1], 2 * ((GROUPS - 1) % 2), KV0, 1)
                if n == 1:
                    turned_stream_lo(GROUPS - 1)
                    stream_sum(h_sq, TILES * GROUPS, 2)
                if n == 3:
                    factor_diagonal(r_h, 2)
                    dve.tensor_tensor(r_h2[:, 0, :], r_h[:, :], r_h[:, :], ALU.mult).then_inc(square_ready, 1)
                    dve.wait_ge(square_ready, 1)
                    for i, width in ((1, KV_LORA), (2, Q_LORA)):
                        dve.tensor_scalar(r_h2[:, i, :], r_h2[:, 0, :], 1.0 / width, None, ALU.mult).then_inc(square_ready, 1)
                if n == 5:
                    take_factor(7, 2)
                if n == 7:
                    dve.wait_ge(c_norm, 1)
                    for t in range(TILES):
                        dve.tensor_scalar(c_nat[:, t, :], bank(t), rnorm[:, t:t + 1], r_h[:, t:t + 1],
                                          ALU.mult, ALU.mult).then_inc(c_scaled, 1)
                    dve.memset(k_even[:, :], 0.0).then_inc(kr_step, 1)
                    dve.memset(k_odd[:, :], 0.0).then_inc(kr_step, 1)
                if n == KV_UNITS + CQ_UNITS - 1:
                    dve.wait_ge(c_sq, 6)
                    dve.tensor_reduce(sums[:, 6:8], sums[:, 2:6].rearrange("p (t g) -> p t g", t=TILES), AX.X,
                                      ALU.add).then_inc(cq_sum, 1)
                    dve.wait_ge(c_norm, 2)
                    for t in range(TILES):
                        for cols, src in ((slice(0, 512), bank(3 + t)), (slice(512, Q_LORA), bank(5 + t)[:, 0:256])):
                            dve.tensor_scalar(cq_nat[t][:, cols], src, rnorm[:, t:t + 1], r_h[:, t:t + 1],
                                              ALU.mult, ALU.mult).then_inc(c_scaled, 1)
                if n == C_UNITS - 1:
                    dve.wait_ge(unit_done, B0)
                    by_factor(rot_sb[:, 0, :], bank(7)[:, 0:TOKENS], 1).then_inc(kr_raw, 1)
                if n == 11:
                    for kt in range(KT_C):
                        dve.wait_ge(c_hi, kt // 2 * 2 + 2)
                        lo_part(dve, cT_lo[:, kt, :], ps[:, kt * TOKENS:(kt + 1) * TOKENS], g_c[:, kt:kt + 1],
                                cT_hi[:, kt, :]).then_inc(c_lo, 1)

            def yb_out(jp):
                def gated():
                    dve.wait_ge(gbsig_ready, jp + 1)
                    for t in range(TILES):
                        last = dve.scalar_tensor_tensor(out=gate_b[:, t, :], in0=bank(2 + t), scalar=r_h[:, t:t + 1],
                                                        in1=gate_b[:, t, :], op0=ALU.mult, op1=ALU.mult)
                    last.then_inc(bsilu_ready, 1)
                    dve.wait_ge(bsilu_ready, jp + 1)
                    dve.wait_ge(inv_ready, jp + 1)
                    dve.wait_ge(pv_done, jp * 2 + 2)
                    for pair in range(2):
                        for i in range(2):
                            for t in range(TILES):
                                m = 2 * pair + i
                                cols = gate_b[:, t, m * V_DIM:(m + 1) * V_DIM]
                                at = (4 + pair) * 512 + (2 * i + t) * V_DIM
                                last = dve.scalar_tensor_tensor(
                                    out=cols, in0=ps[:, at:at + V_DIM], scalar=row_sum[:, pair, 2 * i + t:2 * i + t + 1],
                                    in1=cols, op0=ALU.mult, op1=ALU.mult)
                    last.then_inc(yb_ready, 1)

                def turned_lo():
                    dve.wait_ge(yb_hi, jp + 1)
                    dve.tensor_tensor(aT_lo[:, ds(jp * 4, 4), :].rearrange("p c t -> p (c t)"), bank(6, 2),
                                      aT_hi[:, ds(jp * 4, 4), :].rearrange("p c t -> p (c t)").bitcast(fp32),
                                      ALU.subtract).then_inc(yb_lo, 1)
                return gated, turned_lo

            def b_step(j, first):
                def row_maxima(pair):
                    dve.wait_ge(s_done, j * 2 + (pair + 1))
                    if pair:
                        dve.wait_ge(pturn_done, j * 2 + 1)
                    dve.tensor_tensor(prob[:, :, :], bank(4 + 2 * pair, 2).rearrange("p (i n) -> p i n", i=2)[:, :, 0:384],
                                      causal[:, None, :].to_broadcast([128, 2, 384]), ALU.add).then_inc(score_masked, 1)
                    dve.wait_ge(score_masked, j * 2 + (pair + 1))
                    for t in range(TILES):
                        last = dve.tensor_reduce(row_max[:, pair, t, :], prob[:, :, 128 * t:128 + 256 * t], AX.X, ALU.max)
                    last.then_inc(max_ready, 1)
                    dve.wait_ge(max_ready, j * 2 + (pair + 1))
                    dve.tensor_scalar(row_max[:, pair, :, :], row_max[:, pair, :, :], -ATT_SCALE, None,
                                      ALU.mult).then_inc(neg_ready, 1)

                if not first:
                    gated, turned_lo = yb_out(j - 1)
                for n in range(B_UNITS):
                    split_lo(B0, j, B_UNITS, n + AHEAD, b_cols(n + AHEAD))
                    if n == 0 and not first:
                        gated()
                    if n == 1 and first:
                        for kt in range(KT_Q):
                            dve.wait_ge(c_hi, KT_C + KT_Q)
                            lo_part(dve, cqT_lo[:, kt, :], ps[:, 4 * 512 + kt * TOKENS:4 * 512 + (kt + 1) * TOKENS],
                                    g_q[:, kt:kt + 1], cqT_hi[:, kt, :]).then_inc(c_lo, 1)
                        dve.wait_ge(kr_rot, 1)
                        dve.tensor_tensor(rot_sb[:, 1, :], bank(7)[:, 256:512], sin_sb, ALU.mult).then_inc(kr_step, 1)
                        dve.tensor_tensor(rot_sb[:, 0, :], rot_sb[:, 0, :], cos_sb, ALU.mult).then_inc(kr_step, 1)
                        dve.wait_ge(kr_step, 4)
                        dve.tensor_tensor(k_even[0:64, :], rot_sb[0:64, 0, :], rot_sb[0:64, 1, :], ALU.add).then_inc(kr_step, 1)
                        dve.tensor_tensor(k_odd[64:128, :], rot_sb[64:128, 0, :], rot_sb[64:128, 1, :], ALU.add).then_inc(kr_step, 1)
                    if n == 2 and not first:
                        turned_lo()
                    if n == 3:
                        dve.wait_ge(unit_done, j * B_UNITS + (B0 + 4))
                        dve.tensor_copy(v_sb[:, :, :].rearrange("p t n -> p (t n)"), bank(2, 2)).then_inc(v_ready, 1)
                    if n == 7:
                        dve.wait_ge(unit_done, j * B_UNITS + (B0 + 8))
                        dve.tensor_copy(q_nope[:, :, :].rearrange("p h t -> p (h t)"), bank(4, 2)).then_inc(qn_ready, 1)
                    if n == 8:
                        dve.wait_ge(qr_rot, j + 1)
                        dve.tensor_tensor(rot_sb[:, :, :], bank(1).rearrange("p (i t) -> p i t", i=2),
                                          sin_sb[:, None, :].to_broadcast([128, 2, TOKENS]), ALU.mult).then_inc(qr_step, 1)
                        dve.tensor_tensor(q_rope[:, :, :], q_rope[:, :, :],
                                          cos_sb[:, None, :].to_broadcast([128, 2, TOKENS]), ALU.mult).then_inc(qr_step, 1)
                        dve.wait_ge(qr_step, j * 3 + 2)
                        dve.tensor_tensor(q_rope[:, :, :], q_rope[:, :, :], rot_sb[:, :, :], ALU.add).then_inc(qr_step, 1)
                    if n in (10, 12):
                        row_maxima((10, 12).index(n))
                    if n == 15:
                        dve.wait_ge(p_ready, j * 2 + 2)
                        dve.reciprocal(row_sum[:, :, :], row_sum[:, :, :]).then_inc(inv_ready, 1)

            b_step(0, True)
            with dve.Fori(1, STEPS) as j:
                b_step(j, False)

            gated, turned_lo = yb_out(STEPS - 1)
            for g in range(GROUPS):
                for n in range(O_UNITS):
                    if g * O_UNITS + n + AHEAD < GROUPS * O_UNITS:
                        split_lo(OUT0, g, O_UNITS, n + AHEAD)
                    if g == 0 and n == 0:
                        gated()
                    if g == 0 and n == 2:
                        turned_lo()
                    if g and n == 0:
                        residual(g - 1, h_fin, h_back[g - 1], 2 * ((g - 1) % 2), OUT0 + g * O_UNITS)
            residual(GROUPS - 1, h_fin, h_back[GROUPS - 1], 2 * ((GROUPS - 1) % 2), UNITS, 2)
            stream_sum(h_sq, 2 * TILES * GROUPS, 3)
            dve.wait_ge(fin_norm, 1)
            dve.wait_ge(gain_back, 16)
            for part in range(TILES * GROUPS):
                t, g = divmod(part, GROUPS)
                cols = h_fin[:, t, g * 512:(g + 1) * 512]
                dve.scalar_tensor_tensor(out=cols, in0=cols, scalar=rnorm[:, t:t + 1],
                                         in1=final_sb[:, g * 512:(g + 1) * 512],
                                         op0=ALU.mult, op1=ALU.mult).then_inc(fin_scaled, 1)

        @block.tensor
        def _(pe):
            def natural(base, i, per, n, xT, kts, cols, banks, first, last, tile_done=None):
                s = slot(base, n)
                pe.wait_ge(lo_ready, i * per + (base + n + 1))
                order = [(e, t) for e in range(len(kts)) for t in range(TILES)]
                if tile_done:
                    order.sort(key=lambda et: et[1])
                for e, t in order:
                    w = slice(e * cols, (e + 1) * cols)
                    acc = bank(banks[t])[:, 0:cols]
                    tile = slice(t * 128, (t + 1) * 128)
                    pe.matmul(acc, xT[0][:, kts[e], tile], w_hi[:, s, w], start=first and e == 0, stop=False)
                    pe.matmul(acc, xT[0][:, kts[e], tile], w_lo[:, s, w], start=False, stop=False)
                    mm = pe.matmul(acc, xT[1][:, kts[e], tile], w_hi[:, s, w], start=False,
                                   stop=last and e == len(kts) - 1)
                    if tile_done and t == 0 and e == len(kts) - 1:
                        mm.then_inc(tile_done, 1)
                return mm.then_inc(unit_done, 1)

            def turned_out(base, i, per, n, xT, parts):
                s = slot(base, n)
                pe.wait_ge(lo_ready, i * per + (base + n + 1))
                for place, kt, at, first, last in parts:
                    w = slice(place * 128, (place + 1) * 128)
                    acc = ps[:, at:at + TOKENS]
                    pe.matmul(acc, w_hi[:, s, w], xT[0][:, kt, :], start=first, stop=False, skip_group_check=True)
                    pe.matmul(acc, w_hi[:, s, w], xT[1][:, kt, :], start=False, stop=False, skip_group_check=True)
                    mm = pe.matmul(acc, w_lo[:, s, w], xT[0][:, kt, :], start=False, stop=last, skip_group_check=True)
                return mm.then_inc(unit_done, 1)

            nT = (nT_hi, nT_lo)
            aT = (aT_hi, aT_lo)
            cT = (cT_hi, cT_lo)
            cqT = (cqT_hi, cqT_lo)

            def turn_x(pair):
                pe.wait_ge(x_ready[pair // 2] if pair else x_first, 16)
                if pair >= 6:
                    pe.wait_ge(n_lo, 2 * (pair - 6) + 2)
                for e in range(2):
                    for t in range(TILES):
                        at = x_bank(pair) * 512 + e * TOKENS + t * 128
                        kt = 2 * pair + e
                        mm = pe.transpose(ps[:, at:at + 128], h[:, t, kt * 128:(kt + 1) * 128], ident)
                mm.then_inc(turned, 1)

            def turn_stream(g):
                pe.wait_ge(h_ready, TILES * (g + 1))
                if g:
                    pe.wait_ge(stream_lo, g)
                for c in range(4):
                    for t in range(TILES):
                        at = 4 * 512 + c * TOKENS + t * 128
                        mm = pe.transpose(ps[:, at:at + 128], h[:, t, (4 * g + c) * 128:(4 * g + c + 1) * 128], ident)
                mm.then_inc(stream_turned, 1)

            def factor_rows(b, norm):
                pe.wait_ge(diag_ready, norm)
                pe.matmul(bank(b)[:, 0:TOKENS], ones[:, :], diag[:, :], start=True, stop=True).then_inc(factor_done, 1)

            pe.wait_ge(ident_ready, 16)
            turn_x(0)
            turn_x(1)

            def turn_y(src, first_bank, done):
                for c in range(4):
                    for t in range(TILES):
                        at = first_bank * 512 + c * TOKENS + t * 128
                        mm = pe.transpose(ps[:, at:at + 128], src[:, t, c * 128:(c + 1) * 128], ident)
                mm.then_inc(done, 1)

            def a_step(j, first):
                def scores(head):
                    pe.wait_ge(qk_ready, j * LEVELS + LEVELS)
                    base = (6, 0)[head] * 512
                    for level in range(LEVELS - 1):
                        mm = pe.matmul(ps[:, base + level * 128:base + (level + 1) * 128], qk_dec[:, level, head, 0, :],
                                       qk_dec[:, level, head, 1, :], start=True, stop=True)
                    mm.then_inc(score_done, 1)

                def cross_and_own():
                    pe.wait_ge(vlo_ready, j + 1)
                    pe.wait_ge(own_ready, j + 1)
                    for head in range(2):
                        pe.matmul(bank(2)[:, head * 128:(head + 1) * 128], qk_dec[:, LEVELS - 1, head, 0, :],
                                  qk_dec[:, LEVELS - 1, head, 1, :], start=True, stop=True)
                        for tile in range(TILES):
                            i = 256 + TILES * head + tile
                            mm = pe.matmul(bank(2)[:, i:i + 1], tile_side(kq, tile, 0)[:, head], ones[:, 0:1],
                                           start=True, stop=True)
                    mm.then_inc(cross_done, 1)

                for n in range(A_UNITS):
                    u = n % 8
                    kts = (2 * u, 2 * u + 1)
                    if n < 8:
                        if first:
                            pe.wait_ge(n_lo, 2 * u + 2)
                        elif n == 0:
                            pe.wait_ge(o_sq, j)
                        parts = [(4 * e + m, kts[e], m * TOKENS, u == 0 and e == 0 and m % 2 == 0, u == 7 and e == 1)
                                 for e in range(2) for m in range(4)]
                        turned_out(A0, j, A_UNITS, n, nT, parts)
                        if first and n + 2 < KT // 2:
                            turn_x(n + 2)
                        if first and n == 7:
                            factor_rows(6, 1)
                    elif n < 16:
                        if n == 8 and not first:
                            pe.wait_ge(vlo_ready, j)
                            pe.wait_ge(cross_ready, j)
                        natural(A0, j, A_UNITS, n, nT, kts, 512, (2, 3), u == 0, u == 7)
                    else:
                        if n == 16 and not first:
                            pe.wait_ge(y_lo, j)
                        natural(A0, j, A_UNITS, n, nT, kts, 512, (4, 5), u == 0, u == 7)
                    if n == 2 and not first:
                        pe.wait_ge(y_ready, j)
                        turn_y(gate, 4, yturn_done)
                    if n in SCORES_AT:
                        scores(SCORES_AT.index(n))
                    if n == SCORES_AT[1]:
                        cross_and_own()
                    if n == OUT_AT:
                        pe.wait_ge(att_ready, j + 1)
                        for e in range(2):
                            v = slice(e * HG_VAL, (e + 1) * HG_VAL)
                            at0, at1, cross = ([hi, lo] for hi, lo in ((att_hi[:, e, 0, :], att_lo[:, e, 0, :]),
                                                                      (att_hi[:, e, 1, :], att_lo[:, e, 1, :]),
                                                                      (cross_hi[:, e, :], cross_lo[:, e, :])))
                            for b, pairs in ((6, ((at0, 0),)), (7, ((cross, 0), (at1, 1)))):
                                for k, (a, t) in enumerate(pairs):
                                    pe.matmul(bank(b)[:, v], a[0], val_hi[:, t, v], start=k == 0, stop=False)
                                    pe.matmul(bank(b)[:, v], a[0], val_lo[:, t, v], start=False, stop=False)
                                    mm = pe.matmul(bank(b)[:, v], a[1], val_hi[:, t, v], start=False, stop=k == len(pairs) - 1)
                        mm.then_inc(o_done, 1)

            a_step(0, True)
            with pe.Fori(1, STEPS) as j:
                a_step(j, False)

            def project(base, h_before, y_count, extra, turn):
                for g in range(GROUPS):
                    for n in range(O_UNITS):
                        if g == 0 and n == 0:
                            extra(0)
                        if g == 1 and n == 0:
                            extra(1)
                        if g >= 2 and n == 0:
                            pe.wait_ge(h_ready, TILES * (h_before + g - 1))
                        if g == 0 and n == O_UNITS - 2:
                            pe.wait_ge(y_count, STEPS)
                        b = 2 * (g % 2)
                        natural(base, g, O_UNITS, n, aT, (2 * n, 2 * n + 1), 512, (b, b + 1), n == 0, n == O_UNITS - 1,
                                tile_done if g == GROUPS - 1 and n == O_UNITS - 1 else None)
                        if n == 2:
                            turn(g)

            def wo_banks(g):
                if g == 0:
                    pe.wait_ge(o_sq, STEPS)
                else:
                    pe.wait_ge(vlo_ready, STEPS)
                    pe.wait_ge(cross_ready, STEPS)

            def wo_turn(g):
                if g == 0:
                    pe.wait_ge(y_ready, STEPS)
                    turn_y(gate, 4, yturn_done)
                else:
                    turn_stream(g - 1)

            project(WO0, 0, y_lo, wo_banks, wo_turn)

            def rotated(dst, src):
                return pe.matmul(dst, rotate, src, start=True, stop=True)

            for n in range(C_UNITS):
                if n < 8:
                    if n == 0:
                        pe.wait_ge(h_ready, TILES * 3)
                    pe.wait_ge(stream_lo, n // 2 + 1)
                    natural(KV0, 0, 0, n, nT, (2 * n, 2 * n + 1), 512, (0, 1), n == 0, n == 7)
                elif n < KV_UNITS + 8:
                    u = n - KV_UNITS
                    natural(KV0, 0, 0, n, nT, (2 * u, 2 * u + 1), 512, (3, 4), u == 0, u == 7)
                elif n < KV_UNITS + CQ_UNITS:
                    u = n - KV_UNITS - 8
                    if u == 0:
                        pe.wait_ge(c_sq, 2)
                    natural(KV0, 0, 0, n, nT, range(4 * u, 4 * u + 4), 256, (5, 6), u == 0, u == 3)
                else:
                    u = n - KV_UNITS - CQ_UNITS
                    if u == 0:
                        pe.wait_ge(factor_ready, 2)
                    turned_out(KV0, 0, 0, n, nT, [(e, 8 * u + e, 7 * 512, u == 0 and e == 0, u == 1 and e == 7)
                                                  for e in range(8)])
                if n == 1:
                    turn_stream(GROUPS - 1)
                if n == 5:
                    factor_rows(7, 2)
                if n == 11:
                    pe.wait_ge(c_scaled, 2)
                    for kt in range(KT_C):
                        for t in range(TILES):
                            at = kt * TOKENS + t * 128
                            mm = pe.transpose(ps[:, at:at + 128], c_nat[:, t, kt * 128:(kt + 1) * 128], ident)
                    mm.then_inc(c_turned, 1)

            def b_step(j, first):
                def head_scores(pair):
                    for i in range(2):
                        m = 2 * pair + i
                        key = (k_even, k_odd)[i]
                        for t in range(TILES):
                            q = slice(t * 128, (t + 1) * 128)
                            keys = slice(0, (t + 1) * 128)
                            at = (4 + 2 * pair + i) * 512 + 128 * t
                            acc = ps[:, at:at + (t + 1) * 128]
                            pe.matmul(acc, q_nope[:, m, q], k_nope[:, m, keys], start=True, stop=False)
                            mm = pe.matmul(acc, q_rope[:, pair, q], key[:, keys], start=False, stop=True)
                    mm.then_inc(s_done, 1)

                def turn_probs(pair):
                    pe.wait_ge(p_ready, j * 2 + (pair + 1))
                    for i in range(2):
                        for c in range(3):
                            at = (4 + 2 * pair + i) * 512 + c * 128
                            mm = pe.transpose(ps[:, at:at + 128], prob[:, i, c * 128:(c + 1) * 128], ident)
                    mm.then_inc(pturn_done, 1)

                def weigh_values(pair):
                    pe.wait_ge(pT_ready, j * 2 + (pair + 1))
                    for i in range(2):
                        v = slice((2 * pair + i) * V_DIM, (2 * pair + i + 1) * V_DIM)
                        at = (4 + pair) * 512 + i * 256
                        pe.matmul(ps[:, at:at + 128], probT[:, i, 0:128], v_sb[:, 0, v], start=True, stop=True)
                        pe.matmul(ps[:, at + 128:at + 256], probT[:, i, 128:256], v_sb[:, 0, v], start=True, stop=False)
                        mm = pe.matmul(ps[:, at + 128:at + 256], probT[:, i, 256:384], v_sb[:, 1, v], start=False, stop=True)
                    mm.then_inc(pv_done, 1)

                for n in range(B_UNITS):
                    if n < 2:
                        if first and n == 0:
                            pe.wait_ge(c_lo, KT_C)
                        parts = [(4 * e + m, 2 * n + e, m * TOKENS, n == 0 and e == 0 and m % 2 == 0, n == 1 and e == 1)
                                 for e in range(2) for m in range(4)]
                        turned_out(B0, j, B_UNITS, n, cT, parts)
                    elif n < 4:
                        if n == 2:
                            if first:
                                pe.wait_ge(c_scaled, 6)
                            else:
                                pe.wait_ge(bsilu_ready, j)
                        natural(B0, j, B_UNITS, n, cT, (2 * (n - 2), 2 * (n - 2) + 1), 512, (2, 3), n == 2, n == 3)
                    elif n < 8:
                        if n == 4:
                            pe.wait_ge(kn_ready, j + 1)
                            if first:
                                pe.wait_ge(c_lo, KT_C + KT_Q)
                            else:
                                pe.wait_ge(yb_ready, j)
                        parts = []
                        for place in range(9):
                            kt, m = divmod((n - 4) * 9 + place, 6)
                            at = (4 * 512 + m * TOKENS) if m < 4 else (m - 4) * TOKENS
                            parts.append((place, kt, at, kt == 0 and m % 2 == 0, kt == KT_Q - 1))
                        turned_out(B0, j, B_UNITS, n, cqT, parts)
                    else:
                        if n == 8:
                            pe.wait_ge(v_ready, j + 1)
                        u = n - 8
                        natural(B0, j, B_UNITS, n, nT, (2 * u, 2 * u + 1), 512, (2, 3), u == 0, u == 7)
                    if n == 0 and first:
                        pe.wait_ge(c_scaled, 6)
                        for kt in range(KT_Q):
                            for t in range(TILES):
                                at = 4 * 512 + kt * TOKENS + t * 128
                                mm = pe.transpose(ps[:, at:at + 128], cq_nat[t][:, kt * 128:(kt + 1) * 128], ident)
                        mm.then_inc(c_turned, 1)
                        pe.wait_ge(const_ready, 2 * 16)
                        pe.wait_ge(kr_raw, 1)
                        rotated(bank(7)[:, 256:512], rot_sb[:, 0, :]).then_inc(kr_rot, 1)
                    if n == 2 and not first:
                        pe.wait_ge(yb_ready, j)
                        turn_y(gate_b, 6, ybturn_done)
                    if n == 8:
                        pe.wait_ge(qr_raw, j + 1)
                        rotated(bank(1), q_rope[:, :, :].rearrange("p i t -> p (i t)")).then_inc(qr_rot, 1)
                    if n == 10:
                        pe.wait_ge(qn_ready, j + 1)
                        pe.wait_ge(qr_step, j * 3 + 3)
                        if first:
                            pe.wait_ge(kr_step, 6)
                        head_scores(0)
                    if n == 12:
                        turn_probs(0)
                        if not first:
                            pe.wait_ge(yb_lo, j)
                        head_scores(1)
                    if n == 13:
                        weigh_values(0)
                    if n == 14:
                        turn_probs(1)
                    if n == 15:
                        weigh_values(1)

            b_step(0, True)
            with pe.Fori(1, STEPS) as j:
                b_step(j, False)

            def out_banks(g):
                if g == 1:
                    pe.wait_ge(bsilu_ready, STEPS)

            def out_turn(g):
                if g == 0:
                    pe.wait_ge(yb_ready, STEPS)
                    turn_y(gate_b, 6, ybturn_done)

            project(OUT0, GROUPS, yb_lo, out_banks, out_turn)


def token_order():
    import numpy as np
    return np.concatenate([np.arange(128), np.arange(TOKENS - 1, 127, -1)])


def score_masks():
    import numpy as np
    s, t = np.arange(128)[:, None], np.arange(128)[None, :]
    masks = [(s ^ t) >> level == 1 for level in range(LEVELS - 1)] + [s < t, s > t]
    return np.ascontiguousarray(np.concatenate(masks, axis=1).astype(np.float32))


def constants():
    import numpy as np
    rot = np.zeros((128, 128), np.float32)
    for b in (0, 64):
        for i in range(32):
            rot[b + 32 + i, b + i] = -1.0
            rot[b + i, b + 32 + i] = 1.0
    pos = np.arange(TOKENS, dtype=np.float32)
    freq = (np.float32(10000.0) ** (-np.arange(0, ROPE, 2, dtype=np.float32) / np.float32(ROPE))).astype(np.float32)
    ang = np.tile((pos[:, None] * freq[None, :]).astype(np.float32)[token_order()].T, (4, 1))
    q, k = np.arange(128)[:, None], np.arange(128)[None, :]
    causal = np.concatenate([np.where(k <= q, 0.0, MASKED), np.zeros((128, 128)), np.where(k >= q, 0.0, MASKED)], axis=1)
    parts = [np.eye(128), rot, np.cos(ang), np.sin(ang), causal]
    return np.ascontiguousarray(np.concatenate([p.astype(np.float32) for p in parts], axis=1))


def units(w, rows_per_unit, cols):
    import numpy as np
    k, n = w.shape
    a = w.reshape(k // (128 * rows_per_unit), rows_per_unit, 128, n // cols, cols)
    return np.ascontiguousarray(a.transpose(3, 0, 2, 1, 4)).reshape(n // cols, -1, 128, rows_per_unit * cols)


def by_column(v):
    return v.reshape(-1, 128).T


def kernel(x, norm_g, hg_w_in, hg_g_norm, hg_w_out, hg_lb, kv_in_norm_g, w_kv_down, kv_norm_g,
           w_kv_up, mla_w_in, mla_q_norm_g, mla_w_q_up, mla_w_out, final_norm_g):
    import numpy as np
    import concourse.bacc as bacc
    from concourse import mybir
    from concourse.bass_utils import run_bass_kernel_spmd

    a = {k: np.asarray(v) for k, v in dict(
        x=x, norm_g=norm_g, w_in=hg_w_in, g_norm=hg_g_norm, w_o=hg_w_out, lb=hg_lb, kvin=kv_in_norm_g,
        kv=w_kv_down, kvn=kv_norm_g, up=w_kv_up, mw=mla_w_in, qn=mla_q_norm_g, qup=mla_w_q_up,
        mo=mla_w_out, fin=final_norm_g).items()}
    w_in = a["w_in"][0]
    key = HG_HEADS * KEY_DIM
    q, f = (w_in[:, i * key:(i + 1) * key].reshape(D_MODEL, STEPS, 256) for i in range(2))
    qf = np.concatenate([q, f], axis=2).reshape(D_MODEL, STEPS * 512)
    parts = [qf, w_in[:, 2 * key:2 * key + D_INNER], w_in[:, 2 * key + D_INNER:]]
    w_a = np.stack([units(p, 2, 512) for p in parts], axis=1).reshape(STEPS * A_UNITS, 128, UNIT)
    w_o = units(a["w_o"][0], 2, 512).reshape(-1, 128, UNIT)
    rope2 = np.concatenate([a["kv"][:, KV_LORA:]] * 2, axis=1)
    mw = a["mw"][0]
    w_c = np.concatenate([units(w, rows, cols).reshape(-1, 128, UNIT) for w, rows, cols in (
        (a["kv"][:, :KV_LORA], 2, 512), (mw[:, :512], 2, 512), (mw[:, 512:Q_LORA], 4, 256), (rope2, 8, 128))])
    up = a["up"].reshape(KV_LORA, STEPS, 4, 2, 128)
    w_bkv = np.stack([units(up[:, :, :, i].reshape(KV_LORA, -1), 2, 512) for i in range(2)],
                     axis=1).reshape(-1, 128, UNIT)
    qup = a["qup"][0].reshape(Q_LORA, STEPS, 4, NOPE + ROPE)
    qcols = np.concatenate([qup[..., :NOPE].reshape(Q_LORA, STEPS, -1), qup[..., NOPE:].reshape(Q_LORA, STEPS, -1)], axis=2)
    w_bq = qcols.reshape(KT_Q, 128, STEPS, 6, 128).transpose(2, 0, 3, 1, 4).reshape(STEPS, 4, 9, 128, 128)
    w_bq = np.ascontiguousarray(w_bq.transpose(0, 1, 3, 2, 4)).reshape(-1, 128, UNIT_Q)
    w_bg = units(mw[:, Q_LORA:], 2, 512).reshape(-1, 128, UNIT)
    w_out = units(a["mo"][0], 2, 512).reshape(-1, 128, UNIT)
    gains = np.ascontiguousarray(np.concatenate(
        [by_column(v) for v in (a["norm_g"][0], a["norm_g"][1], a["kvin"], a["kvn"], a["qn"][0], a["g_norm"][0],
                                a["lb"][0], a["lb"][1])], axis=1))
    arrays = dict(w_a=w_a, w_o=w_o, w_c=w_c, w_bkv=w_bkv, w_bq=w_bq, w_bg=w_bg, w_out=w_out,
                  x=a["x"][0][token_order()], consts=constants(), masks=score_masks(), gains=gains,
                  final_g=a["fin"].reshape(1, -1))
    arrays = {k: np.ascontiguousarray(v) for k, v in arrays.items()}

    nc = bacc.Bacc("TRN2", target_bir_lowering=False, num_devices=1)
    args = {k: nc.dram_tensor(k, v.shape, mybir.dt.from_np(v.dtype), kind="ExternalInput").ap()
            for k, v in arrays.items()}
    args["out"] = nc.dram_tensor("out", (1, TOKENS, D_MODEL), mybir.dt.float32, kind="ExternalOutput").ap()
    args["h_store"] = nc.dram_tensor("h_store", (TOKENS, D_MODEL), mybir.dt.float32, kind="Internal").ap()
    build(nc, **args)
    r = run_bass_kernel_spmd(nc, [arrays], core_ids=[0])
    return r.results[0]["out"][:, np.argsort(token_order())]
```
